# Optimizing a Trainium2 kernel written in Bass

```python
import jax
import jax.numpy as jnp
from jax import lax
import numpy as np

D_MODEL = 1024
BATCH = 1
SEQ = 512
DEPTH = 2

N_EVEN = (DEPTH + 1) // 2
N_ODD = DEPTH // 2
D_FF = 4 * D_MODEL
NORM_EPS = 1e-6

SC_WIDTH = D_MODEL // 2
SC_KERNEL = 3
MLA_HEADS = 8
MLA_NOPE = 64
MLA_ROPE = 32
MLA_V = 64
MLA_Q_RANK = 384
MLA_KV_RANK = 256
ROPE_THETA = 10000.0
ATTN_BLOCK = 128
EVEN_SPLITS = (SC_WIDTH, SC_WIDTH, SC_WIDTH, MLA_Q_RANK, MLA_KV_RANK, MLA_ROPE)
EVEN_IN = sum(EVEN_SPLITS)
EVEN_MIX = SC_WIDTH + MLA_HEADS * MLA_V

GLA_HEADS = 4
GLA_DK = 64
GLA_DV = 128
GLA_GATE_RANK = 16
GLA_TAU = 16.0
GLA_CHUNK = 64
LRU_WIDTH = D_MODEL // 2
LRU_BLOCKS = 8
LRU_KERNEL = 4
LRU_C = 8.0
ODD_SPLITS = (GLA_HEADS * GLA_DK, GLA_HEADS * GLA_DK, GLA_HEADS * GLA_DV, GLA_GATE_RANK,
              GLA_HEADS * GLA_DV, LRU_WIDTH, LRU_WIDTH)
ODD_IN = sum(ODD_SPLITS)
ODD_MIX = GLA_HEADS * GLA_DV + LRU_WIDTH

kernel_name = 'hybrid_sconv_mla_gla_rglru_trunk'

def _split(t, sizes):
    return jnp.split(t, np.cumsum(sizes)[:-1].tolist(), axis=-1)

def rmsnorm(x, g):
    xf = x.astype(jnp.float32)
    y = xf * lax.rsqrt(jnp.mean(xf * xf, axis=-1, keepdims=True) + NORM_EPS)
    return (y * g.astype(jnp.float32)).astype(x.dtype)

def causal_dwconv(u, w):
    k = w.shape[0]
    return lax.conv_general_dilated(
        u, w[:, None, :].astype(u.dtype), window_strides=(1,), padding=[(k - 1, 0)],
        dimension_numbers=('NWC', 'WIO', 'NWC'), feature_group_count=u.shape[-1])

def apply_rope(x, cos, sin):
    half = x.shape[-1] // 2
    x1, x2 = x[..., :half], x[..., half:]
    return jnp.concatenate([x1 * cos - x2 * sin, x2 * cos + x1 * sin], axis=-1).astype(x.dtype)

def mla_attention(c_q, c_kv, k_rope_raw, positions, q_norm_g, w_uq, kv_norm_g, w_ukv):
    b, s, _ = c_q.shape
    q = (rmsnorm(c_q, q_norm_g) @ w_uq).reshape(b, s, MLA_HEADS, MLA_NOPE + MLA_ROPE)
    q_nope, q_rope = q[..., :MLA_NOPE], q[..., MLA_NOPE:]
    kv = (rmsnorm(c_kv, kv_norm_g) @ w_ukv).reshape(b, s, MLA_HEADS, MLA_NOPE + MLA_V)
    k_nope, v = kv[..., :MLA_NOPE], kv[..., MLA_NOPE:]
    inv_freq = ROPE_THETA ** (-jnp.arange(0, MLA_ROPE, 2, dtype=jnp.float32) / MLA_ROPE)
    ang = positions[..., None].astype(jnp.float32) * inv_freq
    cos, sin = jnp.cos(ang), jnp.sin(ang)
    q_rope = apply_rope(q_rope, cos[:, :, None, :], sin[:, :, None, :])
    k_rope = apply_rope(k_rope_raw, cos, sin)
    scale = (MLA_NOPE + MLA_ROPE) ** -0.5
    outs = []
    for start in range(0, s, ATTN_BLOCK):
        end = start + ATTN_BLOCK
        sc = (jnp.einsum('bqhd,bkhd->bhqk', q_nope[:, start:end], k_nope[:, :end])
              + jnp.einsum('bqhr,bkr->bhqk', q_rope[:, start:end], k_rope[:, :end]))
        sc = sc.astype(jnp.float32) * scale
        causal = jnp.arange(end)[None, :] <= jnp.arange(start, end)[:, None]
        p = jax.nn.softmax(jnp.where(causal, sc, -jnp.inf), axis=-1).astype(v.dtype)
        outs.append(jnp.einsum('bhqk,bkhd->bqhd', p, v[:, :end]))
    o = jnp.concatenate(outs, axis=1)
    return o.reshape(b, s, MLA_HEADS * MLA_V)

def even_mixer(h, positions, w_in, conv_w, q_norm_g, w_uq, kv_norm_g, w_ukv, w_out):
    gate_b, gate_c, u, c_q, c_kv, k_rope = _split(h @ w_in, EVEN_SPLITS)
    sc_out = gate_b * causal_dwconv(gate_c * u, conv_w)
    mla_out = mla_attention(c_q, c_kv, k_rope, positions, q_norm_g, w_uq, kv_norm_g, w_ukv)
    return jnp.concatenate([sc_out, mla_out.astype(h.dtype)], axis=-1) @ w_out

def gla_chunked(q, k, v, log_a):
    b, s = q.shape[:2]
    n = s // GLA_CHUNK

    def chunk(t):
        return t.reshape(b, n, GLA_CHUNK, GLA_HEADS, t.shape[-1]).transpose(0, 3, 1, 2, 4)

    qc = chunk(q) * (GLA_DK ** -0.5)
    kc = chunk(k)
    vc = chunk(v)
    cum = jnp.cumsum(chunk(log_a).astype(jnp.float32), axis=3)
    last = cum[:, :, :, -1:, :]
    q_in = qc * jnp.exp(cum)
    k_in = kc * jnp.exp(-cum)
    k_out = kc * jnp.exp(last - cum)
    mask = jnp.tril(jnp.ones((GLA_CHUNK, GLA_CHUNK), dtype=bool))
    att = jnp.where(mask, jnp.einsum('bhnid,bhnjd->bhnij', q_in, k_in), 0.0)
    o_intra = jnp.einsum('bhnij,bhnjv->bhniv', att, vc)
    kv = jnp.einsum('bhnjd,bhnjv->bhndv', k_out, vc).astype(jnp.float32)
    decay = jnp.exp(last[:, :, :, 0, :])

    def step(state, inp):
        d, kv_n = inp
        return d[..., None] * state + kv_n, state

    init = jnp.zeros((b, GLA_HEADS, GLA_DK, GLA_DV), jnp.float32)
    _, states = lax.scan(step, init, (jnp.moveaxis(decay, 2, 0), jnp.moveaxis(kv, 2, 0)))
    states = jnp.moveaxis(states, 0, 2)
    o_inter = jnp.einsum('bhnid,bhndv->bhniv', q_in, states)
    o = o_intra + o_inter
    return o.transpose(0, 2, 3, 1, 4).reshape(b, s, GLA_HEADS, GLA_DV)

def rglru(xc, w_a, b_a, w_i, b_i, lam):
    b, s, c = xc.shape
    xb = xc.reshape(b, s, LRU_BLOCKS, c // LRU_BLOCKS)
    r = jax.nn.sigmoid(jnp.einsum('bsnc,ncd->bsnd', xb, w_a).reshape(b, s, c) + b_a)
    i = jax.nn.sigmoid(jnp.einsum('bsnc,ncd->bsnd', xb, w_i).reshape(b, s, c) + b_i)
    log_a = (-LRU_C * r.astype(jnp.float32)) * jax.nn.softplus(-lam.astype(jnp.float32))
    a = jnp.exp(log_a)
    inp = jnp.sqrt(-jnp.expm1(2.0 * log_a)) * (i * xc).astype(jnp.float32)

    def combine(left, right):
        a1, b1 = left
        a2, b2 = right
        return a1 * a2, a2 * b1 + b2

    _, hseq = lax.associative_scan(combine, (a, inp), axis=1)
    return hseq.astype(xc.dtype)

def odd_mixer(h, w_in, gate_up, gate_bias, gla_norm_g, conv_w, conv_b, w_a, b_a, w_i, b_i, lam, w_out):
    b, s, _ = h.shape
    q, k, v, g_lr, o_gate, x_lru, y_lru = _split(h @ w_in, ODD_SPLITS)
    log_a = jax.nn.log_sigmoid((g_lr @ gate_up + gate_bias).astype(jnp.float32)) / GLA_TAU
    o = gla_chunked(q.reshape(b, s, GLA_HEADS, GLA_DK), k.reshape(b, s, GLA_HEADS, GLA_DK),
                    v.reshape(b, s, GLA_HEADS, GLA_DV), log_a.reshape(b, s, GLA_HEADS, GLA_DK))
    o = rmsnorm(o, gla_norm_g).reshape(b, s, GLA_HEADS * GLA_DV)
    gla_out = (o * jax.nn.silu(o_gate)).astype(h.dtype)
    xc = causal_dwconv(x_lru, conv_w) + conv_b
    lru_out = jax.nn.gelu(y_lru) * rglru(xc, w_a, b_a, w_i, b_i, lam)
    return jnp.concatenate([gla_out, lru_out.astype(h.dtype)], axis=-1) @ w_out

def setup_inputs(seed: int = 0) -> dict:
    key = jax.random.key(seed)
    ks = list(jax.random.split(key, 40))
    f32 = jnp.float32

    def nrm(shape, fan_in):
        return jax.random.normal(ks.pop(), shape, f32) * (fan_in ** -0.5)

    def gain(shape):
        return 1.0 + 0.02 * jax.random.normal(ks.pop(), shape, f32)

    def bias(shape):
        return 0.01 * jax.random.normal(ks.pop(), shape, f32)

    x = jax.random.normal(ks.pop(), (BATCH, SEQ, D_MODEL), f32)
    offset = jax.random.randint(ks.pop(), (BATCH, 1), 0, 1024, dtype=jnp.int32)
    positions = offset + jnp.arange(SEQ, dtype=jnp.int32)[None, :]
    u = jax.random.uniform(ks.pop(), (N_ODD, LRU_WIDTH), f32, minval=0.9, maxval=0.999)
    sg = u ** (1.0 / LRU_C)
    lru_lambda = jnp.log(sg) - jnp.log1p(-sg)
    blk = LRU_WIDTH // LRU_BLOCKS
    return {
        'x': x,
        'positions': positions,
        'mixer_norm_g': gain((DEPTH, D_MODEL)),
        'mlp_norm_g': gain((DEPTH, D_MODEL)),
        'mlp_w1': nrm((DEPTH, D_MODEL, D_FF), D_MODEL),
        'mlp_w2': nrm((DEPTH, D_FF, D_MODEL), D_FF),
        'final_norm_g': gain((D_MODEL,)),
        'ev_w_in': nrm((N_EVEN, D_MODEL, EVEN_IN), D_MODEL),
        'ev_conv_w': nrm((N_EVEN, SC_KERNEL, SC_WIDTH), SC_KERNEL),
        'mla_q_norm_g': gain((N_EVEN, MLA_Q_RANK)),
        'mla_w_uq': nrm((N_EVEN, MLA_Q_RANK, MLA_HEADS * (MLA_NOPE + MLA_ROPE)), MLA_Q_RANK),
        'mla_kv_norm_g': gain((N_EVEN, MLA_KV_RANK)),
        'mla_w_ukv': nrm((N_EVEN, MLA_KV_RANK, MLA_HEADS * (MLA_NOPE + MLA_V)), MLA_KV_RANK),
        'ev_w_out': nrm((N_EVEN, EVEN_MIX, D_MODEL), EVEN_MIX),
        'od_w_in': nrm((N_ODD, D_MODEL, ODD_IN), D_MODEL),
        'gla_w_gate_up': nrm((N_ODD, GLA_GATE_RANK, GLA_HEADS * GLA_DK), GLA_GATE_RANK),
        'gla_b_gate': bias((N_ODD, GLA_HEADS * GLA_DK)),
        'gla_norm_g': gain((N_ODD, GLA_DV)),
        'lru_conv_w': nrm((N_ODD, LRU_KERNEL, LRU_WIDTH), LRU_KERNEL),
        'lru_conv_b': bias((N_ODD, LRU_WIDTH)),
        'lru_w_a': nrm((N_ODD, LRU_BLOCKS, blk, blk), blk),
        'lru_b_a': bias((N_ODD, LRU_WIDTH)),
        'lru_w_i': nrm((N_ODD, LRU_BLOCKS, blk, blk), blk),
        'lru_b_i': bias((N_ODD, LRU_WIDTH)),
        'lru_lambda': lru_lambda,
        'od_w_out': nrm((N_ODD, ODD_MIX, D_MODEL), ODD_MIX),
    }

def reference(x, positions, mixer_norm_g, mlp_norm_g, mlp_w1, mlp_w2, final_norm_g,
              ev_w_in, ev_conv_w, mla_q_norm_g, mla_w_uq, mla_kv_norm_g, mla_w_ukv, ev_w_out,
              od_w_in, gla_w_gate_up, gla_b_gate, gla_norm_g, lru_conv_w, lru_conv_b,
              lru_w_a, lru_b_a, lru_w_i, lru_b_i, lru_lambda, od_w_out):
    h = x
    for layer in range(DEPTH):
        j = layer // 2
        hn = rmsnorm(h, mixer_norm_g[layer])
        if layer % 2 == 0:
            mix = even_mixer(hn, positions, ev_w_in[j], ev_conv_w[j], mla_q_norm_g[j], mla_w_uq[j],
                             mla_kv_norm_g[j], mla_w_ukv[j], ev_w_out[j])
        else:
            mix = odd_mixer(hn, od_w_in[j], gla_w_gate_up[j], gla_b_gate[j], gla_norm_g[j],
                            lru_conv_w[j], lru_conv_b[j], lru_w_a[j], lru_b_a[j], lru_w_i[j],
                            lru_b_i[j], lru_lambda[j], od_w_out[j])
        h = h + mix.astype(h.dtype)
        hn = rmsnorm(h, mlp_norm_g[layer])
        h = h + (jnp.square(jax.nn.relu(hn @ mlp_w1[layer])) @ mlp_w2[layer]).astype(h.dtype)
    return rmsnorm(h, final_norm_g)


_drawn_inputs = setup_inputs


def setup_inputs(seed=0):
    import zlib

    import numpy as np

    out = dict(_drawn_inputs(seed))
    spreads = {}
    factors = {'final_norm_g': 20.258,
     'mla_q_norm_g': 8.0,
     'mla_kv_norm_g': 8.0,
     'gla_b_gate': 26.88,
     'gla_norm_g': 200.0,
     'lru_conv_b': 151.472,
     'lru_b_a': 200.0,
     'lru_b_i': 200.0,
     'mlp_norm_g': 7.368,
     'lru_w_a': 38.12,
     'lru_lambda': 26.504,
     'lru_conv_w': 8.0,
     'lru_w_i': 8.0}
    for name, (base, spread) in spreads.items():
        noise = np.random.default_rng([zlib.crc32(name.encode()), seed]).standard_normal(out[name].shape)
        drawn = base * np.exp(spread * noise) if base else spread * noise
        out[name] = jnp.asarray(drawn.astype(out[name].dtype))
    for name, factor in factors.items():
        out[name] = (out[name] * factor).astype(out[name].dtype)
    return out
```

```python
from contextlib import ExitStack

import numpy as np

import concourse.bass as bass
from concourse import mybir

F32 = mybir.dt.float32
F32R = mybir.dt.float32r
BF16 = mybir.dt.bfloat16
I32 = mybir.dt.int32
ALU = mybir.AluOpType
ACT = mybir.ActivationFunctionType
AX_X = mybir.AxisListType.X

P = 128
S = 512
D = 1024
KD = D // P
TB = S // P
D_FF = 4 * D
EPS = 1e-6
CH = 512 // P

SC_K = 3
HEADS, NOPE, ROPE, VD = 8, 64, 32, 64
QR, KVR = 384, 256
QK = NOPE + ROPE
SCALE = QK ** -0.5
MASKED = -1e37

GH, GDK, GDV, GRANK, GTAU, GCH = 4, 64, 128, 16, 16.0, 64
NCH = S // GCH
LRU_K, LRU_C = 4, 8.0

RAW = 4
RING = 3
BLOCKS = D_FF // 512

PARAM_ROWS = [("mix0", KD), ("mlp0", KD), ("mix1", KD), ("mlp1", KD), ("final", KD), ("qg", 3), ("kvg", 2),
              ("evconv", SC_K * CH), ("gbias", 2), ("glag", 1), ("lconvw", LRU_K * CH), ("lconvb", CH),
              ("ba", CH), ("bi", CH), ("lam", CH)]
PCOL = {}
_n = 0
for _name, _rows in PARAM_ROWS:
    PCOL[_name] = _n
    _n += _rows
NPARAM = _n


def tile_table():
    tiles = [("cq01", KD, 256), ("cq2kv0", KD, 256), ("kv1kr", KD, 160)]
    for g in range(2):
        tiles += [(f"c{g}", KD, 256), (f"u{g}", KD, 256), (f"b{g}", KD, 256)]
    tiles += [("ukv", 2, 1024), ("uq0", 3, 384), ("uq1", 3, 384)]
    tiles += [("ewo0a", 4, 512), ("ewo0b", 4, 512), ("ewo1a", 4, 512), ("ewo1b", 4, 512)]
    tiles += [("mlp0", 0, 0)] * (4 * BLOCKS)
    tiles += [("glr", KD, 128), ("gq", KD, 256), ("gk", KD, 256), ("gv0", KD, 256), ("gv1", KD, 256),
              ("og0", KD, 256), ("og1", KD, 256)]
    for g in range(2):
        tiles += [(f"y{g}", KD, 256), (f"x{g}", KD, 256)]
    tiles += [("owo0a", 4, 512), ("owo0b", 4, 512), ("owo1a", 4, 512), ("owo1b", 4, 512)]
    tiles += [("mlp1", 0, 0)] * (4 * BLOCKS)
    return tiles


def gemm_order():
    order, last = [], {}

    def use(tile, names):
        order.extend(names)
        last[tile] = len(order)

    order += [("x", c) for c in range(KD)]
    use("cq01", [("cq", 0), ("cq", 1)])
    use("cq2kv0", [("cq", 2), ("cq", 3)])
    use("kv1kr", [("cq", 4), ("kr", 0)])
    for g in range(2):
        for n in "cub":
            use(f"{n}{g}", [(n, 2 * g), (n, 2 * g + 1)])
    use("ukv", [("v", t) for t in range(TB)] + [("k", h) for h in range(HEADS)])
    use("uq0", [("q", h) for h in range(4)])
    use("uq1", [("q", h) for h in range(4, 8)])
    for h in range(HEADS + 2):
        if h >= 3 and h % 2 == 1:
            order.append(("ot", (h - 3) // 2))
        if h < HEADS:
            order.append(("ewo0", h))
        if h == 3:
            last["ewo0a"] = len(order)
        if h == 7:
            last["ewo0b"] = len(order)
    use("ewo1a", [("ewo1", c) for c in range(4)])
    use("ewo1b", [("ewo1", c) for c in range(4, 8)])
    order += [("mlp0", i) for i in range(12 * BLOCKS)]
    use("glr", [("glr", 0)])
    use("gq", [("gq", 0), ("gq", 1)])
    order += [("z", 0), ("z", 1)]
    use("gk", [("gk", 0), ("gk", 1)])
    use("gv0", [("gv0", t) for t in range(TB)])
    use("gv1", [("gv1", t) for t in range(TB)])
    use("og0", [("og", 0), ("og", 1)])
    use("og1", [("og", 2), ("og", 3)])
    use("y0", [("y", 0), ("y", 1)])
    use("x0", [("xl", 0), ("xl", 1)])
    use("y1", [("y", 2), ("y", 3)])
    order += [("ra", 0), ("ri", 0), ("ra", 1), ("ri", 1)]
    use("x1", [("xl", 2), ("xl", 3)])
    order += [("kt", 0), ("kt", 1)]
    order += [("ra", 2), ("ri", 2), ("ra", 3), ("ri", 3)]
    order += [("att", h) for h in range(GH)]
    order += [("o", h) for h in range(GH)]
    use("owo0a", [("owo0", c) for c in range(4)])
    use("owo0b", [("owo0", c) for c in range(4, 8)])
    use("owo1a", [("owo1", c) for c in range(4)])
    use("owo1b", [("owo1", c) for c in range(4, 8)])
    order += [("mlp1", i) for i in range(12 * BLOCKS - 8)]
    for c in range(KD):
        order.append(("last", c))
        if c:
            order.append(("yt", c - 1))
    order.append(("yt", KD - 1))
    return {key: n for n, key in enumerate(order)}, last


TILES = tile_table()
TILE = {}
for _i, (_key, _k, _c) in enumerate(TILES):
    TILE.setdefault(_key, _i)
G, TILE_LAST = gemm_order()

HID = {"sconv": 0, "attn": 4, "mlp0": 8, "lru": 8 + 4 * BLOCKS, "gla": 12 + 4 * BLOCKS, "mlp1": 16 + 4 * BLOCKS}
READY = {"sconv": 0, "mlp0": 4, "lru": 4 + 4 * BLOCKS, "gla": 8 + 4 * BLOCKS, "mlp1": 12 + 4 * BLOCKS}
MIX_IN = {"sconv": 0, "lru": 4, "gla": 8}
STAT = {"mix0": 0, "q": 1, "kv": 2, "mlp0": 3, "mix1": 4, "mix1col": 5, "gla": 6, "mlp1": 6 + GH, "final": 7 + GH}
SQ = {"mix0": 0, "q": KD, "kv": KD + 3, "mlp0": KD + 5, "mix1": 2 * KD + 5, "gla": 3 * KD + 5,
      "mlp1": 3 * KD + 5 + GH, "final": 4 * KD + 5 + GH}
INST = {"mix0": 0, "mlp0": 1, "mix1": 2, "mlp1": 3}


def trunk(nc, t, out):
    ctx = ExitStack()
    with ctx:
        arena_bytes = 0
        places = []

        def place(name, shape, dt, at=None):
            nonlocal arena_bytes
            size = int(np.prod(shape[1:])) * mybir.dt.size(dt)
            size = (size + 31) // 32 * 32
            where = arena_bytes if at is None else at
            if at is None:
                arena_bytes += size
            places.append(where + size)
            return nc.alloc_sbuf_tensor_at(name, shape, dt, offset=base + where), where

        base = (nc.sbuf_base + 31) // 32 * 32

        hT, _ = place("hT", [P, KD, S], F32)
        hgH, hg_at = place("hgH", [P, KD, S], F32R)
        hgL, _ = place("hgL", [P, KD, S], F32R)
        raw, _ = place("raw", [P, RAW, 2048], F32)
        wH, _ = place("wH", [P, 2, 2048], F32R)
        wL, _ = place("wL", [P, 2, 2048], F32R)
        hidH, hidH_at = place("hidH", [P, 2, 4, S], F32R)
        hidL, hidL_at = place("hidL", [P, 2, 4, S], F32R)
        rstd, _ = place("rstd", [P, S], F32)
        rstd_t, _ = place("rstd_t", [P, S], F32)
        var_t, _ = place("var_t", [P, S], F32)
        acc, _ = place("acc", [P, 2, S], F32)
        tmpR, _ = place("tmpR", [P, S], F32)
        tmpS, _ = place("tmpS", [P, S], F32)
        ident, _ = place("ident", [P, P], F32)
        ones, _ = place("ones", [P, P], F32)
        identb, _ = place("identb", [P, P], BF16)
        causal, _ = place("causal", [P, P], BF16)
        pcol, _ = place("pcol", [P, NPARAM], F32)
        small, _ = place("small", [P, 128], F32)
        resets, _ = place("resets", [P, S], F32)
        gmask, _ = place("gmask", [P, P], F32)
        gup, _ = place("gup", [GRANK, 2 * P], F32)
        area_at = arena_bytes

        NS = P * TB * (TB + 1) // 2
        conv_at = area_at + 22528
        v_tok, _ = place("v_tok", [P, TB, HEADS * VD], F32, area_at)
        o_tok, _ = place("o_tok", [P, 2, TB, P], F32, area_at + 8192)
        c_raw, _ = place("c_raw", [P, 5, S], F32, area_at)
        rope_cs, _ = place("rope_cs", [P, 2, S], F32, area_at + 12288)
        kr_s, _ = place("kr_s", [P, S], F32, area_at + 16384)
        rope_tmp, _ = place("rope_tmp", [P, 2, S], F32, area_at + 18432)
        b_s, _ = place("b_s", [P, CH, S], F32, conv_at)
        cu, _ = place("cu", [P, CH, S + SC_K - 1], F32, conv_at + 8192)
        c_s, _ = place("c_s", [P, 2, S], F32, conv_at + 16416)
        probs, _ = place("probs", [P, 2, NS], F32, conv_at)
        probsT, _ = place("probsT", [P, 2, NS], F32, conv_at + 8 * NS)
        qT, _ = place("qT", [P, HEADS, S], F32, hg_at)
        kT, _ = place("kT", [P, HEADS, S], F32, hg_at + 4 * HEADS * S)
        x_tok, _ = place("x_tok", [P, TB, D], F32, conv_at)
        prm, _ = place("prm", [NPARAM, P], F32, area_at + 16384)
        pos_i, _ = place("pos_i", [P, S], I32, area_at + 18432)
        ang, _ = place("ang", [P, S], F32, area_at + 20480)
        ang_k, _ = place("ang_k", [P, 2, S], F32, area_at)
        gq, _ = place("gq", [P, 2, S], F32, area_at)
        gk, _ = place("gk", [P, 2, S], F32, area_at + 4096)
        gki, _ = place("gki", [P, 2, S], F32, area_at + 8192)
        cum, _ = place("cum", [P, 2, S], F32, area_at + 12288)
        ge, _ = place("ge", [P, 2, S], F32, area_at + 16384)
        glr, _ = place("glr", [GRANK, S], F32, area_at + 16384)
        gel, _ = place("gel", [P, CH, S], F32, area_at + 12288)
        gv, _ = place("gv", [P, TB, GH * GDV], F32, area_at + 20480)
        og, _ = place("og", [P, GH, S], F32, area_at + 28672)
        xl, _ = place("xl", [P, S + LRU_K - 1], F32, area_at + 36864)
        wgate, _ = place("wgate", [P, 2, CH, P], F32, area_at + 38944)
        xc, _ = place("xc", [P, CH, S], F32, hidL_at + 8192)
        lr, _ = place("lr", [P, 2, S], F32, hidH_at + 8192)
        li, _ = place("li", [P, 2, S], F32, hidH_at + 12288)
        gkT, _ = place("gkT", [P, TB, 2 * P], F32, hg_at)
        attT, _ = place("attT", [P, GH, TB, P], F32, hg_at + 4096)
        states, _ = place("states", [P, 2, NCH, GDV], F32, hg_at + 12288)
        o_sb, _ = place("o_sb", [P, GH, S], F32, hg_at + 20480)
        yT, _ = place("yT", [P, KD, S], F32, hg_at)
        y_tok, _ = place("y_tok", [P, TB, D], F32, area_at)
        ctx.enter_context(nc.sbuf_tensor("arena", [P, (max(places) + 3) // 4 + 16], F32))

        bank = [ctx.enter_context(nc.psum_tensor(f"bank{i}", [P, S], F32)) for i in range(8)]
        stat_bank = o_bank = bank[7]
        s_banks, pt_banks = bank[3:5], bank[5:7]

        mx, nmx, sums, rinv = small[:, 0:8], small[:, 8:16], small[:, 16:24], small[:, 24:28]
        vcol, rcol = small[:, 32:36], small[:, 28:32]
        decay = small[:, 36:52].rearrange("p (a n) -> p a n", a=2)
        lam_e, lam_d, lam_s, lam_s2 = (small[:, 52 + 4 * i:56 + 4 * i] for i in range(4))
        lam_p, lam_k, lam_nk = (small[:, 68 + 4 * i:72 + 4 * i] for i in range(3))
        eps_col = small[:, 80:81]
        freq = small[:, 82:84]

        def col(name, c, n=1):
            return pcol[:, PCOL[name] + c:PCOL[name] + c + n]

        def sem(name):
            return ctx.enter_context(nc.semaphore(name))

        ld_x = [sem(f"ld_x{i}") for i in range(TB)]
        ld_prm, ld_pos, ld_gup, ld_wgate, ld_out = sem("ld_prm"), sem("ld_pos"), sem("ld_gup"), sem("ld_wgate"), sem("ld_out")
        raw_loaded = [sem(f"raw_loaded{i}") for i in range(RAW)]
        wh_ready, wl_ready = sem("wh_ready"), sem("wl_ready")
        gemm_done, gemm_out = sem("gemm_done"), sem("gemm_out")
        consts_ready, params_done, params_ready = sem("consts_ready"), sem("params_done"), sem("params_ready")
        hi_new, hg_ready, sq_ready, acc_ready = sem("hi_new"), sem("hg_ready"), sem("sq_ready"), sem("acc_ready")
        stat_done, var_ready, rt_ready = sem("stat_done"), sem("var_ready"), sem("rt_ready")
        dve_link, act_link, pool_link = sem("dve_link"), sem("act_link"), sem("pool_link")
        rope_arg, rope_ready = sem("rope_arg"), sem("rope_ready")
        cn_scaled, cn_hi, cn_ready = sem("cn_scaled"), sem("cn_hi"), sem("cn_ready")
        cu_ready, mix_in, hid_hi, hid_ready = sem("cu_ready"), sem("mix_in"), sem("hid_hi"), sem("hid_ready")
        kr_ready, kr_spread = sem("kr_ready"), sem("kr_spread")
        q_turned, q_roped = sem("q_turned"), sem("q_roped")
        s_done, nmax_ready, p_ready = sem("s_done"), sem("nmax_ready"), sem("p_ready")
        pt_done, pt_out, o_done, o_out = sem("pt_done"), sem("pt_out"), sem("o_done"), sem("o_out")
        sq_self = sem("sq_self")
        ls_ready, cum_ready, e_ready, e_used = sem("ls_ready"), sem("cum_ready"), sem("e_ready"), sem("e_used")
        lam_exp, lam_ready, gel_ready, og_ready = sem("lam_exp"), sem("lam_ready"), sem("gel_ready"), sem("og_ready")
        gla_ready, kv_done, states_ready = sem("gla_ready"), sem("kv_done"), sem("states_ready")
        xc_ready, sig_ready, gates_ready = sem("xc_ready"), sem("sig_ready"), sem("gates_ready")
        lru_m, lru_rt, ix_ready = sem("lru_m"), sem("lru_rt"), sem("ix_ready")
        y_new, y_scaled = sem("y_new"), sem("y_scaled")
        wzero = sem("wzero")

        p_at = [P * i * (i + 1) // 2 for i in range(TB)]
        turned = [(j, i) for j in range(TB) for i in range(j, TB)]
        pt_groups = [turned[n:n + 4] for n in range(0, len(turned), 4)]
        s_units = [(0, 1), (2,), (3,)]
        NU, NG = len(s_units), len(pt_groups)

        def rows(w):
            return w.rearrange("(k p) n -> p k n", p=P)

        e_in, o_in = rows(t["ev_w_in"][0]), rows(t["od_w_in"][0])
        src = {"cq01": e_in[:, :, 1536:1792], "cq2kv0": e_in[:, :, 1792:2048], "kv1kr": e_in[:, :, 2048:2208],
               "ukv": rows(t["mla_w_ukv"][0]), "glr": o_in[:, :, 1024:1152],
               "gq": o_in[:, :, 0:256], "gk": o_in[:, :, 256:512]}
        for g in range(2):
            c = 256 * g
            src[f"b{g}"], src[f"c{g}"], src[f"u{g}"] = (e_in[:, :, o + c:o + c + 256] for o in (0, 512, 1024))
            src[f"uq{g}"] = rows(t["mla_w_uq"][0])[:, :, 384 * g:384 * g + 384]
            src[f"gv{g}"], src[f"og{g}"] = (o_in[:, :, o + c:o + c + 256] for o in (512, 1040))
            src[f"x{g}"], src[f"y{g}"] = (o_in[:, :, o + c:o + c + 256] for o in (1552, 2064))
            for m, half in enumerate("ab"):
                src[f"ewo{g}{half}"] = rows(t["ev_w_out"][0])[:, 4 * g:4 * g + 4, 512 * m:512 * m + 512]
                src[f"owo{g}{half}"] = rows(t["od_w_out"][0])[:, 4 - 4 * g:8 - 4 * g, 512 * m:512 * m + 512]

        def tile_view(buf, slot, kc, n):
            return buf[:, slot, 0:kc * n].rearrange("p (k n) -> p k n", k=kc)

        def static_tiles(lo, hi):
            return [n for n in range(lo, hi) if TILES[n][1]]

        LOOPS = (BLOCKS - 2) // 2

        block = ctx.enter_context(nc.Block())

        @block.sync
        def _(sp):
            def load(n, view, kc, cols, count=None):
                first = isinstance(n, int) and n < RAW
                slot = n % RAW if isinstance(n, int) else count
                if not first:
                    sp.wait_ge(wl_ready, n - RAW + 1)
                sp.dma_start(tile_view(raw, slot, kc, cols), view).then_inc(raw_loaded[slot], 16)

            def plain(lo, hi):
                for n in range(lo, hi):
                    key, kc, cols = TILES[n]
                    load(n, src[key], kc, cols)

            def mlp(layer):
                w1 = rows(t["mlp_w1"][layer])
                w2 = t["mlp_w2"][layer].rearrange("(b k p) n -> b p k n", k=4, p=P)
                n0 = TILE[f"mlp{layer}"]

                def up(n, j, slot):
                    for half in range(2):
                        load(n + half, w1[:, :, bass.ds(512 * j + 256 * half, 256)], KD, 256, (slot + half) % RAW)

                def down(n, j, slot):
                    for half in range(2):
                        view = w2[bass.ds(j, 1), :, :, 512 * half:512 * half + 512].rearrange("b p k n -> p (b k) n")
                        load(n + half, view, 4, 512, (slot + half) % RAW)

                up(n0, 0, n0)
                with sp.Fori(1, LOOPS + 1) as i:
                    for pair in range(2):
                        n, j = n0 + 2 - 8 + 4 * pair, 2 * i - 2 + pair
                        up(n + 8 * i, j + 1, n)
                        down(n + 2 + 8 * i, j, n + 2)
                n = n0 + 2 + 8 * LOOPS
                up(n, BLOCKS - 1, n)
                down(n + 2, BLOCKS - 2, n + 2)
                down(n + 4, BLOCKS - 1, n + 4)

            for b in range(TB):
                sp.dma_start(x_tok[:, b, :], t["x"][0, b * P:(b + 1) * P, :]).then_inc(ld_x[b], 16)
                if b == 0:
                    plain(0, 1)
                    pieces = [("mix0", t["mixer_norm_g"][0]), ("mlp0", t["mlp_norm_g"][0]),
                              ("mix1", t["mixer_norm_g"][1]), ("mlp1", t["mlp_norm_g"][1]),
                              ("final", t["final_norm_g"]), ("qg", t["mla_q_norm_g"][0]),
                              ("kvg", t["mla_kv_norm_g"][0]), ("evconv", t["ev_conv_w"][0].rearrange("k n -> (k n)")),
                              ("gbias", t["gla_b_gate"][0]), ("glag", t["gla_norm_g"][0]),
                              ("lconvw", t["lru_conv_w"][0].rearrange("k n -> (k n)")), ("lconvb", t["lru_conv_b"][0]),
                              ("ba", t["lru_b_a"][0]), ("bi", t["lru_b_i"][0]), ("lam", t["lru_lambda"][0])]
                    for name, vec in pieces:
                        v = vec.rearrange("(c p) -> c p", p=P)
                        at = PCOL[name]
                        sp.dma_start(prm[at:at + v.shape[0], :], v).then_inc(ld_prm, 16)
                    sp.dma_start(pos_i[64:96, :], t["positions"].broadcast_to((ROPE, S))).then_inc(ld_pos, 16)
                    sp.dma_start(freq[64:96, :], t["rope_freq"]).then_inc(ld_pos, 16)
            plain(1, RAW)
            sp.dma_start(gup[:, :], t["gla_w_gate_up"][0]).then_inc(ld_gup, 16)
            plain(RAW, TILE["mlp0"])
            mlp(0)
            plain(TILE["glr"], TILE["gv0"])
            sp.wait_ge(wzero, 1)
            for gate, w in enumerate((t["lru_w_a"][0], t["lru_w_i"][0])):
                pairs = w.rearrange("(c b) i j -> b i c j", b=2)
                for b in range(2):
                    sp.dma_start(wgate[64 * b:64 * b + 64, gate, :, 64 * b:64 * b + 64], pairs[b]).then_inc(ld_wgate, 16)
            plain(TILE["gv0"], TILE["mlp1"])
            mlp(1)
            for b in range(TB):
                sp.wait_ge(y_scaled, b + 1)
                sp.dma_start(out[0, b * P:(b + 1) * P, :], y_tok[:, b, :]).then_inc(ld_out, 16)
            sp.wait_ge(ld_out, 16 * TB)

        @block.gpsimd
        def _(pool):
            n_link = 0

            def link(ins):
                nonlocal n_link
                n_link += 1
                ins.then_inc(pool_link, 1)
                pool.wait_ge(pool_link, n_link)

            link(pool.memset(ones[:, :], 1.0))
            link(pool.memset(ident[:, :], 0.0))
            link(pool.affine_select(out=ident[:, :], in_=ident[:, :], compare_op=ALU.not_equal, fill=1.0, base=0,
                                    pattern=[[-1, P]], channel_multiplier=1))
            link(pool.memset(causal[:, :], 0.0))
            link(pool.affine_select(out=causal[:, :], in_=causal[:, :], compare_op=ALU.is_ge, fill=MASKED, base=0,
                                    pattern=[[-1, P]], channel_multiplier=1))
            link(pool.memset(gmask[:, :], 1.0))
            link(pool.affine_select(out=gmask[:, :], in_=gmask[:, :], compare_op=ALU.is_ge, fill=0.0, base=0,
                                    pattern=[[1, P]], channel_multiplier=-1))
            link(pool.memset(gmask[0:GCH, GCH:P], 0.0))
            link(pool.memset(resets[:, :], 1.0))
            link(pool.memset(resets[:, 0:S:GCH], 0.0))
            link(pool.memset(eps_col, EPS))
            pool.tensor_copy(identb[:, :], ident[:, :]).then_inc(consts_ready, 1)

            for g in range(2):
                for c in (2 * g, 2 * g + 1):
                    pool.wait_ge(gemm_out, G["u", c] + 1)
                    pool.tensor_tensor(cu[:, c, 2:2 + S], cu[:, c, 2:2 + S], c_s[:, c % 2, :], ALU.mult).then_inc(cu_ready, 1)

            pool.wait_ge(cu_ready, CH)
            pool.wait_ge(kr_ready, 1)
            pool.wait_ge(gemm_done, G["v", 0] + 1)
            for h in range(HEADS):
                if h:
                    pool.wait_ge(kr_spread, h)
                pool.tensor_copy(kT[64:96, h, :], kr_s[64:96, :]).then_inc(kr_spread, 1)

            pool.wait_ge(kr_spread, HEADS)
            for h in range(HEADS):
                if h:
                    pool.wait_ge(q_roped, h)
                pool.wait_ge(q_turned, h + 1)
                turned_q, own_q = rope_tmp[64:96, h % 2, :], qT[64:96, h, :]
                link(pool.tensor_tensor(own_q, own_q, rope_cs[64:96, 0, :], ALU.mult))
                link(pool.tensor_tensor(turned_q, turned_q, rope_cs[64:96, 1, :], ALU.mult))
                pool.tensor_tensor(own_q, own_q, turned_q, ALU.add).then_inc(q_roped, 1)

            pool.wait_ge(q_roped, HEADS)
            pool.wait_ge(gemm_done, G["glr", 0] + 1)
            pool.memset(wgate[:, :, :, :], 0.0).then_inc(wzero, 1)

            for c in range(CH):
                pool.wait_ge(sig_ready, c + 1)
                pool.wait_ge(xc_ready, c + 1)
                pool.tensor_tensor(li[:, c % 2, :], li[:, c % 2, :], xc[:, c, :], ALU.mult).then_inc(ix_ready, 1)

        @block.scalar
        def _(act):
            def split(n, slot=None, size=2048):
                if isinstance(n, int):
                    slot, size = n, TILES[n][1] * TILES[n][2] or 2048
                    act.wait_ge(raw_loaded[slot % RAW], 16 * (n // RAW + 1))
                act.activation(wH[:, slot % 2, 0:size], raw[:, slot % RAW, 0:size], ACT.Copy).then_inc(wh_ready, 1)

            def used(n):
                act.wait_ge(gemm_done, TILE_LAST[TILES[n][0]])

            def split_after(key):
                n = TILE[key]
                used(n)
                split(n + 2)

            n_link = 0

            def link(ins):
                nonlocal n_link
                n_link += 1
                ins.then_inc(act_link, 1)
                act.wait_ge(act_link, n_link)

            def square(source, n):
                if n:
                    act.wait_ge(acc_ready, n)
                act.activation(tmpS[:, :], source, ACT.Square).then_inc(sq_ready, 1)

            def finalize(norm, c, k):
                act.wait_ge(gemm_out, k + 1)
                act.activation(hgH[:, c, :], hT[:, c, :], ACT.Copy, scale=col(norm, c)).then_inc(hi_new, 1)
                square(hT[:, c, :], SQ[norm] + c)

            def root(s, buf):
                act.wait_ge(var_ready, s + 1)
                act.activation(buf, buf, ACT.Sqrt).then_inc(rt_ready, 1)

            def hid_split(n, source, dst):
                act.wait_ge(mix_in, n + 1)
                act.activation(dst, source, ACT.Copy).then_inc(hid_hi, 1)

            def mlp(layer):
                n0, g0 = TILE[f"mlp{layer}"], G[f"mlp{layer}", 0]
                s0 = 32 * layer

                def after(n, k, slot, first=None):
                    act.wait_ge(gemm_done, k + 1)
                    if first is None:
                        split(n + 2)
                    else:
                        act.wait_ge(raw_loaded[(slot + 2) % RAW], first)
                        split(n + 2, slot + 2)

                def up(k, buf, chunks, sq):
                    for m in chunks:
                        act.wait_ge(gemm_out, k + m + 1)
                        act.activation(tmpS[:, :], tmpR[:, :], ACT.Square).then_inc(sq_self, 1)
                        act.wait_ge(sq_self, sq + m + 1)
                        act.activation(hidH[:, buf, m, :], tmpS[:, :], ACT.Copy).then_inc(hid_hi, 1)

                for half in range(2):
                    up(g0, 0, (2 * half, 2 * half + 1), s0)
                    after(n0 + half, g0 + 2 * half + 1, n0 + half)
                with act.Fori(1, LOOPS + 1) as i:
                    for pair in range(2):
                        n, g = n0 - 6 + 4 * pair, g0 + 4 - 24 + 12 * pair
                        for half in range(2):
                            up(g + 24 * i, (pair + 1) % 2, (2 * half, 2 * half + 1), s0 + 4 - 8 + 4 * pair + 8 * i)
                            m = n + half
                            after(m + 8 * i, g + 2 * half + 1 + 24 * i, m, 32 * i + 16 * ((m + 2) // RAW + 1))
                        for half in range(2):
                            m = n + 2 + half
                            after(m + 8 * i, g + 4 + 4 * half + 3 + 24 * i, m, 32 * i + 16 * ((m + 2) // RAW + 1))
                n, g = n0 + 2 + 8 * LOOPS, g0 + 4 + 24 * LOOPS
                for half in range(2):
                    up(g, (BLOCKS - 1) % 2, (2 * half, 2 * half + 1), s0 + 4 + 8 * LOOPS)
                    after(n + half, g + 2 * half + 1, n + half)
                for half in range(2):
                    m = n + 2 + half
                    if m + 2 < len(TILES):
                        after(m, g + 4 + 4 * half + 3, m)
                for c in range(KD):
                    if layer == 0:
                        finalize("mix1", c, g + 12 + c)
                    else:
                        act.wait_ge(gemm_out, G["last", c] + 1)
                        act.activation(yT[:, c, :], hT[:, c, :], ACT.Copy, scale=col("final", c)).then_inc(y_new, 1)
                        square(hT[:, c, :], SQ["final"] + c)
                    if c % 4 == 3 and n + 4 + c // 4 + 2 < len(TILES):
                        m = n + 4 + c // 4
                        after(m, g + 12 + c, m)

            act.wait_ge(rope_arg, 1)
            act.activation(rope_cs[64:96, 0, :], ang_k[64:96, 0, :], ACT.Sin).then_inc(rope_ready, 1)
            act.activation(rope_cs[64:96, 1, :], ang_k[64:96, 1, :], ACT.Sin, scale=freq[64:96, 1:2]).then_inc(rope_ready, 1)
            split(0)
            split(1)
            act.wait_ge(params_ready, 1)
            for c in range(KD):
                finalize("mix0", c, G["x", c])
            root(STAT["mix0"], var_t[:, :])

            def latent_square(c):
                act.wait_ge(gemm_out, G["cq", c] + 1)
                square(c_raw[:, c, :], SQ["q"] + c)

            latent_square(0)
            latent_square(1)
            split_after("cq01")
            latent_square(2)
            latent_square(3)
            split_after("cq2kv0")
            latent_square(4)
            split_after("kv1kr")
            root(STAT["q"], var_t[:, :])
            root(STAT["kv"], var_t[:, :])
            split_after("c0")
            for c in range(5):
                act.wait_ge(cn_scaled, c + 1)
                dst = hidH[:, 1, c, :] if c < 4 else hidH[:, 0, 3, :]
                act.activation(dst, c_raw[:, c, :], ACT.Copy).then_inc(cn_hi, 1)
            for key in ("u0", "b0", "c1", "u1", "b1"):
                split_after(key)
            for c in range(CH):
                if c == 3:
                    act.wait_ge(gemm_done, G["k", HEADS - 1] + 1)
                    split_after("ukv")
                hid_split(MIX_IN["sconv"] + c, b_s[:, c, :], hidH[:, 0, c, :])
            split_after("uq0")
            split_after("uq1")

            def exps(h, units):
                for u in units:
                    blocks = s_units[u]
                    n = NU * h + u
                    act.wait_ge(nmax_ready, n + 1)
                    if u == 0 and h >= 2:
                        act.wait_ge(pt_done, NG * (h - 1))
                    for i in blocks:
                        at = 0 if i != 1 else P
                        w = P * (i + 1)
                        e = 4 * (h % 2) + i
                        ins = act.activation(probs[:, h % 2, p_at[i]:p_at[i] + w], s_banks[n % 2][:, at:at + w], ACT.Exp,
                                             bias=nmx[:, e:e + 1], scale=SCALE, accum_out=sums[:, e:e + 1])
                    ins.then_inc(p_ready, 1)

            for h in range(HEADS + 2):
                if h < HEADS:
                    exps(h, (0, 1))
                if h >= 3 and h % 2 == 1:
                    pr = (h - 3) // 2
                    act.wait_ge(gemm_done, G["ot", pr] + 1)
                    act.activation(hidH[:, 1, pr, :], bank[G["ot", pr] % RING][:, :], ACT.Copy).then_inc(hid_hi, 1)
                if h < HEADS:
                    exps(h, (2,))
                if h == 3:
                    split_after("ewo0a")
                if h == 7:
                    split_after("ewo0b")
            for c in range(KD):
                finalize("mlp0", c, G["ewo1", c])
                if c == 3:
                    split_after("ewo1a")
            root(STAT["mlp0"], var_t[:, :])
            split_after("ewo1b")
            mlp(0)

            root(STAT["mix1"], var_t[:, :])
            root(STAT["mix1col"], vcol)
            split_after("glr")
            link(act.activation(lam_e, col("lam", 0, CH), ACT.Abs))
            act.activation(lam_e, lam_e, ACT.Exp, scale=-1.0).then_inc(lam_exp, 1)
            split_after("gq")
            act.wait_ge(gemm_out, G["z", 1] + 1)
            for p in range(2):
                link(act.activation(ge[:, p, :], cum[:, p, :], ACT.Abs))
                link(act.activation(ge[:, p, :], ge[:, p, :], ACT.Exp, scale=-1.0))
                act.activation(ge[:, p, :], ge[:, p, :], ACT.Ln, bias=ones[:, 0:1]).then_inc(ls_ready, 1)
            split_after("gk")
            act.wait_ge(cum_ready, 1)
            act.activation(ge[:, :, :], cum[:, :, :], ACT.Exp, scale=1 / GTAU).then_inc(e_ready, 1)
            act.wait_ge(e_used, 1)
            act.activation(ge[:, :, :], cum[:, :, :], ACT.Exp, scale=-1 / GTAU).then_inc(e_ready, 1)
            ends = cum[:, :, :].rearrange("p a (n t) -> p a n t", t=GCH)[:, :, :, GCH - 1]
            act.activation(decay, ends, ACT.Exp, scale=1 / GTAU).then_inc(e_ready, 1)
            act.wait_ge(cum_ready, 2)
            act.activation(ge[:, :, :], ge[:, :, :], ACT.Exp, scale=1 / GTAU).then_inc(e_ready, 1)
            split_after("gv0")
            split_after("gv1")
            for h in range(GH):
                act.wait_ge(gemm_out, G["og", h] + 1)
                act.activation(og[:, h, :], og[:, h, :], ACT.Silu).then_inc(og_ready, 1)
                if h == 1:
                    split_after("og0")
            split_after("og1")

            def gelu(c):
                act.wait_ge(gemm_out, G["y", c] + 1)
                act.activation(gel[:, c, :], gel[:, c, :], ACT.Gelu_apprx_tanh).then_inc(gel_ready, 1)

            def gates(c):
                act.wait_ge(gemm_out, G["ri", c] + 1)
                if c == 0:
                    act.wait_ge(lam_ready, 1)
                act.activation(li[:, c % 2, :], li[:, c % 2, :], ACT.Sigmoid).then_inc(sig_ready, 1)
                link(act.activation(lr[:, c % 2, :], lr[:, c % 2, :], ACT.Sigmoid))
                if c:
                    act.wait_ge(mix_in, MIX_IN["lru"] + c)
                act.activation(tmpR[:, :], lr[:, c % 2, :], ACT.Tanh, scale=lam_k[:, c:c + 1])
                link(act.activation(lr[:, c % 2, :], lr[:, c % 2, :], ACT.Exp, scale=lam_nk[:, c:c + 1]))
                act.activation(tmpS[:, :], lr[:, c % 2, :], ACT.Square).then_inc(gates_ready, 1)
                act.wait_ge(lru_m, c + 1)
                act.activation(tmpR[:, :], tmpR[:, :], ACT.Sqrt).then_inc(lru_rt, 1)
                hid_split(MIX_IN["lru"] + c, gel[:, c, :], hidH[:, 0, c, :])

            gelu(0)
            gelu(1)
            split_after("y0")
            split_after("x0")
            gelu(2)
            gelu(3)
            split_after("y1")
            split_after("x1")
            for c in range(CH):
                gates(c)
            for h in range(GH):
                root(STAT["gla"] + h, var_t[:, :])
                hid_split(MIX_IN["gla"] + h, o_sb[:, h, :], hidH[:, 1, h, :])
            split_after("owo0a")
            split_after("owo0b")
            for c in range(KD):
                finalize("mlp1", c, G["owo1", c])
                if c == 3:
                    split_after("owo1a")
            root(STAT["mlp1"], var_t[:, :])
            split_after("owo1b")
            mlp(1)
            root(STAT["final"], vcol)

        @block.vector
        def _(dve):
            n_link = 0

            def link(ins):
                nonlocal n_link
                n_link += 1
                ins.then_inc(dve_link, 1)
                dve.wait_ge(dve_link, n_link)

            def f32(ap):
                return ap.bitcast(F32)

            def split(n, slot=None, size=2048):
                if isinstance(n, int):
                    slot, size = n, TILES[n][1] * TILES[n][2] or 2048
                dve.wait_ge(wh_ready, n + 1)
                dve.tensor_tensor(wL[:, slot % 2, 0:size], raw[:, slot % RAW, 0:size], f32(wH[:, slot % 2, 0:size]),
                                  ALU.subtract).then_inc(wl_ready, 1)

            def split_after(key):
                split(TILE[key] + 2)

            def out_of(k, rows=P, lo=0, cols=S):
                dve.wait_ge(gemm_done, k + 1)
                return bank[k % RING][lo:rows, 0:cols]

            def accumulate(n, first, half):
                dve.wait_ge(sq_ready, n + 1 - (GH if n > SQ["gla"] else 0))
                if first:
                    dve.tensor_copy(acc[:, half, :], tmpS[:, :]).then_inc(acc_ready, 1)
                else:
                    dve.wait_ge(acc_ready, n)
                    dve.tensor_tensor(acc[:, half, :], acc[:, half, :], tmpS[:, :], ALU.add).then_inc(acc_ready, 1)

            def finalize(norm, c):
                dve.wait_ge(hi_new, KD * INST[norm] + c + 1)
                dve.scalar_tensor_tensor(out=hgL[:, c, :], in0=hT[:, c, :], scalar=col(norm, c), in1=f32(hgH[:, c, :]),
                                         op0=ALU.mult, op1=ALU.subtract).then_inc(hg_ready, 1)
                accumulate(SQ[norm] + c, c == 0, STAT[norm] % 2)

            def one_over_rms(s, count, dst, var=None, source=None):
                var = var_t[:, :] if var is None else var
                source = stat_bank[:, :] if source is None else source
                dve.wait_ge(stat_done, s + 1)
                dve.tensor_scalar(var, source, 1.0 / count, EPS, ALU.mult, ALU.add).then_inc(var_ready, 1)
                dve.wait_ge(rt_ready, s + 1)
                link(dve.reciprocal(dst, var))

            def add_to_h(k, c):
                dve.tensor_tensor(hT[:, c, :], out_of(k), hT[:, c, :], ALU.add).then_inc(gemm_out, 1)

            def hid_low(hid, source, dst_hi, dst):
                dve.wait_ge(hid_hi, hid + 1)
                dve.tensor_tensor(dst, source, f32(dst_hi), ALU.subtract).then_inc(hid_ready, 1)

            def mlp(layer):
                n0, g0, h0 = TILE[f"mlp{layer}"], G[f"mlp{layer}", 0], HID[f"mlp{layer}"]

                def result(k, ring):
                    dve.wait_ge(gemm_done, k + 1)
                    return bank[ring % RING][:, :]

                def up(k, ring, hid, buf, chunks):
                    for m in chunks:
                        dve.scalar_tensor_tensor(out=tmpR[:, :], in0=result(k + m, ring + m), scalar=0.0, in1=rstd[:, :],
                                                 op0=ALU.max, op1=ALU.mult).then_inc(gemm_out, 1)
                        hid_low(hid + m, tmpS[:, :], hidH[:, buf, m, :], hidL[:, buf, m, :])

                def down(k, ring, chunks):
                    for c in chunks:
                        dve.tensor_tensor(hT[:, c, :], result(k + c, ring + c), hT[:, c, :], ALU.add).then_inc(gemm_out, 1)

                def lo(n, slot):
                    split(n + 2, slot + 2)

                for half in range(2):
                    up(g0, g0, h0, 0, (2 * half, 2 * half + 1))
                    lo(n0 + half, n0 + half)
                with dve.Fori(1, LOOPS + 1) as i:
                    for pair in range(2):
                        n, g, hid = n0 - 6 + 4 * pair, g0 + 4 - 24 + 12 * pair, h0 + 4 - 8 + 4 * pair
                        for half in range(2):
                            up(g + 24 * i, g, hid + 8 * i, (pair + 1) % 2, (2 * half, 2 * half + 1))
                            lo(n + half + 8 * i, n + half)
                        for half in range(2):
                            down(g + 4 + 24 * i, g + 4, range(4 * half, 4 * half + 4))
                            lo(n + 2 + half + 8 * i, n + 2 + half)
                n, g, hid = n0 + 2 + 8 * LOOPS, g0 + 4 + 24 * LOOPS, h0 + 4 + 8 * LOOPS
                for half in range(2):
                    up(g, g, hid, (BLOCKS - 1) % 2, (2 * half, 2 * half + 1))
                    split(n + half + 2)
                for half in range(2):
                    down(g + 4, g + 4, range(4 * half, 4 * half + 4))
                    if n + 4 + half < len(TILES):
                        split(n + 4 + half)
                for c in range(KD):
                    if layer == 0:
                        add_to_h(g + 12 + c, c)
                        finalize("mix1", c)
                    else:
                        add_to_h(G["last", c], c)
                        accumulate(SQ["final"] + c, c == 0, STAT["final"] % 2)
                        if c:
                            y_out(c - 1)
                    if c % 4 == 3 and n + 6 + c // 4 < len(TILES):
                        split(n + 6 + c // 4)

            def y_out(c):
                k = G["yt", c]
                dve.tensor_copy(y_tok[:, :, c * P:(c + 1) * P], out_of(k).rearrange("p (b f) -> p b f", b=TB)).then_inc(gemm_out, 1)

            rp = slice(64, 96)
            dve.wait_ge(ld_pos, 32)
            link(dve.tensor_copy(ang[rp, :], pos_i[rp, :]))
            link(dve.tensor_scalar(ang[rp, :], ang[rp, :], freq[rp, 0:1], None, ALU.mult))
            two_pi = 2 * np.pi
            C1 = 6.28125
            C2 = float(np.round((two_pi - C1) * 2 ** 20) / 2 ** 20)
            C3 = float(two_pi - C1 - C2)
            BIG = 1.5 * 2 ** 23
            for part, quarter in ((0, 0.25), (1, 0.0)):
                k = ang_k[rp, part, :]
                turns = rope_cs[rp, part, :]
                link(dve.tensor_scalar(k, ang[rp, :], 1 / two_pi, quarter, ALU.mult, ALU.add))
                link(dve.tensor_scalar(k, k, BIG, None, ALU.add))
                link(dve.tensor_scalar(turns, k, BIG, None, ALU.subtract))
                link(dve.scalar_tensor_tensor(out=k, in0=turns, scalar=-C1, in1=ang[rp, :], op0=ALU.mult, op1=ALU.add))
                link(dve.scalar_tensor_tensor(out=k, in0=turns, scalar=-C2, in1=k, op0=ALU.mult, op1=ALU.add))
                link(dve.scalar_tensor_tensor(out=k, in0=turns, scalar=-C3, in1=k, op0=ALU.mult, op1=ALU.add))
                link(dve.tensor_scalar(k, k, quarter * two_pi, 3.1415925, ALU.add, ALU.min))
                ins = dve.tensor_scalar(k, k, -3.1415925, None, ALU.max)
                if part == 0:
                    link(ins)
                else:
                    ins.then_inc(rope_arg, 1)
            dve.wait_ge(params_done, 1)
            dve.tensor_copy(pcol[:, :], stat_bank[:, 0:NPARAM]).then_inc(params_ready, 1)
            dve.wait_ge(params_ready, 1)
            split(0)
            split(1)
            for c in range(KD):
                dve.tensor_copy(hT[:, c, :], out_of(G["x", c])).then_inc(gemm_out, 1)
                finalize("mix0", c)
            one_over_rms(STAT["mix0"], D, rstd[:, :])

            def latent(c):
                dve.tensor_tensor(c_raw[:, c, :], out_of(G["cq", c]), rstd[:, :], ALU.mult).then_inc(gemm_out, 1)
                accumulate(SQ["q"] + c, c in (0, 3), STAT["q" if c < 3 else "kv"] % 2)

            latent(0)
            latent(1)
            split_after("cq01")
            latent(2)
            latent(3)
            split_after("cq2kv0")
            latent(4)
            dve.tensor_tensor(kr_s[rp, :], out_of(G["kr", 0], 96, 64), rstd[rp, :], ALU.mult).then_inc(gemm_out, 1)
            dve.wait_ge(gemm_out, G["kr", 0] + 1)
            dve.wait_ge(rope_ready, 2)
            link(dve.stream_shuffle(rope_tmp[rp, 0, :], kr_s[rp, :], [(i + ROPE // 2) % ROPE for i in range(ROPE)]))
            link(dve.tensor_tensor(kr_s[rp, :], kr_s[rp, :], rope_cs[rp, 0, :], ALU.mult))
            link(dve.tensor_tensor(rope_tmp[rp, 0, :], rope_tmp[rp, 0, :], rope_cs[rp, 1, :], ALU.mult))
            dve.tensor_tensor(kr_s[rp, :], kr_s[rp, :], rope_tmp[rp, 0, :], ALU.add).then_inc(kr_ready, 1)
            split_after("kv1kr")

            def scale_latent(c, gain):
                dve.scalar_tensor_tensor(out=c_raw[:, c, :], in0=c_raw[:, c, :], scalar=gain, in1=rstd_t[:, :],
                                         op0=ALU.mult, op1=ALU.mult).then_inc(cn_scaled, 1)

            def c_out(c):
                dve.tensor_tensor(c_s[:, c % 2, :], out_of(G["c", c]), rstd[:, :], ALU.mult).then_inc(gemm_out, 1)

            def u_out(c):
                dve.tensor_tensor(cu[:, c, 2:2 + S], out_of(G["u", c]), rstd[:, :], ALU.mult).then_inc(gemm_out, 1)

            def b_out(c):
                dve.tensor_tensor(b_s[:, c, :], out_of(G["b", c]), rstd[:, :], ALU.mult).then_inc(gemm_out, 1)

            def short_conv(c):
                dve.wait_ge(cu_ready, c + 1)
                if c:
                    dve.wait_ge(mix_in, MIX_IN["sconv"] + c)
                w = [col("evconv", CH * k + c) for k in range(SC_K)]
                link(dve.tensor_scalar(tmpR[:, :], cu[:, c, 0:S], w[0], None, ALU.mult))
                for k in range(1, SC_K):
                    link(dve.scalar_tensor_tensor(out=tmpR[:, :], in0=cu[:, c, k:k + S], scalar=w[k], in1=tmpR[:, :],
                                                  op0=ALU.mult, op1=ALU.add))
                dve.tensor_tensor(b_s[:, c, :], b_s[:, c, :], tmpR[:, :], ALU.mult).then_inc(mix_in, 1)

            link(dve.memset(cu[:, :, 0:SC_K - 1], 0.0))
            c_out(0)
            c_out(1)
            one_over_rms(STAT["q"], QR, rstd_t[:, :])
            for c in range(3):
                scale_latent(c, col("qg", c))
            one_over_rms(STAT["kv"], KVR, rstd_t[:, :])
            for c in range(2):
                scale_latent(3 + c, col("kvg", c))
            split_after("c0")
            for c in range(5):
                dve.wait_ge(cn_hi, c + 1)
                hi, lo = (hidH[:, 1, c, :], hidL[:, 1, c, :]) if c < 4 else (hidH[:, 0, 3, :], hidL[:, 0, 3, :])
                dve.tensor_tensor(lo, c_raw[:, c, :], f32(hi), ALU.subtract).then_inc(cn_ready, 1)
            u_out(0)
            u_out(1)
            split_after("u0")
            b_out(0)
            b_out(1)
            split_after("b0")
            short_conv(0)
            c_out(2)
            short_conv(1)
            c_out(3)
            split_after("c1")
            u_out(2)
            u_out(3)
            split_after("u1")
            b_out(2)
            b_out(3)
            split_after("b1")
            short_conv(2)
            for tb in range(TB):
                dve.tensor_copy(v_tok[:, tb, :], out_of(G["v", tb])).then_inc(gemm_out, 1)
            short_conv(3)
            for h in range(HEADS):
                dve.tensor_copy(kT[0:NOPE, h, :], out_of(G["k", h], NOPE)).then_inc(gemm_out, 1)
                if h < 3:
                    hid_low(HID["sconv"] + h, b_s[:, h, :], hidH[:, 0, h, :], hidL[:, 0, h, :])
            split_after("ukv")
            hid_low(HID["sconv"] + 3, b_s[:, 3, :], hidH[:, 0, 3, :], hidL[:, 0, 3, :])

            def q_out(h):
                dve.tensor_copy(qT[0:QK, h, :], out_of(G["q", h], QK)).then_inc(gemm_out, 1)
                dve.wait_ge(gemm_out, G["q", h] + 1)
                if h >= 2:
                    dve.wait_ge(q_roped, h - 1)
                dve.stream_shuffle(rope_tmp[rp, h % 2, :], qT[rp, h, :],
                                   [(i + ROPE // 2) % ROPE for i in range(ROPE)]).then_inc(q_turned, 1)

            for h in range(HEADS):
                q_out(h)
                if h == 3:
                    split_after("uq0")
            split_after("uq1")

            def maxima(h, u):
                n = NU * h + u
                dve.wait_ge(s_done, n + 1)
                for i in s_units[u]:
                    at = 0 if i != 1 else P
                    e = 4 * (h % 2) + i
                    link(dve.tensor_reduce(mx[:, e:e + 1], s_banks[n % 2][:, at:at + P * (i + 1)], AX_X, ALU.max))
                lo, hi = 4 * (h % 2) + s_units[u][0], 4 * (h % 2) + s_units[u][-1] + 1
                dve.tensor_scalar(nmx[:, lo:hi], mx[:, lo:hi], -SCALE, None, ALU.mult).then_inc(nmax_ready, 1)

            def turned_out(h):
                for g, blocks in enumerate(pt_groups):
                    n = NG * h + g
                    dve.wait_ge(pt_done, n + 1)
                    w = P * len(blocks)
                    dve.tensor_copy(probsT[:, h % 2, 4 * P * g:4 * P * g + w], pt_banks[n % 2][:, 0:w]).then_inc(pt_out, 1)

            def head_out(h):
                dve.wait_ge(o_done, h + 1)
                dve.wait_ge(p_ready, NU * (h + 1))
                link(dve.reciprocal(rinv, sums[:, 4 * (h % 2):4 * (h % 2) + 4]))
                dst = o_tok[:, h // 2 % 2, :, VD * (h % 2):VD * (h % 2) + VD]
                dve.tensor_tensor(dst, o_bank[:, 0:TB * VD].rearrange("p (b v) -> p b v", b=TB),
                                  rinv.unsqueeze(2).to_broadcast((P, TB, VD)), ALU.mult).then_inc(o_out, 1)

            for h in range(HEADS + 2):
                if h < HEADS:
                    maxima(h, 0)
                    maxima(h, 1)
                if 1 <= h <= HEADS:
                    turned_out(h - 1)
                if h >= 3 and h % 2 == 1:
                    pr = (h - 3) // 2
                    ot = out_of(G["ot", pr])
                    dve.wait_ge(hid_hi, HID["attn"] + pr + 1)
                    dve.tensor_tensor(hidL[:, 1, pr, :], ot, f32(hidH[:, 1, pr, :]), ALU.subtract).then_inc(gemm_out, 1)
                if h < HEADS:
                    maxima(h, 2)
                    add_to_h(G["ewo0", h], h)
                if h == 3:
                    split_after("ewo0a")
                if h == 7:
                    split_after("ewo0b")
                if 1 <= h <= HEADS:
                    head_out(h - 1)
            for c in range(KD):
                add_to_h(G["ewo1", c], c)
                finalize("mlp0", c)
                if c == 3:
                    split_after("ewo1a")
            one_over_rms(STAT["mlp0"], D, rstd[:, :])
            split_after("ewo1b")
            mlp(0)

            one_over_rms(STAT["mix1"], D, rstd[:, :])
            one_over_rms(STAT["mix1col"], D, rcol, vcol, stat_bank[:, 0:TB])
            dve.tensor_tensor(glr[:, :], out_of(G["glr", 0], GRANK), rstd[0:GRANK, :], ALU.mult).then_inc(gemm_out, 1)
            split_after("glr")

            dve.wait_ge(lam_exp, 1)
            link(dve.tensor_scalar(lam_d, lam_e, 2.0, None, ALU.add))
            link(dve.reciprocal(lam_d, lam_d))
            link(dve.tensor_tensor(lam_s, lam_e, lam_d, ALU.mult))
            link(dve.tensor_tensor(lam_s2, lam_s, lam_s, ALU.mult))
            link(dve.tensor_scalar(lam_p, lam_s2, 1 / 17, None, ALU.mult))
            for odd in (15, 13, 11, 9, 7, 5, 3):
                link(dve.scalar_tensor_tensor(out=lam_p, in0=lam_p, scalar=1 / odd, in1=lam_s2, op0=ALU.add, op1=ALU.mult))
            link(dve.scalar_tensor_tensor(out=lam_p, in0=lam_p, scalar=1.0, in1=lam_s, op0=ALU.add, op1=ALU.mult))
            link(dve.tensor_scalar(lam_d, col("lam", 0, CH), -1.0, 0.0, ALU.mult, ALU.max))
            link(dve.scalar_tensor_tensor(out=lam_p, in0=lam_p, scalar=2.0, in1=lam_d, op0=ALU.mult, op1=ALU.add))
            link(dve.tensor_scalar(lam_k, lam_p, LRU_C, None, ALU.mult))
            dve.tensor_scalar(lam_nk, lam_p, -LRU_C, None, ALU.mult).then_inc(lam_ready, 1)

            def scaled_out(name, c, dst):
                dve.tensor_tensor(dst, out_of(G[name, c]), rstd[:, :], ALU.mult).then_inc(gemm_out, 1)

            scaled_out("gq", 0, gq[:, 0, :])
            scaled_out("gq", 1, gq[:, 1, :])
            for p in range(2):
                dve.tensor_scalar(cum[:, p, :], out_of(G["z", p]), col("gbias", p), None, ALU.add).then_inc(gemm_out, 1)
            split_after("gq")
            scaled_out("gk", 0, gk[:, 0, :])
            scaled_out("gk", 1, gk[:, 1, :])
            split_after("gk")
            for p in range(2):
                dve.wait_ge(ls_ready, p + 1)
                link(dve.scalar_tensor_tensor(out=gki[:, p, :], in0=cum[:, p, :], scalar=0.0, in1=ge[:, p, :],
                                              op0=ALU.min, op1=ALU.subtract))
                ins = dve.tensor_tensor_scan(cum[:, p, :], resets[:, :], gki[:, p, :], 0.0, ALU.mult, ALU.add)
                if p == 0:
                    link(ins)
                else:
                    ins.then_inc(cum_ready, 1)

            def v_out(half):
                for tb in range(TB):
                    dve.tensor_scalar(gv[:, tb, 256 * half:256 * half + 256], out_of(G[f"gv{half}", tb], cols=256),
                                      rcol[:, tb:tb + 1], None, ALU.mult).then_inc(gemm_out, 1)

            v_out(0)
            dve.wait_ge(e_ready, 1)
            dve.scalar_tensor_tensor(out=gq[:, :, :], in0=gq[:, :, :], scalar=GDK ** -0.5, in1=ge[:, :, :],
                                     op0=ALU.mult, op1=ALU.mult).then_inc(e_used, 1)
            dve.wait_ge(e_ready, 3)
            link(dve.tensor_tensor(gki[:, :, :], gk[:, :, :], ge[:, :, :], ALU.mult))
            for p in range(2):
                by_chunk = cum[:, p, :].rearrange("p (n t) -> p n t", t=GCH)
                ins = dve.tensor_tensor(ge[:, p, :].rearrange("p (n t) -> p n t", t=GCH),
                                        by_chunk[:, :, GCH - 1:GCH].to_broadcast((P, NCH, GCH)), by_chunk, ALU.subtract)
                if p == 0:
                    link(ins)
                else:
                    ins.then_inc(cum_ready, 1)
            split_after("gv0")
            dve.wait_ge(e_ready, 4)
            dve.tensor_tensor(gk[:, :, :], gk[:, :, :], ge[:, :, :], ALU.mult).then_inc(gla_ready, 1)
            v_out(1)
            split_after("gv1")
            for h in range(GH):
                scaled_out("og", h, og[:, h, :])
                if h == 1:
                    split_after("og0")
            split_after("og1")
            link(dve.memset(xl[:, 0:LRU_K - 1], 0.0))
            dve.wait_ge(gla_ready, 1)
            scaled_out("y", 0, gel[:, 0, :])
            scaled_out("y", 1, gel[:, 1, :])
            split_after("y0")

            def lru_conv(c):
                if c:
                    dve.wait_ge(xc_ready, c)
                scaled_out("xl", c, xl[:, LRU_K - 1:LRU_K - 1 + S])
                dve.wait_ge(gemm_out, G["xl", c] + 1)
                w = [col("lconvw", CH * k + c) for k in range(LRU_K)]
                link(dve.tensor_scalar(xc[:, c, :], xl[:, 0:S], w[0], col("lconvb", c), ALU.mult, ALU.add))
                for k in range(1, LRU_K):
                    ins = dve.scalar_tensor_tensor(out=xc[:, c, :], in0=xl[:, k:k + S], scalar=w[k], in1=xc[:, c, :],
                                                   op0=ALU.mult, op1=ALU.add)
                    if k < LRU_K - 1:
                        link(ins)
                    else:
                        ins.then_inc(xc_ready, 1)

            def gates_out(c):
                if c >= 2:
                    dve.wait_ge(mix_in, MIX_IN["lru"] + c - 1)
                dve.tensor_scalar(lr[:, c % 2, :], out_of(G["ra", c]), col("ba", c), None, ALU.add).then_inc(gemm_out, 1)
                dve.tensor_scalar(li[:, c % 2, :], out_of(G["ri", c]), col("bi", c), None, ALU.add).then_inc(gemm_out, 1)

            def recurrence(c):
                dve.wait_ge(gates_ready, c + 1)
                dve.scalar_tensor_tensor(out=tmpR[:, :], in0=tmpS[:, :], scalar=1.0, in1=tmpR[:, :],
                                         op0=ALU.add, op1=ALU.mult).then_inc(lru_m, 1)
                dve.wait_ge(lru_rt, c + 1)
                dve.wait_ge(ix_ready, c + 1)
                link(dve.tensor_tensor(li[:, c % 2, :], li[:, c % 2, :], tmpR[:, :], ALU.mult))
                link(dve.tensor_tensor_scan(tmpS[:, :], lr[:, c % 2, :], li[:, c % 2, :], 0.0, ALU.mult, ALU.add))
                dve.wait_ge(gel_ready, c + 1)
                dve.tensor_tensor(gel[:, c, :], gel[:, c, :], tmpS[:, :], ALU.mult).then_inc(mix_in, 1)
                hid_low(HID["lru"] + c, gel[:, c, :], hidH[:, 0, c, :], hidL[:, 0, c, :])

            lru_conv(0)
            lru_conv(1)
            split_after("x0")
            scaled_out("y", 2, gel[:, 2, :])
            scaled_out("y", 3, gel[:, 3, :])
            split_after("y1")
            gates_out(0)
            gates_out(1)
            lru_conv(2)
            lru_conv(3)
            split_after("x1")
            for p in range(2):
                dve.tensor_copy(gkT[:, :, p * P:(p + 1) * P],
                                out_of(G["kt", p]).rearrange("p (b d) -> p b d", b=TB)).then_inc(gemm_out, 1)
            recurrence(0)
            recurrence(1)
            gates_out(2)
            gates_out(3)
            for p in range(2):
                dve.wait_ge(kv_done, p + 1)
                for n in range(NCH - 1):
                    kv = bank[3 + 2 * p + n % 2][:, (n // 2) * P:(n // 2 + 1) * P]
                    if n == 0:
                        ins = dve.tensor_copy(states[:, p, 1, :], kv)
                    else:
                        ins = dve.scalar_tensor_tensor(out=states[:, p, n + 1, :], in0=states[:, p, n, :],
                                                       scalar=decay[:, p, n:n + 1], in1=kv, op0=ALU.mult, op1=ALU.add)
                    if n < NCH - 2:
                        link(ins)
                    else:
                        ins.then_inc(states_ready, 1)
            for h in range(GH):
                dve.tensor_tensor(attT[:, h, :, :], out_of(G["att", h]).rearrange("p (b i) -> p b i", b=TB),
                                  gmask[:, :].unsqueeze(1).to_broadcast((P, TB, P)), ALU.mult).then_inc(gemm_out, 1)
            for h in range(GH):
                dve.tensor_copy(o_sb[:, h, :], out_of(G["o", h])).then_inc(gemm_out, 1)
            recurrence(2)
            recurrence(3)

            def head_square(h):
                if h >= 2:
                    dve.wait_ge(stat_done, STAT["gla"] + h - 1)
                dve.tensor_tensor(acc[:, h % 2, :], o_sb[:, h, :], o_sb[:, h, :], ALU.mult).then_inc(acc_ready, 1)

            dve.wait_ge(gemm_out, G["o", GH - 1] + 1)
            head_square(0)
            head_square(1)
            for h in range(GH):
                one_over_rms(STAT["gla"] + h, GDV, rstd_t[:, :])
                link(dve.tensor_tensor(o_sb[:, h, :], o_sb[:, h, :], rstd_t[:, :], ALU.mult))
                dve.wait_ge(og_ready, h + 1)
                dve.scalar_tensor_tensor(out=o_sb[:, h, :], in0=o_sb[:, h, :], scalar=col("glag", 0), in1=og[:, h, :],
                                         op0=ALU.mult, op1=ALU.mult).then_inc(mix_in, 1)
                if h + 2 < GH:
                    head_square(h + 2)
                hid_low(HID["gla"] + h, o_sb[:, h, :], hidH[:, 1, h, :], hidL[:, 1, h, :])
                add_to_h(G["owo0", 2 * h], 2 * h)
                add_to_h(G["owo0", 2 * h + 1], 2 * h + 1)
            split_after("owo0a")
            split_after("owo0b")
            for c in range(KD):
                add_to_h(G["owo1", c], c)
                finalize("mlp1", c)
                if c == 3:
                    split_after("owo1a")
            one_over_rms(STAT["mlp1"], D, rstd[:, :])
            split_after("owo1b")
            mlp(1)
            y_out(KD - 1)
            one_over_rms(STAT["final"], D, rcol, vcol, stat_bank[:, 0:TB])
            for b in range(TB):
                dve.tensor_scalar(y_tok[:, b, :], y_tok[:, b, :], rcol[:, b:b + 1], None, ALU.mult).then_inc(y_scaled, 1)

        @block.tensor
        def _(pe):
            mm = nc.tensor.matmul

            def ring(k, static=None):
                if static is not None or k >= RING:
                    pe.wait_ge(gemm_out, k - RING + 1)
                return bank[(k if static is None else static) % RING]

            def tile(n, slot=None, kc=None, cols=None):
                if slot is None:
                    slot, kc, cols = n, TILES[n][1], TILES[n][2]
                pe.wait_ge(wl_ready, n + 1)
                return tile_view(wH, slot % 2, kc, cols), tile_view(wL, slot % 2, kc, cols)

            def project(dst, w, xs, c0, m=P, ready=None):
                wh, wl = w
                for kc, (xh, xlo) in enumerate(xs):
                    if ready is not None:
                        ready(kc)
                    for n, (a, b) in enumerate(((wh, xh), (wh, xlo), (wl, xh))):
                        last = mm(dst, a[:, kc, c0:c0 + m], b, start=(kc == 0 and n == 0),
                                  stop=(kc == len(xs) - 1 and n == 2))
                return last

            def project_tokens(dst, w, xs, tb, cols):
                wh, wl = (v(cols) for v in w)
                for kc, (xh, xlo) in enumerate(xs):
                    at = slice(tb * P, (tb + 1) * P)
                    for n, (a, b) in enumerate(((xh, wh), (xh, wl), (xlo, wh))):
                        last = mm(dst, a[:, at], b[kc], start=(kc == 0 and n == 0), stop=(kc == len(xs) - 1 and n == 2))
                return last

            hg = [(hgH[:, c, :], hgL[:, c, :]) for c in range(KD)]
            hid = [[(hidH[:, b, c, :], hidL[:, b, c, :]) for c in range(4)] for b in range(2)]
            latent_q = hid[1][0:3]
            latent_kv = [hid[1][3], hid[0][3]]

            def hg_wait(norm):
                return lambda kc: pe.wait_ge(hg_ready, KD * INST[norm] + kc + 1)

            def hid_wait(h0):
                return lambda kc: pe.wait_ge(hid_ready, h0 + kc + 1)

            def statistic(s, squares, by_token=False):
                pe.wait_ge(acc_ready, squares)
                if s:
                    pe.wait_ge(var_ready, s)
                a = acc[:, s % 2, :]
                if by_token:
                    for b in range(TB):
                        last = mm(stat_bank[:, b:b + 1], a[:, b * P:(b + 1) * P], ones[:, 0:1], start=True, stop=True)
                else:
                    last = mm(stat_bank[:, :], ones[:, :], a, start=True, stop=True)
                last.then_inc(stat_done, 1)

            pe.wait_ge(consts_ready, 1)
            pe.wait_ge(ld_prm, 16 * len(PARAM_ROWS))
            pe.transpose(stat_bank[:, 0:NPARAM], prm[:, :], ident[0:NPARAM, 0:NPARAM]).then_inc(params_done, 1)
            for c in range(KD):
                dst = ring(G["x", c])
                for b in range(TB):
                    if c == 0:
                        pe.wait_ge(ld_x[b], 16)
                    last = pe.transpose(dst[:, b * P:(b + 1) * P], x_tok[:, b, c * P:(c + 1) * P], ident[:, :])
                last.then_inc(gemm_done, 1)

            def pair_of(key, names, norm=None, m=P):
                w = tile(TILE[key])
                for i, name in enumerate(names):
                    project(ring(G[name])[:, :], w, hg, i * P, ready=hg_wait(norm) if norm and i == 0 else None).then_inc(gemm_done, 1)
                    if norm and i == 0:
                        statistic(STAT[norm], SQ[norm] + KD)

            pair_of("cq01", [("cq", 0), ("cq", 1)], "mix0")
            pair_of("cq2kv0", [("cq", 2), ("cq", 3)])
            w = tile(TILE["kv1kr"])
            project(ring(G["cq", 4])[:, :], w, hg, 0).then_inc(gemm_done, 1)
            project(ring(G["kr", 0])[0:96, :], w, hg, 64, 96).then_inc(gemm_done, 1)
            for g in range(2):
                for n in "cub":
                    pair_of(f"{n}{g}", [(n, 2 * g), (n, 2 * g + 1)])
                    if g == 0 and n == "c":
                        statistic(STAT["q"], SQ["q"] + 3)
                        statistic(STAT["kv"], SQ["q"] + 5)
            wh, wl = tile(TILE["ukv"])
            pe.wait_ge(cn_ready, 5)

            def value_cols(v):
                return lambda _: [v[:, k, :].rearrange("p (h d) -> p h d", h=HEADS)[:, :, NOPE:NOPE + VD] for k in range(2)]

            for tb in range(TB):
                dst = ring(G["v", tb])[:, :].rearrange("p (h d) -> p h d", h=HEADS)
                project_tokens(dst, (value_cols(wh), value_cols(wl)), latent_kv, tb, None).then_inc(gemm_done, 1)
            for h in range(HEADS):
                project(ring(G["k", h])[:, :], (wh, wl), latent_kv, P * h).then_inc(gemm_done, 1)
            for g in range(2):
                w = tile(TILE[f"uq{g}"])
                for h in range(4 * g, 4 * g + 4):
                    project(ring(G["q", h])[0:QK, :], w, latent_q, QK * (h % 4), QK).then_inc(gemm_done, 1)

            def scores(h, u):
                n = NU * h + u
                if u == 0:
                    pe.wait_ge(q_roped, h + 1)
                    pe.wait_ge(kr_spread, h + 1)
                    pe.wait_ge(gemm_out, G["q", h] + 1)
                if n >= 2:
                    pe.wait_ge(p_ready, n - 1)
                for i in s_units[u]:
                    at = 0 if i != 1 else P
                    dst = s_banks[n % 2]
                    mm(dst[:, at:at + P * (i + 1)], qT[0:QK, h, i * P:(i + 1) * P], kT[0:QK, h, 0:P * (i + 1)],
                       start=True, stop=False)
                    last = mm(dst[:, at + P * i:at + P * (i + 1)], identb[:, :], causal[:, :], start=False, stop=True)
                last.then_inc(s_done, 1)

            def turn(h):
                pe.wait_ge(p_ready, NU * (h + 1))
                for g, blocks in enumerate(pt_groups):
                    n = NG * h + g
                    if n >= 2:
                        pe.wait_ge(pt_out, n - 1)
                    for b, (j, i) in enumerate(blocks):
                        last = pe.transpose(pt_banks[n % 2][:, b * P:(b + 1) * P],
                                            probs[:, h % 2, p_at[i] + j * P:p_at[i] + (j + 1) * P], ident[:, :])
                    last.then_inc(pt_done, 1)

            def weigh(h):
                pe.wait_ge(pt_out, NG * (h + 1))
                if h:
                    pe.wait_ge(o_out, h)
                for i in range(TB):
                    for j in range(i + 1):
                        at = P * turned.index((j, i))
                        last = mm(o_bank[:, i * VD:(i + 1) * VD], probsT[:, h % 2, at:at + P],
                                  v_tok[:, j, h * VD:(h + 1) * VD], start=(j == 0), stop=(j == i))
                last.then_inc(o_done, 1)

            pe.wait_ge(gemm_out, G["v", TB - 1] + 1)
            for h in range(HEADS + 2):
                if h < HEADS:
                    scores(h, 0)
                    scores(h, 1)
                if 1 <= h <= HEADS:
                    turn(h - 1)
                if h >= 3 and h % 2 == 1:
                    pr = (h - 3) // 2
                    pe.wait_ge(o_out, 2 * pr + 2)
                    dst = ring(G["ot", pr])
                    for b in range(TB):
                        last = pe.transpose(dst[:, b * P:(b + 1) * P], o_tok[:, pr % 2, b, :], ident[:, :])
                    last.then_inc(gemm_done, 1)
                if h < HEADS:
                    scores(h, 2)
                    if h % 4 == 0:
                        wo = tile(TILE["ewo0" + "ab"[h // 4]])
                    project(ring(G["ewo0", h])[:, :], wo, hid[0], P * (h % 4),
                            ready=hid_wait(READY["sconv"]) if h == 0 else None).then_inc(gemm_done, 1)
                if 1 <= h <= HEADS:
                    weigh(h - 1)

            def down(name, half, buf, chunks):
                wo = tile(TILE[f"{name}{half}"])
                for c in chunks:
                    project(ring(G[name, c])[:, :], wo, hid[buf], P * (c % 4)).then_inc(gemm_done, 1)

            pe.wait_ge(gemm_out, G["ot", HEADS // 2 - 1] + 1)
            down("ewo1", "a", 1, range(4))
            down("ewo1", "b", 1, range(4, 8))

            def mlp(layer):
                n0, g0, h0 = TILE[f"mlp{layer}"], G[f"mlp{layer}", 0], READY[f"mlp{layer}"]

                def up(n, slot, k, rk, norm=None):
                    for half in range(2):
                        w = tile(n + half, slot + half, KD, 256)
                        for m in range(2):
                            c = 2 * half + m
                            first = norm and c == 0
                            project(ring(k + c, rk + c)[:, :], w, hg, m * P,
                                    ready=hg_wait(norm) if first else None).then_inc(gemm_done, 1)
                            if first:
                                statistic(STAT[norm], SQ[norm] + KD)

                def down(n, slot, k, rk, hid0, buf):
                    pe.wait_ge(hid_ready, hid0 + 4)
                    for half in range(2):
                        w = tile(n + half, slot + half, 4, 512)
                        for m in range(4):
                            c = 4 * half + m
                            project(ring(k + c, rk + c)[:, :], w, hid[buf], m * P).then_inc(gemm_done, 1)

                up(n0, n0, g0, g0, f"mlp{layer}")
                with pe.Fori(1, LOOPS + 1) as i:
                    for pair in range(2):
                        n, g = n0 - 6 + 4 * pair, g0 + 4 - 24 + 12 * pair
                        up(n + 8 * i, n, g + 24 * i, g)
                        down(n + 2 + 8 * i, n + 2, g + 4 + 24 * i, g + 4, h0 - 8 + 4 * pair + 8 * i, pair)
                n, g = n0 + 2 + 8 * LOOPS, g0 + 4 + 24 * LOOPS
                up(n, n, g, g)
                down(n + 2, n + 2, g + 4, g + 4, h0 + 8 * LOOPS, 0)
                if layer == 0:
                    down(n + 4, n + 4, g + 12, g + 12, h0 + 4 + 8 * LOOPS, 1)
                    return
                pe.wait_ge(hid_ready, h0 + 4 * BLOCKS)
                for c in range(KD):
                    if c % 4 == 0:
                        w = tile(n + 4 + c // 4, n + 4 + c // 4, 4, 512)
                    project(ring(G["last", c])[:, :], w, hid[1], P * (c % 4)).then_inc(gemm_done, 1)
                    if c:
                        y_turn(c - 1)

            def y_turn(c):
                pe.wait_ge(y_new, c + 1)
                dst = ring(G["yt", c])
                for b in range(TB):
                    last = pe.transpose(dst[:, b * P:(b + 1) * P], yT[:, c, b * P:(b + 1) * P], ident[:, :])
                last.then_inc(gemm_done, 1)

            mlp(0)

            w = tile(TILE["glr"])
            project(ring(G["glr", 0])[:, :], w, hg, 0, ready=hg_wait("mix1")).then_inc(gemm_done, 1)
            statistic(STAT["mix1"], SQ["mix1"] + KD)
            pe.wait_ge(var_ready, STAT["mix1"] + 1)
            for b in range(TB):
                last = mm(stat_bank[:, b:b + 1], acc[:, STAT["mix1"] % 2, b * P:(b + 1) * P], ones[:, 0:1], start=True, stop=True)
            last.then_inc(stat_done, 1)
            pair_of("gq", [("gq", 0), ("gq", 1)])
            pe.wait_ge(ld_gup, 16)
            pe.wait_ge(gemm_out, G["glr", 0] + 1)
            for p in range(2):
                mm(ring(G["z", p])[:, :], gup[:, p * P:(p + 1) * P], glr[:, :], start=True, stop=True).then_inc(gemm_done, 1)
            pair_of("gk", [("gk", 0), ("gk", 1)])
            for half in range(2):
                wh, wl = tile(TILE[f"gv{half}"])
                cols = [(lambda v: (lambda _: [v[:, k, :] for k in range(KD)]))(v) for v in (wh, wl)]
                for tb in range(TB):
                    project_tokens(ring(G[f"gv{half}", tb])[:, 0:256], cols, hg, tb, None).then_inc(gemm_done, 1)
            pair_of("og0", [("og", 0), ("og", 1)])
            pair_of("og1", [("og", 2), ("og", 3)])
            pair_of("y0", [("y", 0), ("y", 1)])
            pair_of("x0", [("xl", 0), ("xl", 1)])
            pair_of("y1", [("y", 2), ("y", 3)])

            def lru_gates(c):
                pe.wait_ge(xc_ready, c + 1)
                pe.wait_ge(ld_wgate, 64)
                for gate, name in enumerate(("ra", "ri")):
                    mm(ring(G[name, c])[:, :], wgate[:, gate, c, :], xc[:, c, :], start=True, stop=True).then_inc(gemm_done, 1)

            lru_gates(0)
            lru_gates(1)
            pair_of("x1", [("xl", 2), ("xl", 3)])
            pe.wait_ge(gla_ready, 1)
            for p in range(2):
                dst = ring(G["kt", p])
                for b in range(TB):
                    last = pe.transpose(dst[:, b * P:(b + 1) * P], gk[:, p, b * P:(b + 1) * P], ident[:, :])
                last.then_inc(gemm_done, 1)
            for p in range(2):
                pe.wait_ge(gemm_out, G["kt", p] + 1)
                for n in range(NCH - 1):
                    tok = slice(GCH * (n % 2), GCH * (n % 2) + GCH)
                    for side in range(2):
                        h = 2 * p + side
                        last = mm(bank[3 + 2 * p + n % 2][64 * side:64 * side + 64, (n // 2) * P:(n // 2 + 1) * P],
                                  gkT[tok, n // 2, P * p + 64 * side:P * p + 64 * side + 64],
                                  gv[tok, n // 2, h * GDV:(h + 1) * GDV], start=True, stop=True)
                last.then_inc(kv_done, 1)
            lru_gates(2)
            lru_gates(3)
            for h in range(GH):
                half, p = slice(64 * (h % 2), 64 * (h % 2) + 64), h // 2
                dst = ring(G["att", h])
                for b in range(TB):
                    last = mm(dst[:, b * P:(b + 1) * P], gki[half, p, b * P:(b + 1) * P], gq[half, p, b * P:(b + 1) * P],
                              start=True, stop=True)
                last.then_inc(gemm_done, 1)
            for h in range(GH):
                half, p = slice(64 * (h % 2), 64 * (h % 2) + 64), h // 2
                pe.wait_ge(states_ready, p + 1)
                pe.wait_ge(gemm_out, G["att", h] + 1)
                dst = ring(G["o", h])
                for b in range(TB):
                    mm(dst[:, b * P:(b + 1) * P], gv[:, b, h * GDV:(h + 1) * GDV], attT[:, h, b, :], start=True, stop=False)
                    for n in (2 * b, 2 * b + 1):
                        if n:
                            last = mm(dst[:, n * GCH:(n + 1) * GCH], states[half, p, n, :], gq[half, p, n * GCH:(n + 1) * GCH],
                                      start=False, stop=(n % 2 == 1))
                last.then_inc(gemm_done, 1)
            for h in range(GH):
                statistic(STAT["gla"] + h, SQ["gla"] + h + 1)
                if h % 2 == 0:
                    wo = tile(TILE["owo0" + "ab"[h // 2]])
                for c in (2 * h, 2 * h + 1):
                    project(ring(G["owo0", c])[:, :], wo, hid[0], P * (c % 4),
                            ready=hid_wait(READY["lru"]) if c == 0 else None).then_inc(gemm_done, 1)
            pe.wait_ge(hid_ready, READY["gla"] + GH)
            down("owo1", "a", 1, range(4))
            down("owo1", "b", 1, range(4, 8))
            mlp(1)
            y_turn(KD - 1)
            statistic(STAT["final"], SQ["final"] + KD, by_token=True)


_INS = ['x', 'positions', 'mixer_norm_g', 'mlp_norm_g', 'mlp_w1', 'mlp_w2', 'final_norm_g', 'ev_w_in', 'ev_conv_w',
        'mla_q_norm_g', 'mla_w_uq', 'mla_kv_norm_g', 'mla_w_ukv', 'ev_w_out', 'od_w_in', 'gla_w_gate_up', 'gla_b_gate',
        'gla_norm_g', 'lru_conv_w', 'lru_conv_b', 'lru_w_a', 'lru_b_a', 'lru_w_i', 'lru_b_i', 'lru_lambda', 'od_w_out']


def kernel(**inputs):
    import concourse.bacc as bacc
    from concourse.bass_utils import run_bass_kernel_spmd

    nc = bacc.Bacc("TRN2", target_bir_lowering=False, num_devices=1)
    arrays, t = {}, {}
    for name in _INS:
        a = np.ascontiguousarray(inputs[name])
        arrays[f"in_{name}"] = a
        t[name] = nc.dram_tensor(f"in_{name}", a.shape, mybir.dt.from_np(a.dtype), kind="ExternalInput").ap()
    freq = np.float32(10000.0) ** (-np.arange(0, ROPE, 2, dtype=np.float32) / np.float32(ROPE))
    table = np.stack([np.concatenate([freq, freq]), np.repeat(np.array([-1, 1], np.float32), ROPE // 2)], 1)
    arrays["in_rope_freq"] = np.ascontiguousarray(table.astype(np.float32))
    t["rope_freq"] = nc.dram_tensor("in_rope_freq", table.shape, F32, kind="ExternalInput").ap()
    out = nc.dram_tensor("out_0", (1, S, D), F32, kind="ExternalOutput").ap()
    trunk(nc, t, out)
    r = run_bass_kernel_spmd(nc, [arrays], core_ids=[0])
    return r.results[0]["out_0"]
```

```python
from contextlib import ExitStack

import numpy as np

import concourse.bass as bass
from concourse import mybir

F32 = mybir.dt.float32
F32R = mybir.dt.float32r
BF16 = mybir.dt.bfloat16
I32 = mybir.dt.int32
ALU = mybir.AluOpType
ACT = mybir.ActivationFunctionType
AX_X = mybir.AxisListType.X

P = 128
S = 512
D = 1024
KD = D // P
TB = S // P
D_FF = 4 * D
EPS = 1e-6
CH = 512 // P

SC_K = 3
HEADS, NOPE, ROPE, VD = 8, 64, 32, 64
QR, KVR = 384, 256
QK = NOPE + ROPE
SCALE = QK ** -0.5
MASKED = -1e37

GH, GDK, GDV, GRANK, GTAU, GCH = 4, 64, 128, 16, 16.0, 64
NCH = S // GCH
LRU_K, LRU_C = 4, 8.0

RAW = 4
RING = 3
BLOCKS = D_FF // 512

PARAM_ROWS = [("mix0", KD), ("mlp0", KD), ("mix1", KD), ("mlp1", KD), ("final", KD), ("qg", 3), ("kvg", 2),
              ("evconv", SC_K * CH), ("gbias", 2), ("glag", 1), ("lconvw", LRU_K * CH), ("lconvb", CH),
              ("ba", CH), ("bi", CH), ("lam", CH)]
PCOL = {}
_n = 0
for _name, _rows in PARAM_ROWS:
    PCOL[_name] = _n
    _n += _rows
NPARAM = _n


def tile_table():
    tiles = [("cq01", KD, 256), ("cq2kv0", KD, 256), ("kv1kr", KD, 160)]
    for g in range(2):
        tiles += [(f"c{g}", KD, 256), (f"u{g}", KD, 256), (f"b{g}", KD, 256)]
    tiles += [("ukv", 2, 1024), ("uq0", 3, 384), ("uq1", 3, 384)]
    tiles += [("ewo0a", 4, 512), ("ewo0b", 4, 512), ("ewo1a", 4, 512), ("ewo1b", 4, 512)]
    tiles += [("mlp0", 0, 0)] * (4 * BLOCKS)
    tiles += [("glr", KD, 128), ("gq", KD, 256), ("gk", KD, 256)]
    for g in range(2):
        tiles += [(f"x{g}", KD, 256), (f"y{g}", KD, 256)]
    tiles += [("gv0", KD, 256), ("gv1", KD, 256), ("og0", KD, 256), ("og1", KD, 256)]
    tiles += [("owo0a", 4, 512), ("owo0b", 4, 512), ("owo1a", 4, 512), ("owo1b", 4, 512)]
    tiles += [("mlp1", 0, 0)] * (4 * BLOCKS)
    return tiles


STEPS = HEADS + 2
Q_AHEAD = 2


def gemm_order():
    order, last = [], {}

    def use(tile, names):
        order.extend(names)
        last[tile] = len(order)

    order += [("x", c) for c in range(KD)]
    use("cq01", [("cq", 0), ("cq", 1)])
    use("cq2kv0", [("cq", 2), ("cq", 3)])
    use("kv1kr", [("cq", 4), ("kr", 0)])
    for g in range(2):
        for n in "cub":
            use(f"{n}{g}", [(n, 2 * g), (n, 2 * g + 1)])
    use("ukv", [("v", t) for t in range(TB)] + [("k", h) for h in range(HEADS)])
    order += [("q", h) for h in range(Q_AHEAD)]
    for step in range(STEPS):
        h = step + Q_AHEAD
        if h < HEADS:
            order.append(("q", h))
            if h == 3:
                last["uq0"] = len(order)
            if h == 7:
                last["uq1"] = len(order)
        if step >= 3 and step % 2 == 1:
            order.append(("ot", (step - 3) // 2))
        if step >= 2:
            order.append(("ewo0", step - 2))
            if step == 5:
                last["ewo0a"] = len(order)
            if step == 9:
                last["ewo0b"] = len(order)
    use("ewo1a", [("ewo1", c) for c in range(4)])
    use("ewo1b", [("ewo1", c) for c in range(4, 8)])
    order += [("mlp0", i) for i in range(12 * BLOCKS)]
    use("glr", [("glr", 0)])
    use("gq", [("gq", 0), ("gq", 1)])
    order += [("z", 0), ("z", 1)]
    use("gk", [("gk", 0), ("gk", 1)])
    use("x0", [("xl", 0), ("xl", 1)])
    use("y0", [("y", 0), ("y", 1)])
    order += [("ra", 0), ("ri", 0), ("ra", 1), ("ri", 1)]
    use("x1", [("xl", 2), ("xl", 3)])
    use("y1", [("y", 2), ("y", 3)])
    order += [("ra", 2), ("ri", 2), ("ra", 3), ("ri", 3)]
    use("gv0", [("gv0", t) for t in range(TB)])
    use("gv1", [("gv1", t) for t in range(TB)])
    use("og0", [("og", 0), ("og", 1)])
    use("og1", [("og", 2), ("og", 3)])
    order += [("kt", 0), ("kt", 1)]
    order += [("att", h) for h in range(GH)]
    order += [("owo0", c) for c in range(2)]
    order += [("o", h) for h in range(GH)]
    order += [("owo0", c) for c in range(2, 4)]
    last["owo0a"] = len(order)
    use("owo0b", [("owo0", c) for c in range(4, 8)])
    use("owo1a", [("owo1", c) for c in range(4)])
    use("owo1b", [("owo1", c) for c in range(4, 8)])
    order += [("mlp1", i) for i in range(12 * BLOCKS - 8)]
    for c in range(KD):
        order.append(("last", c))
        if c:
            order.append(("yt", c - 1))
    order.append(("yt", KD - 1))
    return order, {key: n for n, key in enumerate(order)}, last


TILES = tile_table()
TILE = {}
for _i, (_key, _k, _c) in enumerate(TILES):
    TILE.setdefault(_key, _i)
ORDER, G, TILE_LAST = gemm_order()

BY_ACT = ("v", "k", "z", "ra", "ri", "gv0", "gv1", "kt", "o")
MOVED = []
_act = _dve = 0
for _key in ORDER:
    if _key[0] in BY_ACT:
        _act += 1
        MOVED.append((True, _act))
    else:
        _dve += 1
        MOVED.append((False, _dve))

HID = {"sconv": 0, "attn": 4, "mlp0": 8, "lru": 8 + 4 * BLOCKS, "gla": 12 + 4 * BLOCKS, "mlp1": 16 + 4 * BLOCKS}
READY = {"sconv": 0, "mlp0": 4, "lru": 4 + 4 * BLOCKS, "gla": 8 + 4 * BLOCKS, "mlp1": 12 + 4 * BLOCKS}
MIX_IN = {"sconv": 0, "lru": 4, "gla": 8}
STATS = [("mix0", KD, True), ("q", 3, True), ("kv", 2, True), ("mlp0", KD, True), ("mix1", KD, True)]
STATS += [(f"gla{h}", 1, True) for h in range(GH)] + [("mlp1", KD, True), ("final", KD, False)]
STAT = {name: i for i, (name, _, _) in enumerate(STATS)}
SPREAD = {name: sum(b for _, _, b in STATS[:i]) for i, (name, _, _) in enumerate(STATS)}
SQ, ADDS = {}, {}
_s = _a = 0
for _name, _chunks, _ in STATS:
    SQ[_name], ADDS[_name] = _s, _a
    _s += _chunks
    _a += _chunks - 1
INST = {"mix0": 0, "mlp0": 1, "mix1": 2, "mlp1": 3}


def trunk(nc, t, out):
    ctx = ExitStack()
    with ctx:
        arena_bytes = 0
        places = []

        def place(name, shape, dt, at=None):
            nonlocal arena_bytes
            size = int(np.prod(shape[1:])) * mybir.dt.size(dt)
            size = (size + 31) // 32 * 32
            where = arena_bytes if at is None else at
            if at is None:
                arena_bytes += size
            places.append(where + size)
            return nc.alloc_sbuf_tensor_at(name, shape, dt, offset=base + where), where

        base = (nc.sbuf_base + 31) // 32 * 32

        hT, _ = place("hT", [P, KD, S], F32)
        hgH, hg_at = place("hgH", [P, KD, S], F32R)
        hgL, _ = place("hgL", [P, KD, S], F32R)
        raw, _ = place("raw", [P, RAW, 2048], F32)
        wH, _ = place("wH", [P, 2, 2048], F32R)
        wL, _ = place("wL", [P, 2, 2048], F32R)
        hidH, hidH_at = place("hidH", [P, 2, 4, S], F32R)
        hidL, hidL_at = place("hidL", [P, 2, 4, S], F32R)
        rstd, _ = place("rstd", [P, S], F32)
        sqb, _ = place("sqb", [P, 2, S], F32)
        diag, _ = place("diag", [P, TB, P], F32)
        acc, _ = place("acc", [P, 2, S], F32)
        tmpR, _ = place("tmpR", [P, S], F32)
        tmpS, _ = place("tmpS", [P, S], F32)
        ident, _ = place("ident", [P, P], F32)
        ones, _ = place("ones", [P, P], F32)
        identb, _ = place("identb", [P, P], BF16)
        causal, _ = place("causal", [P, P], BF16)
        pcol, _ = place("pcol", [P, NPARAM], F32)
        small, _ = place("small", [P, 92], F32)
        resets, _ = place("resets", [P, S], F32)
        gmask, _ = place("gmask", [P, P], F32)
        gup, _ = place("gup", [GRANK, 2 * P], F32)
        area_at = arena_bytes

        NS = P * TB * (TB + 1) // 2
        conv_at = area_at + 22528
        v_tok, _ = place("v_tok", [P, TB, HEADS * VD], F32, area_at)
        o_tok, _ = place("o_tok", [P, 2, TB, P], F32, area_at + 8192)
        c_raw, _ = place("c_raw", [P, 5, S], F32, area_at)
        rope_cs, _ = place("rope_cs", [P, S], F32, area_at + 12288)
        kr_s, _ = place("kr_s", [P, S], F32, area_at + 16384)
        rope_tmp, _ = place("rope_tmp", [P, 2, S], F32, area_at + 18432)
        b_s, _ = place("b_s", [P, CH, S], F32, conv_at)
        cu, _ = place("cu", [P, CH, S + SC_K - 1], F32, conv_at + 8192)
        c_s, _ = place("c_s", [P, 2, S], F32, conv_at + 16416)
        probs, _ = place("probs", [P, 2, NS], F32, conv_at)
        probsT, _ = place("probsT", [P, 2, NS], F32, conv_at + 8 * NS)
        qT, _ = place("qT", [P, HEADS, S], F32, hg_at)
        kT, _ = place("kT", [P, HEADS, S], F32, hg_at + 4 * HEADS * S)
        x_tok, _ = place("x_tok", [P, TB, D], F32, conv_at)
        prm, _ = place("prm", [NPARAM, P], F32, area_at + 16384)
        pos_i, _ = place("pos_i", [P, S], I32, area_at + 18432)
        ang, _ = place("ang", [P, S], F32, area_at + 20480)
        ang_k, _ = place("ang_k", [P, S], F32, area_at + 14336)
        turns, _ = place("turns", [P, S], F32, area_at)
        gq, _ = place("gq", [P, 2, S], F32, area_at)
        gk, _ = place("gk", [P, 2, S], F32, area_at + 4096)
        gki, _ = place("gki", [P, 2, S], F32, area_at + 8192)
        cum, _ = place("cum", [P, 2, S], F32, area_at + 12288)
        ge, _ = place("ge", [P, 2, S], F32, area_at + 16384)
        glr, _ = place("glr", [GRANK, S], F32, area_at + 16384)
        gel, _ = place("gel", [P, CH, S], F32, area_at + 12288)
        gv, _ = place("gv", [P, TB, GH * GDV], F32, area_at + 20480)
        og, _ = place("og", [P, GH, S], F32, area_at + 28672)
        xl, _ = place("xl", [P, S + LRU_K - 1], F32, area_at + 36864)
        wgate, _ = place("wgate", [P, 2, CH, P], F32, area_at + 38944)
        xc, _ = place("xc", [P, CH, S], F32, hidL_at + 8192)
        lr, _ = place("lr", [P, 2, S], F32, hidH_at + 8192)
        li, _ = place("li", [P, 2, S], F32, hidH_at + 12288)
        gkT, _ = place("gkT", [P, TB, 2 * P], F32, hg_at)
        attT, _ = place("attT", [P, GH, TB, P], F32, hg_at + 4096)
        states, _ = place("states", [P, 2, NCH, GDV], F32, hg_at + 12288)
        o_sb, _ = place("o_sb", [P, GH, S], F32, hg_at + 20480)
        yT, _ = place("yT", [P, KD, S], F32, hg_at)
        y_tok, _ = place("y_tok", [P, TB, D], F32, area_at)
        ctx.enter_context(nc.sbuf_tensor("arena", [P, (max(places) + 3) // 4], F32))

        bank = [ctx.enter_context(nc.psum_tensor(f"bank{i}", [P, S], F32)) for i in range(8)]
        stat_bank = o_bank = bank[7]
        s_banks, pt_banks = bank[3:5], bank[5:7]

        mx, nmx, sums, rinv = small[:, 0:8], small[:, 8:16], small[:, 16:24], small[:, 24:28]
        vcol, rcol, rcol_mix1 = small[:, 32:36], small[:, 28:32], small[:, 88:92]
        decay = small[:, 36:52].rearrange("p (a n) -> p a n", a=2)
        lam_e, lam_d, lam_s, lam_s2 = (small[:, 52 + 4 * i:56 + 4 * i] for i in range(4))
        lam_p, lam_k, lam_nk = (small[:, 68 + 4 * i:72 + 4 * i] for i in range(3))
        eps_col = small[:, 80:81]
        rope_par = small[:, 82:86]

        def col(name, c, n=1):
            return pcol[:, PCOL[name] + c:PCOL[name] + c + n]

        def sem(name):
            return ctx.enter_context(nc.semaphore(name))

        ld_x = [sem(f"ld_x{i}") for i in range(TB)]
        ld_freq, ld_prm, ld_pos, ld_gup, ld_wgate, ld_out = sem("ld_freq"), sem("ld_prm"), sem("ld_pos"), sem("ld_gup"), sem("ld_wgate"), sem("ld_out")
        raw_loaded = [sem(f"raw_loaded{i}") for i in range(RAW)]
        wh_ready, wl_ready = sem("wh_ready"), sem("wl_ready")
        gemm_done, gemm_out, gemm_out_act = sem("gemm_done"), sem("gemm_out"), sem("gemm_out_act")
        ident_ready, consts_ready, params_done, params_ready = sem("ident_ready"), sem("consts_ready"), sem("params_done"), sem("params_ready")
        hi_new, hg_ready, sq_ready, acc_ready = sem("hi_new"), sem("hg_ready"), sem("sq_ready"), sem("acc_ready")
        stat_done, var_ready, rt_ready = sem("stat_done"), sem("var_ready"), sem("rt_ready")
        diag_ready, spread_done, rstd_ready = sem("diag_ready"), sem("spread_done"), sem("rstd_ready")
        dve_link, act_link, pool_link = sem("dve_link"), sem("act_link"), sem("pool_link")
        rope_arg, rope_ready = sem("rope_arg"), sem("rope_ready")
        cn_scaled, cn_hi, cn_ready = sem("cn_scaled"), sem("cn_hi"), sem("cn_ready")
        cu_ready, mix_in, hid_hi, hid_ready = sem("cu_ready"), sem("mix_in"), sem("hid_hi"), sem("hid_ready")
        kr_ready, kr_copied = sem("kr_ready"), sem("kr_copied")
        q_nope, q_parts, q_roped = sem("q_nope"), sem("q_parts"), sem("q_roped")
        s_done, nmax_ready, p_ready = sem("s_done"), sem("nmax_ready"), sem("p_ready")
        pt_done, pt_out, pt_out_act, o_done, o_out = sem("pt_done"), sem("pt_out"), sem("pt_out_act"), sem("o_done"), sem("o_out")
        sq_self = sem("sq_self")
        ls_ready, cum_ready, e_ready, e_used = sem("ls_ready"), sem("cum_ready"), sem("e_ready"), sem("e_used")
        lam_exp, lam_ready, gel_ready, og_ready = sem("lam_exp"), sem("lam_ready"), sem("gel_ready"), sem("og_ready")
        gla_ready, kv_done, states_ready = sem("gla_ready"), sem("kv_done"), sem("states_ready")
        xc_ready, gates_ready = sem("xc_ready"), sem("gates_ready")
        lru_m, lru_rt, ix_ready = sem("lru_m"), sem("lru_rt"), sem("ix_ready")
        y_new, y_scaled = sem("y_new"), sem("y_scaled")
        wzero = sem("wzero")

        p_at = [P * i * (i + 1) // 2 for i in range(TB)]
        turned = [(j, i) for j in range(TB) for i in range(j, TB)]
        pt_groups = [turned[n:n + 4] for n in range(0, len(turned), 4)]
        s_units = [(0, 1), (2,), (3,)]
        NU, NG = len(s_units), len(pt_groups)

        def rows(w):
            return w.rearrange("(k p) n -> p k n", p=P)

        e_in, o_in = rows(t["ev_w_in"][0]), rows(t["od_w_in"][0])
        src = {"cq01": e_in[:, :, 1536:1792], "cq2kv0": e_in[:, :, 1792:2048], "kv1kr": e_in[:, :, 2048:2208],
               "ukv": rows(t["mla_w_ukv"][0]), "glr": o_in[:, :, 1024:1152],
               "gq": o_in[:, :, 0:256], "gk": o_in[:, :, 256:512]}
        for g in range(2):
            c = 256 * g
            src[f"b{g}"], src[f"c{g}"], src[f"u{g}"] = (e_in[:, :, o + c:o + c + 256] for o in (0, 512, 1024))
            src[f"uq{g}"] = rows(t["mla_w_uq"][0])[:, :, 384 * g:384 * g + 384]
            src[f"gv{g}"], src[f"og{g}"] = (o_in[:, :, o + c:o + c + 256] for o in (512, 1040))
            src[f"x{g}"], src[f"y{g}"] = (o_in[:, :, o + c:o + c + 256] for o in (1552, 2064))
            for m, half in enumerate("ab"):
                src[f"ewo{g}{half}"] = rows(t["ev_w_out"][0])[:, 4 * g:4 * g + 4, 512 * m:512 * m + 512]
                src[f"owo{g}{half}"] = rows(t["od_w_out"][0])[:, 4 - 4 * g:8 - 4 * g, 512 * m:512 * m + 512]

        def tile_view(buf, slot, kc, n):
            return buf[:, slot, 0:kc * n].rearrange("p (k n) -> p k n", k=kc)

        def static_tiles(lo, hi):
            return [n for n in range(lo, hi) if TILES[n][1]]

        LOOPS = (BLOCKS - 2) // 2

        pieces = [("mix0", t["mixer_norm_g"][0]), ("mlp0", t["mlp_norm_g"][0]),
                  ("mix1", t["mixer_norm_g"][1]), ("mlp1", t["mlp_norm_g"][1]),
                  ("final", t["final_norm_g"]), ("qg", t["mla_q_norm_g"][0]),
                  ("kvg", t["mla_kv_norm_g"][0]), ("evconv", t["ev_conv_w"][0].rearrange("k n -> (k n)")),
                  ("gbias", t["gla_b_gate"][0]), ("glag", t["gla_norm_g"][0]),
                  ("lconvw", t["lru_conv_w"][0].rearrange("k n -> (k n)")), ("lconvb", t["lru_conv_b"][0]),
                  ("ba", t["lru_b_a"][0]), ("bi", t["lru_b_i"][0]), ("lam", t["lru_lambda"][0])]
        latent_at = [(1, 1), (1, 2), (1, 3), (1, 0), (0, 3)]
        latent_hi = [hidH[:, b, c, :] for b, c in latent_at]
        latent_lo = [hidL[:, b, c, :] for b, c in latent_at]

        def turned_move(eng, h, groups, signal):
            for g in groups:
                n = NG * h + g
                eng.wait_ge(pt_done, n + 1)
                w = P * len(pt_groups[g])
                dst, source = probsT[:, h % 2, 4 * P * g:4 * P * g + w], pt_banks[n % 2][:, 0:w]
                if signal is pt_out_act:
                    eng.activation(dst, source, ACT.Copy).then_inc(signal, 1)
                else:
                    eng.tensor_copy(dst, source).then_inc(signal, 1)

        def moved(eng, k, static=None):
            by_act, count = MOVED[k if static is None else static]
            if static is not None:
                count = k + (count - static)
            eng.wait_ge(gemm_out_act if by_act else gemm_out, count)

        def split_pieces(key, dst, rawv):
            if key.startswith("uq"):
                d = dst.rearrange("p (k h n) -> p k h n", k=3, h=4)
                r = rawv.rearrange("p (k h n) -> p k h n", k=3, h=4)
                return ([(d[:, :, :, 0:QK], r)], [(d[:, k, :, a:a + 16], r[:, k, :, b:b + 16])
                                                  for k in range(3) for a, b in ((96, 80), (112, 64))])
            if key == "kv1kr":
                d = dst.rearrange("p (k n) -> p k n", k=KD)
                r = rawv.rearrange("p (k n) -> p k n", k=KD)
                return ([(d[:, :, 0:160], r)], [(d[:, :, 160:176], r[:, :, 144:160]), (d[:, :, 176:192], r[:, :, 128:144])])
            return ([(dst, rawv)], [])

        def split_width(n):
            key, kc, cols = TILES[n]
            return 3 * 4 * P if key.startswith("uq") else KD * 192 if key == "kv1kr" else kc * cols or 2048

        block = ctx.enter_context(nc.Block())

        @block.sync
        def _(sp):
            def load(n, view, kc, cols, count=None):
                first = isinstance(n, int) and n < RAW
                slot = n % RAW if isinstance(n, int) else count
                if not first:
                    sp.wait_ge(wl_ready, n - RAW + 1)
                sp.dma_start(tile_view(raw, slot, kc, cols), view).then_inc(raw_loaded[slot], 16)

            def plain(lo, hi):
                for n in range(lo, hi):
                    key, kc, cols = TILES[n]
                    load(n, src[key], kc, cols)

            def mlp(layer):
                w1 = rows(t["mlp_w1"][layer])
                w2 = t["mlp_w2"][layer].rearrange("(b k p) n -> b p k n", k=4, p=P)
                n0 = TILE[f"mlp{layer}"]

                def up(n, j, slot):
                    for half in range(2):
                        load(n + half, w1[:, :, bass.ds(512 * j + 256 * half, 256)], KD, 256, (slot + half) % RAW)

                def down(n, j, slot):
                    for half in range(2):
                        view = w2[bass.ds(j, 1), :, :, 512 * half:512 * half + 512].rearrange("b p k n -> p (b k) n")
                        load(n + half, view, 4, 512, (slot + half) % RAW)

                up(n0, 0, n0)
                with sp.Fori(1, LOOPS + 1) as i:
                    for pair in range(2):
                        n, j = n0 + 2 - 8 + 4 * pair, 2 * i - 2 + pair
                        up(n + 8 * i, j + 1, n)
                        down(n + 2 + 8 * i, j, n + 2)
                n = n0 + 2 + 8 * LOOPS
                up(n, BLOCKS - 1, n)
                down(n + 2, BLOCKS - 2, n + 2)
                down(n + 4, BLOCKS - 1, n + 4)

            for b in range(TB):
                sp.dma_start(x_tok[:, b, :], t["x"][0, b * P:(b + 1) * P, :]).then_inc(ld_x[b], 16)
            plain(0, 1)
            plain(1, RAW)
            sp.dma_start(gup[:, :], t["gla_w_gate_up"][0]).then_inc(ld_gup, 16)
            plain(RAW, TILE["mlp0"])
            mlp(0)
            plain(TILE["glr"], TILE["x0"])
            sp.wait_ge(wzero, 1)
            for gate, w in enumerate((t["lru_w_a"][0], t["lru_w_i"][0])):
                pairs = w.rearrange("(c b) i j -> b i c j", b=2)
                for b in range(2):
                    sp.dma_start(wgate[64 * b:64 * b + 64, gate, :, 64 * b:64 * b + 64], pairs[b]).then_inc(ld_wgate, 16)
            plain(TILE["x0"], TILE["mlp1"])
            mlp(1)
            for b in range(TB):
                sp.wait_ge(y_scaled, b + 1)
                sp.dma_start(out[0, b * P:(b + 1) * P, :], y_tok[:, b, :]).then_inc(ld_out, 16)
            sp.wait_ge(ld_out, 16 * TB)

        @block.gpsimd
        def _(pool):
            n_link = 0

            def link(ins):
                nonlocal n_link
                n_link += 1
                ins.then_inc(pool_link, 1)
                pool.wait_ge(pool_link, n_link)

            link(pool.memset(ident[:, :], 0.0))
            pool.affine_select(out=ident[:, :], in_=ident[:, :], compare_op=ALU.not_equal, fill=1.0, base=0,
                               pattern=[[-1, P]], channel_multiplier=1).then_inc(ident_ready, 1)
            pool.wait_ge(ident_ready, 1)
            link(pool.memset(ones[:, :], 1.0))
            link(pool.memset(causal[:, :], 0.0))
            link(pool.affine_select(out=causal[:, :], in_=causal[:, :], compare_op=ALU.is_ge, fill=MASKED, base=0,
                                    pattern=[[-1, P]], channel_multiplier=1))
            link(pool.memset(gmask[:, :], 1.0))
            link(pool.affine_select(out=gmask[:, :], in_=gmask[:, :], compare_op=ALU.is_ge, fill=0.0, base=0,
                                    pattern=[[1, P]], channel_multiplier=-1))
            link(pool.memset(gmask[0:GCH, GCH:P], 0.0))
            link(pool.memset(resets[:, :], 1.0))
            link(pool.memset(resets[:, 0:S:GCH], 0.0))
            pool.tensor_copy(identb[:, :], ident[:, :]).then_inc(consts_ready, 1)
            pool.wait_ge(consts_ready, 1)

            def add_squares(name, chunks):
                a = acc[:, STAT[name] % 2, :]
                for c in range(1, chunks):
                    n = ADDS[name] + c - 1
                    pool.wait_ge(sq_ready, SQ[name] + c + 1)
                    if n:
                        pool.wait_ge(acc_ready, n)
                    pool.tensor_tensor(a, a, sqb[:, n % 2, :], ALU.add).then_inc(acc_ready, 1)

            add_squares("mix0", KD)
            add_squares("q", 3)
            add_squares("kv", 2)

            pool.wait_ge(acc_ready, ADDS["mlp0"])
            for c in range(CH):
                if c:
                    pool.wait_ge(cu_ready, c)
                moved(pool, G["u", c])
                pool.tensor_tensor(cu[:, c, 2:2 + S], cu[:, c, 2:2 + S], c_s[:, c % 2, :], ALU.mult).then_inc(cu_ready, 1)

            pool.wait_ge(cu_ready, CH)
            for h in range(HEADS):
                if h:
                    pool.wait_ge(q_roped, h)
                pool.wait_ge(q_parts, h + 1)
                moved(pool, G["q", h])
                pool.tensor_tensor(qT[64:96, h, :], qT[64:96, h, :], rope_tmp[64:96, h % 2, :], ALU.add).then_inc(q_roped, 1)

            pool.wait_ge(q_roped, HEADS)
            add_squares("mlp0", KD)
            add_squares("mix1", KD)

            pool.wait_ge(acc_ready, ADDS["mlp1"])
            pool.wait_ge(gemm_done, G["glr", 0] + 1)
            pool.memset(wgate[:, :, :, :], 0.0).then_inc(wzero, 1)
            pool.wait_ge(wzero, 1)

            for c in range(CH):
                if c:
                    pool.wait_ge(ix_ready, c)
                moved(pool, G["ri", c])
                pool.wait_ge(xc_ready, c + 1)
                pool.tensor_tensor(li[:, c % 2, :], li[:, c % 2, :], xc[:, c, :], ALU.mult).then_inc(ix_ready, 1)
            pool.wait_ge(ix_ready, CH)
            add_squares("mlp1", KD)
            add_squares("final", KD)

        @block.scalar
        def _(act):
            def split(n, slot=None, size=2048):
                width, key = size, ""
                if isinstance(n, int):
                    key, slot, size, width = TILES[n][0], n, TILES[n][1] * TILES[n][2] or 2048, split_width(n)
                    act.wait_ge(raw_loaded[slot % RAW], 16 * (n // RAW + 1))
                main, extra = split_pieces(key, wH[:, slot % 2, 0:width], raw[:, slot % RAW, 0:size])
                for dst, source in main + extra:
                    ins = act.activation(dst, source, ACT.Copy)
                ins.then_inc(wh_ready, 1)

            def used(n):
                act.wait_ge(gemm_done, TILE_LAST[TILES[n][0]])

            def split_after(key):
                n = TILE[key]
                used(n)
                split(n + 2)

            n_link = 0

            def link(ins):
                nonlocal n_link
                n_link += 1
                ins.then_inc(act_link, 1)
                act.wait_ge(act_link, n_link)

            def square(source, name, c):
                n = ADDS[name] + c - 1
                if c and n >= 2:
                    act.wait_ge(acc_ready, n - 1)
                dst = sqb[:, n % 2, :] if c else acc[:, STAT[name] % 2, :]
                act.activation(dst, source, ACT.Square).then_inc(sq_ready, 1)

            def finalize(norm, c, k):
                moved(act, k)
                act.activation(hgH[:, c, :], hT[:, c, :], ACT.Copy, scale=col(norm, c)).then_inc(hi_new, 1)
                square(hT[:, c, :], norm, c)

            def root(name):
                act.wait_ge(var_ready, STAT[name] + 1)
                act.activation(vcol, vcol, ACT.Sqrt).then_inc(rt_ready, 1)

            def spread_out(name):
                act.wait_ge(spread_done, SPREAD[name] + 1)
                act.activation(rstd[:, :], bank[5 + SPREAD[name] % 2][:, :], ACT.Copy).then_inc(rstd_ready, 1)

            def hid_split(n, source, dst):
                act.wait_ge(mix_in, n + 1)
                act.activation(dst, source, ACT.Copy).then_inc(hid_hi, 1)

            def mlp(layer):
                n0, g0 = TILE[f"mlp{layer}"], G[f"mlp{layer}", 0]
                s0 = 32 * layer

                def after(n, k, slot, first=None):
                    act.wait_ge(gemm_done, k + 1)
                    if first is None:
                        split(n + 2)
                    else:
                        act.wait_ge(raw_loaded[(slot + 2) % RAW], first)
                        split(n + 2, slot + 2)

                def up(k, static, buf, chunks, sq):
                    for m in chunks:
                        moved(act, k + m, static + m)
                        act.activation(tmpS[:, :], tmpR[:, :], ACT.Square).then_inc(sq_self, 1)
                        act.wait_ge(sq_self, sq + m + 1)
                        act.activation(hidH[:, buf, m, :], tmpS[:, :], ACT.Copy).then_inc(hid_hi, 1)

                for half in range(2):
                    up(g0, g0, 0, (2 * half, 2 * half + 1), s0)
                    after(n0 + half, g0 + 2 * half + 1, n0 + half)
                with act.Fori(1, LOOPS + 1) as i:
                    for pair in range(2):
                        n, g = n0 - 6 + 4 * pair, g0 + 4 - 24 + 12 * pair
                        for half in range(2):
                            up(g + 24 * i, g + 24, (pair + 1) % 2, (2 * half, 2 * half + 1), s0 + 4 - 8 + 4 * pair + 8 * i)
                            m = n + half
                            after(m + 8 * i, g + 2 * half + 1 + 24 * i, m, 32 * i + 16 * ((m + 2) // RAW + 1))
                        for half in range(2):
                            m = n + 2 + half
                            after(m + 8 * i, g + 4 + 4 * half + 3 + 24 * i, m, 32 * i + 16 * ((m + 2) // RAW + 1))
                n, g = n0 + 2 + 8 * LOOPS, g0 + 4 + 24 * LOOPS
                for half in range(2):
                    up(g, g, (BLOCKS - 1) % 2, (2 * half, 2 * half + 1), s0 + 4 + 8 * LOOPS)
                    after(n + half, g + 2 * half + 1, n + half)
                for half in range(2):
                    m = n + 2 + half
                    if m + 2 < len(TILES):
                        after(m, g + 4 + 4 * half + 3, m)
                for c in range(KD):
                    if layer == 0:
                        finalize("mix1", c, g + 12 + c)
                    else:
                        moved(act, G["last", c])
                        act.activation(yT[:, c, :], hT[:, c, :], ACT.Copy, scale=col("final", c)).then_inc(y_new, 1)
                        square(hT[:, c, :], "final", c)
                    if c % 4 == 3 and n + 4 + c // 4 + 2 < len(TILES):
                        m = n + 4 + c // 4
                        after(m, g + 12 + c, m)

            for name, vec in pieces:
                v = vec.rearrange("(c p) -> c p", p=P)
                at = PCOL[name]
                act.dma_start(prm[at:at + v.shape[0], :], v).then_inc(ld_prm, 16)
            act.dma_start(rope_par[64:128, :], t["rope_par"]).then_inc(ld_freq, 16)
            act.dma_start(pos_i[64:128, :], t["positions"].broadcast_to((2 * ROPE, S))).then_inc(ld_pos, 16)
            act.wait_ge(params_ready, 1)
            for c in range(KD):
                finalize("mix0", c, G["x", c])
                if c == 2:
                    split(0)
                if c == 5:
                    split(1)
            root("mix0")
            spread_out("mix0")
            act.wait_ge(rope_arg, 1)
            act.activation(rope_cs[64:128, :], ang_k[64:128, :], ACT.Sin, scale=rope_par[64:128, 3:4]).then_inc(rope_ready, 1)

            def latent_square(c):
                moved(act, G["cq", c])
                square(c_raw[:, c, :], *(("q", c) if c < 3 else ("kv", c - 3)))

            latent_square(0)
            latent_square(1)
            split_after("cq01")
            latent_square(2)
            latent_square(3)
            split_after("cq2kv0")
            latent_square(4)
            split_after("kv1kr")
            root("q")
            root("kv")
            split_after("c0")
            for c in range(5):
                act.wait_ge(cn_scaled, c + 1)
                act.activation(latent_hi[c], c_raw[:, c, :], ACT.Copy).then_inc(cn_hi, 1)
            for key in ("u0", "b0", "c1", "u1", "b1"):
                split_after(key)

            def move(key, dst, source, **how):
                act.wait_ge(gemm_done, G[key] + 1)
                act.activation(dst, source, ACT.Copy, **how).then_inc(gemm_out_act, 1)

            for tb in range(TB):
                move(("v", tb), v_tok[:, tb, :], bank[G["v", tb] % RING][:, :])
            act.wait_ge(kr_ready, 1)
            act.activation(kT[64:96, :, :], kr_s[64:96, :].unsqueeze(1).to_broadcast((ROPE, HEADS, S)), ACT.Copy).then_inc(kr_copied, 1)
            for h in range(HEADS):
                move(("k", h), kT[0:NOPE, h, :], bank[G["k", h] % RING][0:NOPE, :])
                if h < 3:
                    hid_split(MIX_IN["sconv"] + h, b_s[:, h, :], hidH[:, 0, h, :])
            split_after("ukv")

            def q_out(h):
                act.wait_ge(gemm_done, G["q", h] + 1)
                act.activation(qT[0:NOPE, h, :], bank[G["q", h] % RING][0:NOPE, :], ACT.Copy).then_inc(q_nope, 1)

            for h in range(Q_AHEAD):
                q_out(h)
            hid_split(MIX_IN["sconv"] + 3, b_s[:, 3, :], hidH[:, 0, 3, :])

            def exps(h, units):
                for u in units:
                    blocks = s_units[u]
                    n = NU * h + u
                    act.wait_ge(nmax_ready, n + 1)
                    if u == 0 and h >= 2:
                        act.wait_ge(pt_done, NG * (h - 1))
                    for i in blocks:
                        at = 0 if i != 1 else P
                        w = P * (i + 1)
                        e = 4 * (h % 2) + i
                        ins = act.activation(probs[:, h % 2, p_at[i]:p_at[i] + w], s_banks[n % 2][:, at:at + w], ACT.Exp,
                                             bias=nmx[:, e:e + 1], scale=SCALE, accum_out=sums[:, e:e + 1])
                    ins.then_inc(p_ready, 1)

            for step in range(STEPS):
                h = step
                if h < HEADS:
                    exps(h, (0, 1))
                if 1 <= h <= HEADS:
                    turned_move(act, h - 1, (0, 2), pt_out_act)
                if step + Q_AHEAD < HEADS:
                    q_out(step + Q_AHEAD)
                    if step + Q_AHEAD == 3:
                        split_after("uq0")
                    if step + Q_AHEAD == 7:
                        split_after("uq1")
                if step >= 3 and step % 2 == 1:
                    pr = (step - 3) // 2
                    act.wait_ge(gemm_done, G["ot", pr] + 1)
                    act.activation(hidH[:, 1, pr, :], bank[G["ot", pr] % RING][:, :], ACT.Copy).then_inc(hid_hi, 1)
                if h < HEADS:
                    exps(h, (2,))
                if step == 5:
                    split_after("ewo0a")
            split_after("ewo0b")
            for c in range(KD):
                finalize("mlp0", c, G["ewo1", c])
                if c == 3:
                    split_after("ewo1a")
            split_after("ewo1b")
            root("mlp0")
            spread_out("mlp0")
            mlp(0)

            root("mix1")
            split_after("glr")
            spread_out("mix1")
            link(act.activation(lam_e, col("lam", 0, CH), ACT.Abs))
            act.activation(lam_e, lam_e, ACT.Exp, scale=-1.0).then_inc(lam_exp, 1)
            split_after("gq")
            for p in range(2):
                act.wait_ge(gemm_done, G["z", p] + 1)
                act.activation(cum[:, p, :], bank[G["z", p] % RING][:, :], ACT.Identity, bias=col("gbias", p)).then_inc(gemm_out_act, 1)
            moved(act, G["z", 1])
            link(act.activation(ge[:, :, :], cum[:, :, :], ACT.Abs))
            link(act.activation(ge[:, :, :], ge[:, :, :], ACT.Exp, scale=-1.0))
            act.activation(ge[:, :, :], ge[:, :, :], ACT.Ln, bias=ones[:, 0:1]).then_inc(ls_ready, 1)
            split_after("gk")
            act.wait_ge(cum_ready, 1)
            act.activation(ge[:, :, :], cum[:, :, :], ACT.Exp, scale=1 / GTAU).then_inc(e_ready, 1)
            act.wait_ge(e_used, 1)
            act.activation(ge[:, :, :], cum[:, :, :], ACT.Exp, scale=-1 / GTAU).then_inc(e_ready, 1)
            ends = cum[:, :, :].rearrange("p a (n t) -> p a n t", t=GCH)[:, :, :, GCH - 1]
            act.activation(decay, ends, ACT.Exp, scale=1 / GTAU).then_inc(e_ready, 1)
            act.wait_ge(cum_ready, 2)
            act.activation(ge[:, :, :], ge[:, :, :], ACT.Exp, scale=1 / GTAU).then_inc(e_ready, 1)
            split_after("x0")

            def gelu(c):
                moved(act, G["y", c])
                act.activation(gel[:, c, :], gel[:, c, :], ACT.Gelu_apprx_tanh).then_inc(gel_ready, 1)

            def sigmoids(c):
                if c == 0:
                    act.wait_ge(lam_ready, 1)
                if c >= 2:
                    act.wait_ge(mix_in, MIX_IN["lru"] + c - 1)
                for name, dst, bias in (("ra", lr, "ba"), ("ri", li, "bi")):
                    act.wait_ge(gemm_done, G[name, c] + 1)
                    act.activation(dst[:, c % 2, :], bank[G[name, c] % RING][:, :], ACT.Sigmoid,
                                   bias=col(bias, c)).then_inc(gemm_out_act, 1)

            def gates(c):
                if c:
                    act.wait_ge(mix_in, MIX_IN["lru"] + c)
                act.activation(tmpR[:, :], lr[:, c % 2, :], ACT.Tanh, scale=lam_k[:, c:c + 1])
                link(act.activation(lr[:, c % 2, :], lr[:, c % 2, :], ACT.Exp, scale=lam_nk[:, c:c + 1]))
                act.activation(tmpS[:, :], lr[:, c % 2, :], ACT.Square).then_inc(gates_ready, 1)
                act.wait_ge(lru_m, c + 1)
                act.activation(tmpR[:, :], tmpR[:, :], ACT.Sqrt).then_inc(lru_rt, 1)

            def lru_hi(c):
                hid_split(MIX_IN["lru"] + c, gel[:, c, :], hidH[:, 0, c, :])

            def v_out(half, blocks):
                for tb in blocks:
                    move((f"gv{half}", tb), gv[:, tb, 256 * half:256 * half + 256],
                         bank[G[f"gv{half}", tb] % RING][:, 0:256], scale=rcol_mix1[:, tb:tb + 1])

            gelu(0)
            gelu(1)
            split_after("y0")
            sigmoids(0)
            sigmoids(1)
            gates(0)
            split_after("x1")
            gates(1)
            lru_hi(0)
            gelu(2)
            gelu(3)
            split_after("y1")
            sigmoids(2)
            lru_hi(1)
            sigmoids(3)
            v_out(0, range(2))
            gates(2)
            v_out(0, range(2, TB))
            split_after("gv0")
            gates(3)
            v_out(1, range(TB))
            split_after("gv1")
            lru_hi(2)
            lru_hi(3)
            for h in range(GH):
                moved(act, G["og", h])
                act.activation(og[:, h, :], og[:, h, :], ACT.Silu).then_inc(og_ready, 1)
                if h == 1:
                    split_after("og0")
            split_after("og1")
            for p in range(2):
                move(("kt", p), gkT[:, :, p * P:(p + 1) * P], bank[G["kt", p] % RING][:, :].rearrange("p (b d) -> p b d", b=TB))
            for h in range(GH):
                act.wait_ge(gemm_done, G["o", h] + 1)
                source = bank[G["o", h] % RING][:, :]
                if h >= 2:
                    act.wait_ge(stat_done, STAT["gla0"] + h - 1)
                square(source, f"gla{h}", 0)
                act.activation(o_sb[:, h, :], source, ACT.Copy).then_inc(gemm_out_act, 1)
                if h == 1:
                    root("gla0")
                    root("gla1")
            root("gla2")
            root("gla3")
            split_after("owo0a")
            for h in range(GH):
                hid_split(MIX_IN["gla"] + h, o_sb[:, h, :], hidH[:, 1, h, :])
            split_after("owo0b")
            for c in range(KD):
                finalize("mlp1", c, G["owo1", c])
                if c == 3:
                    split_after("owo1a")
            split_after("owo1b")
            root("mlp1")
            spread_out("mlp1")
            mlp(1)
            root("final")

        @block.vector
        def _(dve):
            n_link = 0

            def link(ins):
                nonlocal n_link
                n_link += 1
                ins.then_inc(dve_link, 1)
                dve.wait_ge(dve_link, n_link)

            def f32(ap):
                return ap.bitcast(F32)

            def split(n, slot=None, size=2048):
                width, key = size, ""
                if isinstance(n, int):
                    key, slot, size, width = TILES[n][0], n, TILES[n][1] * TILES[n][2] or 2048, split_width(n)
                dve.wait_ge(wh_ready, n + 1)
                main, extra = split_pieces(key, wL[:, slot % 2, 0:width], raw[:, slot % RAW, 0:size])
                hi_main, hi_extra = split_pieces(key, f32(wH[:, slot % 2, 0:width]), raw[:, slot % RAW, 0:size])
                for (dst, source), (hi, _) in zip(main + extra, hi_main + hi_extra):
                    ins = dve.tensor_tensor(dst, source, hi, ALU.subtract)
                ins.then_inc(wl_ready, 1)

            def split_after(key):
                split(TILE[key] + 2)

            def out_of(k, rows=P, lo=0, cols=S):
                dve.wait_ge(gemm_done, k + 1)
                return bank[k % RING][lo:rows, 0:cols]

            def lo_part(norm, c):
                dve.wait_ge(hi_new, KD * INST[norm] + c + 1)
                dve.scalar_tensor_tensor(out=hgL[:, c, :], in0=hT[:, c, :], scalar=col(norm, c), in1=f32(hgH[:, c, :]),
                                         op0=ALU.mult, op1=ALU.subtract).then_inc(hg_ready, 1)

            def variance(name, count):
                dve.wait_ge(stat_done, STAT[name] + 1)
                dve.tensor_scalar(vcol, stat_bank[:, 0:TB], 1.0 / count, EPS, ALU.mult, ALU.add).then_inc(var_ready, 1)

            def inverse(name):
                dst = rcol_mix1 if name == "mix1" else rcol
                dve.wait_ge(rt_ready, STAT[name] + 1)
                if name in SPREAD and SPREAD[name]:
                    dve.wait_ge(diag_ready, SPREAD[name])
                link(dve.reciprocal(dst, vcol))
                if name != "final":
                    if SPREAD[name]:
                        dve.wait_ge(spread_done, SPREAD[name])
                    dve.tensor_tensor(diag[:, :, :], ident[:, :].unsqueeze(1).to_broadcast((P, TB, P)),
                                      dst.unsqueeze(2).to_broadcast((P, TB, P)), ALU.mult).then_inc(diag_ready, 1)

            def spread_of(name):
                dve.wait_ge(spread_done, SPREAD[name] + 1)
                return bank[5 + SPREAD[name] % 2][:, :]

            def add_to_h(k, c):
                dve.tensor_tensor(hT[:, c, :], out_of(k), hT[:, c, :], ALU.add).then_inc(gemm_out, 1)

            def hid_low(hid, source, dst_hi, dst):
                dve.wait_ge(hid_hi, hid + 1)
                dve.tensor_tensor(dst, source, f32(dst_hi), ALU.subtract).then_inc(hid_ready, 1)

            def mlp(layer):
                n0, g0, h0 = TILE[f"mlp{layer}"], G[f"mlp{layer}", 0], HID[f"mlp{layer}"]

                def result(k, ring):
                    dve.wait_ge(gemm_done, k + 1)
                    return bank[ring % RING][:, :]

                def up(k, ring, hid, buf, chunks):
                    for m in chunks:
                        dve.scalar_tensor_tensor(out=tmpR[:, :], in0=result(k + m, ring + m), scalar=0.0, in1=rstd[:, :],
                                                 op0=ALU.max, op1=ALU.mult).then_inc(gemm_out, 1)
                        hid_low(hid + m, tmpS[:, :], hidH[:, buf, m, :], hidL[:, buf, m, :])

                def down(k, ring, chunks):
                    for c in chunks:
                        dve.tensor_tensor(hT[:, c, :], result(k + c, ring + c), hT[:, c, :], ALU.add).then_inc(gemm_out, 1)

                def lo(n, slot):
                    split(n + 2, slot + 2)

                for half in range(2):
                    up(g0, g0, h0, 0, (2 * half, 2 * half + 1))
                    lo(n0 + half, n0 + half)
                with dve.Fori(1, LOOPS + 1) as i:
                    for pair in range(2):
                        n, g, hid = n0 - 6 + 4 * pair, g0 + 4 - 24 + 12 * pair, h0 + 4 - 8 + 4 * pair
                        for half in range(2):
                            up(g + 24 * i, g, hid + 8 * i, (pair + 1) % 2, (2 * half, 2 * half + 1))
                            lo(n + half + 8 * i, n + half)
                        for half in range(2):
                            down(g + 4 + 24 * i, g + 4, range(4 * half, 4 * half + 4))
                            lo(n + 2 + half + 8 * i, n + 2 + half)
                n, g, hid = n0 + 2 + 8 * LOOPS, g0 + 4 + 24 * LOOPS, h0 + 4 + 8 * LOOPS
                for half in range(2):
                    up(g, g, hid, (BLOCKS - 1) % 2, (2 * half, 2 * half + 1))
                    split(n + half + 2)
                for half in range(2):
                    down(g + 4, g + 4, range(4 * half, 4 * half + 4))
                    if n + 4 + half < len(TILES):
                        split(n + 4 + half)
                for c in range(KD):
                    if layer == 0:
                        add_to_h(g + 12 + c, c)
                        lo_part("mix1", c)
                    else:
                        add_to_h(G["last", c], c)
                        if c:
                            y_out(c - 1)
                    if c % 4 == 3 and n + 6 + c // 4 < len(TILES):
                        split(n + 6 + c // 4)

            def y_out(c):
                k = G["yt", c]
                dve.tensor_copy(y_tok[:, :, c * P:(c + 1) * P], out_of(k).rearrange("p (b f) -> p b f", b=TB)).then_inc(gemm_out, 1)

            dve.wait_ge(params_done, 1)
            dve.tensor_copy(pcol[:, :], stat_bank[:, 0:NPARAM]).then_inc(params_ready, 1)
            dve.wait_ge(params_ready, 1)

            def x_out(c):
                dve.tensor_copy(hT[:, c, :], out_of(G["x", c])).then_inc(gemm_out, 1)
                moved(dve, G["x", c])

            x_out(0)
            for c in range(KD):
                if c + 1 < KD:
                    x_out(c + 1)
                lo_part("mix0", c)
                if c == 2:
                    split(0)
                if c == 5:
                    split(1)

            rows = slice(64, P)
            dve.wait_ge(ld_pos, 16)
            dve.wait_ge(ld_freq, 16)
            a, k, whole = ang[rows, :], ang_k[rows, :], turns[rows, :]
            link(dve.tensor_copy(a, pos_i[rows, :]))
            link(dve.tensor_scalar(a, a, rope_par[rows, 0:1], None, ALU.mult))
            two_pi = 2 * np.pi
            C1 = 6.28125
            C2 = float(np.round((two_pi - C1) * 2 ** 20) / 2 ** 20)
            C3 = float(two_pi - C1 - C2)
            BIG = 1.5 * 2 ** 23
            link(dve.tensor_scalar(k, a, 1 / two_pi, rope_par[rows, 1:2], ALU.mult, ALU.add))
            variance("mix0", D)
            link(dve.tensor_scalar(k, k, BIG, None, ALU.add))
            inverse("mix0")
            link(dve.tensor_scalar(whole, k, BIG, None, ALU.subtract))
            link(dve.scalar_tensor_tensor(out=k, in0=whole, scalar=-C1, in1=a, op0=ALU.mult, op1=ALU.add))
            link(dve.scalar_tensor_tensor(out=k, in0=whole, scalar=-C2, in1=k, op0=ALU.mult, op1=ALU.add))
            link(dve.scalar_tensor_tensor(out=k, in0=whole, scalar=-C3, in1=k, op0=ALU.mult, op1=ALU.add))
            link(dve.tensor_scalar(k, k, rope_par[rows, 2:3], 3.1415925, ALU.add, ALU.min))
            dve.tensor_scalar(k, k, -3.1415925, None, ALU.max).then_inc(rope_arg, 1)

            def scaled_out(name, c, dst):
                dve.tensor_tensor(dst, out_of(G[name, c]), rstd[:, :], ALU.mult).then_inc(gemm_out, 1)

            dve.wait_ge(rstd_ready, 1)
            scaled_out("cq", 0, c_raw[:, 0, :])
            scaled_out("cq", 1, c_raw[:, 1, :])
            split_after("cq01")
            scaled_out("cq", 2, c_raw[:, 2, :])
            scaled_out("cq", 3, c_raw[:, 3, :])
            split_after("cq2kv0")
            scaled_out("cq", 4, c_raw[:, 4, :])
            cos, sin = slice(64, 96), slice(96, P)
            dve.tensor_tensor(tmpR[64:P, :], out_of(G["kr", 0], P, 64), rstd[64:P, :], ALU.mult).then_inc(gemm_out, 1)
            moved(dve, G["kr", 0])
            variance("q", QR)
            dve.wait_ge(rope_ready, 1)
            link(dve.tensor_tensor(kr_s[cos, :], tmpR[cos, :], rope_cs[cos, :], ALU.mult))
            link(dve.tensor_tensor(rope_tmp[cos, 0, :], tmpR[sin, :], rope_cs[sin, :], ALU.mult))
            dve.tensor_tensor(kr_s[cos, :], kr_s[cos, :], rope_tmp[cos, 0, :], ALU.add).then_inc(kr_ready, 1)
            dve.wait_ge(kr_ready, 1)
            split_after("kv1kr")
            inverse("q")

            def scale_latent(name, c, gain):
                dve.scalar_tensor_tensor(out=c_raw[:, c, :], in0=c_raw[:, c, :], scalar=gain, in1=spread_of(name),
                                         op0=ALU.mult, op1=ALU.mult).then_inc(cn_scaled, 1)

            def c_out(c):
                scaled_out("c", c, c_s[:, c % 2, :])

            def u_out(c):
                scaled_out("u", c, cu[:, c, 2:2 + S])

            def b_out(c):
                scaled_out("b", c, b_s[:, c, :])

            def short_conv(c):
                dve.wait_ge(cu_ready, c + 1)
                if c:
                    dve.wait_ge(mix_in, MIX_IN["sconv"] + c)
                w = [col("evconv", CH * k + c) for k in range(SC_K)]
                link(dve.tensor_scalar(tmpR[:, :], cu[:, c, 0:S], w[0], None, ALU.mult))
                for k in range(1, SC_K):
                    link(dve.scalar_tensor_tensor(out=tmpR[:, :], in0=cu[:, c, k:k + S], scalar=w[k], in1=tmpR[:, :],
                                                  op0=ALU.mult, op1=ALU.add))
                dve.tensor_tensor(b_s[:, c, :], b_s[:, c, :], tmpR[:, :], ALU.mult).then_inc(mix_in, 1)

            link(dve.memset(cu[:, :, 0:SC_K - 1], 0.0))
            c_out(0)
            variance("kv", KVR)
            for c in range(3):
                scale_latent("q", c, col("qg", c))
            inverse("kv")
            c_out(1)
            split_after("c0")
            for c in range(2):
                scale_latent("kv", 3 + c, col("kvg", c))
            for c in range(5):
                dve.wait_ge(cn_hi, c + 1)
                dve.tensor_tensor(latent_lo[c], c_raw[:, c, :], f32(latent_hi[c]), ALU.subtract).then_inc(cn_ready, 1)
            u_out(0)
            u_out(1)
            split_after("u0")
            b_out(0)
            b_out(1)
            split_after("b0")
            short_conv(0)
            c_out(2)
            short_conv(1)
            c_out(3)
            split_after("c1")
            u_out(2)
            u_out(3)
            split_after("u1")
            b_out(2)
            b_out(3)
            split_after("b1")
            short_conv(2)
            short_conv(3)
            for c in range(3):
                hid_low(HID["sconv"] + c, b_s[:, c, :], hidH[:, 0, c, :], hidL[:, 0, c, :])
            split_after("ukv")

            def q_rotary(h):
                if h >= 2:
                    dve.wait_ge(q_roped, h - 1)
                k = G["q", h]
                dve.tensor_tensor(rope_tmp[cos, h % 2, :], out_of(k, P, 96), rope_cs[sin, :], ALU.mult).then_inc(q_parts, 1)
                dve.wait_ge(q_nope, h + 1)
                dve.tensor_tensor(qT[cos, h, :], out_of(k, 96, 64), rope_cs[cos, :], ALU.mult).then_inc(gemm_out, 1)

            for h in range(Q_AHEAD):
                q_rotary(h)
            hid_low(HID["sconv"] + 3, b_s[:, 3, :], hidH[:, 0, 3, :], hidL[:, 0, 3, :])

            def maxima(h, u):
                n = NU * h + u
                dve.wait_ge(s_done, n + 1)
                for i in s_units[u]:
                    at = 0 if i != 1 else P
                    e = 4 * (h % 2) + i
                    link(dve.tensor_reduce(mx[:, e:e + 1], s_banks[n % 2][:, at:at + P * (i + 1)], AX_X, ALU.max))
                lo, hi = 4 * (h % 2) + s_units[u][0], 4 * (h % 2) + s_units[u][-1] + 1
                dve.tensor_scalar(nmx[:, lo:hi], mx[:, lo:hi], -SCALE, None, ALU.mult).then_inc(nmax_ready, 1)

            def head_out(h):
                dve.wait_ge(o_done, h + 1)
                dve.wait_ge(p_ready, NU * (h + 1))
                link(dve.reciprocal(rinv, sums[:, 4 * (h % 2):4 * (h % 2) + 4]))
                dst = o_tok[:, h // 2 % 2, :, VD * (h % 2):VD * (h % 2) + VD]
                dve.tensor_tensor(dst, o_bank[:, 0:TB * VD].rearrange("p (b v) -> p b v", b=TB),
                                  rinv.unsqueeze(2).to_broadcast((P, TB, VD)), ALU.mult).then_inc(o_out, 1)

            for step in range(STEPS):
                if step < HEADS:
                    maxima(step, 0)
                    maxima(step, 1)
                if 1 <= step <= HEADS:
                    turned_move(dve, step - 1, (1,), pt_out)
                h = step + Q_AHEAD
                if h < HEADS:
                    q_rotary(h)
                    if h == 3:
                        split_after("uq0")
                    if h == 7:
                        split_after("uq1")
                if step >= 3 and step % 2 == 1:
                    pr = (step - 3) // 2
                    ot = out_of(G["ot", pr])
                    dve.wait_ge(hid_hi, HID["attn"] + pr + 1)
                    dve.tensor_tensor(hidL[:, 1, pr, :], ot, f32(hidH[:, 1, pr, :]), ALU.subtract).then_inc(gemm_out, 1)
                if step < HEADS:
                    maxima(step, 2)
                if step >= 2:
                    add_to_h(G["ewo0", step - 2], step - 2)
                if step == 5:
                    split_after("ewo0a")
                if 1 <= step <= HEADS:
                    head_out(step - 1)
            split_after("ewo0b")
            for c in range(KD):
                add_to_h(G["ewo1", c], c)
                lo_part("mlp0", c)
                if c == 3:
                    split_after("ewo1a")
            split_after("ewo1b")
            variance("mlp0", D)
            inverse("mlp0")
            dve.wait_ge(rstd_ready, 2)
            mlp(0)

            variance("mix1", D)
            inverse("mix1")
            split_after("glr")
            dve.wait_ge(rstd_ready, 3)
            dve.tensor_tensor(glr[:, :], out_of(G["glr", 0], GRANK), rstd[0:GRANK, :], ALU.mult).then_inc(gemm_out, 1)
            scaled_out("gq", 0, gq[:, 0, :])
            scaled_out("gq", 1, gq[:, 1, :])
            split_after("gq")

            dve.wait_ge(lam_exp, 1)
            link(dve.tensor_scalar(lam_d, lam_e, 2.0, None, ALU.add))
            link(dve.reciprocal(lam_d, lam_d))
            link(dve.tensor_tensor(lam_s, lam_e, lam_d, ALU.mult))
            link(dve.tensor_tensor(lam_s2, lam_s, lam_s, ALU.mult))
            link(dve.tensor_scalar(lam_p, lam_s2, 1 / 17, None, ALU.mult))
            for odd in (15, 13, 11, 9, 7, 5, 3):
                link(dve.scalar_tensor_tensor(out=lam_p, in0=lam_p, scalar=1 / odd, in1=lam_s2, op0=ALU.add, op1=ALU.mult))
            link(dve.scalar_tensor_tensor(out=lam_p, in0=lam_p, scalar=1.0, in1=lam_s, op0=ALU.add, op1=ALU.mult))
            link(dve.tensor_scalar(lam_d, col("lam", 0, CH), -1.0, 0.0, ALU.mult, ALU.max))
            link(dve.scalar_tensor_tensor(out=lam_p, in0=lam_p, scalar=2.0, in1=lam_d, op0=ALU.mult, op1=ALU.add))
            link(dve.tensor_scalar(lam_k, lam_p, LRU_C, None, ALU.mult))
            dve.tensor_scalar(lam_nk, lam_p, -LRU_C, None, ALU.mult).then_inc(lam_ready, 1)

            link(dve.memset(xl[:, 0:LRU_K - 1], 0.0))
            scaled_out("gk", 0, gk[:, 0, :])
            dve.wait_ge(ls_ready, 1)
            for p in range(2):
                link(dve.scalar_tensor_tensor(out=gki[:, p, :], in0=cum[:, p, :], scalar=0.0, in1=ge[:, p, :],
                                              op0=ALU.min, op1=ALU.subtract))
                ins = dve.tensor_tensor_scan(cum[:, p, :], resets[:, :], gki[:, p, :], 0.0, ALU.mult, ALU.add)
                if p == 0:
                    link(ins)
                else:
                    ins.then_inc(cum_ready, 1)
            scaled_out("gk", 1, gk[:, 1, :])
            split_after("gk")
            dve.wait_ge(e_ready, 1)
            dve.scalar_tensor_tensor(out=gq[:, :, :], in0=gq[:, :, :], scalar=GDK ** -0.5, in1=ge[:, :, :],
                                     op0=ALU.mult, op1=ALU.mult).then_inc(e_used, 1)
            dve.wait_ge(e_ready, 3)
            link(dve.tensor_tensor(gki[:, :, :], gk[:, :, :], ge[:, :, :], ALU.mult))
            for p in range(2):
                by_chunk = cum[:, p, :].rearrange("p (n t) -> p n t", t=GCH)
                ins = dve.tensor_tensor(ge[:, p, :].rearrange("p (n t) -> p n t", t=GCH),
                                        by_chunk[:, :, GCH - 1:GCH].to_broadcast((P, NCH, GCH)), by_chunk, ALU.subtract)
                if p == 0:
                    link(ins)
                else:
                    ins.then_inc(cum_ready, 1)

            def lru_conv(c):
                if c:
                    dve.wait_ge(xc_ready, c)
                scaled_out("xl", c, xl[:, LRU_K - 1:LRU_K - 1 + S])
                moved(dve, G["xl", c])
                w = [col("lconvw", CH * k + c) for k in range(LRU_K)]
                link(dve.tensor_scalar(xc[:, c, :], xl[:, 0:S], w[0], col("lconvb", c), ALU.mult, ALU.add))
                for k in range(1, LRU_K):
                    ins = dve.scalar_tensor_tensor(out=xc[:, c, :], in0=xl[:, k:k + S], scalar=w[k], in1=xc[:, c, :],
                                                   op0=ALU.mult, op1=ALU.add)
                    if k < LRU_K - 1:
                        link(ins)
                    else:
                        ins.then_inc(xc_ready, 1)

            def recurrence(c):
                dve.wait_ge(gates_ready, c + 1)
                dve.scalar_tensor_tensor(out=tmpR[:, :], in0=tmpS[:, :], scalar=1.0, in1=tmpR[:, :],
                                         op0=ALU.add, op1=ALU.mult).then_inc(lru_m, 1)
                dve.wait_ge(lru_rt, c + 1)
                dve.wait_ge(ix_ready, c + 1)
                link(dve.tensor_tensor(li[:, c % 2, :], li[:, c % 2, :], tmpR[:, :], ALU.mult))
                link(dve.tensor_tensor_scan(tmpS[:, :], lr[:, c % 2, :], li[:, c % 2, :], 0.0, ALU.mult, ALU.add))
                dve.wait_ge(gel_ready, c + 1)
                dve.tensor_tensor(gel[:, c, :], gel[:, c, :], tmpS[:, :], ALU.mult).then_inc(mix_in, 1)

            def lru_low(c):
                hid_low(HID["lru"] + c, gel[:, c, :], hidH[:, 0, c, :], hidL[:, 0, c, :])

            dve.wait_ge(e_ready, 4)
            dve.tensor_tensor(gk[:, :, :], gk[:, :, :], ge[:, :, :], ALU.mult).then_inc(gla_ready, 1)
            lru_conv(0)
            lru_conv(1)
            split_after("x0")
            dve.wait_ge(gla_ready, 1)
            scaled_out("y", 0, gel[:, 0, :])
            scaled_out("y", 1, gel[:, 1, :])
            split_after("y0")
            recurrence(0)
            lru_conv(2)
            lru_conv(3)
            split_after("x1")
            recurrence(1)
            lru_low(0)
            scaled_out("y", 2, gel[:, 2, :])
            scaled_out("y", 3, gel[:, 3, :])
            split_after("y1")
            lru_low(1)
            recurrence(2)
            split_after("gv0")
            recurrence(3)
            split_after("gv1")
            lru_low(2)
            lru_low(3)
            for h in range(GH):
                scaled_out("og", h, og[:, h, :])
                if h == 1:
                    split_after("og0")
            split_after("og1")

            def chunk_states(p):
                dve.wait_ge(kv_done, p + 1)
                for n in range(NCH - 1):
                    kv = bank[3 + 2 * p + n % 2][:, (n // 2) * P:(n // 2 + 1) * P]
                    if n == 0:
                        ins = dve.tensor_copy(states[:, p, 1, :], kv)
                    else:
                        ins = dve.scalar_tensor_tensor(out=states[:, p, n + 1, :], in0=states[:, p, n, :],
                                                       scalar=decay[:, p, n:n + 1], in1=kv, op0=ALU.mult, op1=ALU.add)
                    if n < NCH - 2:
                        link(ins)
                    else:
                        ins.then_inc(states_ready, 1)

            def att_out(h):
                dve.tensor_tensor(attT[:, h, :, :], out_of(G["att", h]).rearrange("p (b i) -> p b i", b=TB),
                                  gmask[:, :].unsqueeze(1).to_broadcast((P, TB, P)), ALU.mult).then_inc(gemm_out, 1)

            att_out(0)
            chunk_states(0)
            att_out(1)
            chunk_states(1)
            att_out(2)
            att_out(3)
            add_to_h(G["owo0", 0], 0)
            add_to_h(G["owo0", 1], 1)

            def head_gate(h):
                moved(dve, G["o", h])
                link(dve.tensor_tensor(o_sb[:, h, :], o_sb[:, h, :], spread_of(f"gla{h}"), ALU.mult))
                dve.wait_ge(og_ready, h + 1)
                dve.scalar_tensor_tensor(out=o_sb[:, h, :], in0=o_sb[:, h, :], scalar=col("glag", 0), in1=og[:, h, :],
                                         op0=ALU.mult, op1=ALU.mult).then_inc(mix_in, 1)

            def gla_low(h):
                hid_low(HID["gla"] + h, o_sb[:, h, :], hidH[:, 1, h, :], hidL[:, 1, h, :])

            variance("gla0", GDV)
            inverse("gla0")
            variance("gla1", GDV)
            inverse("gla1")
            head_gate(0)
            variance("gla2", GDV)
            inverse("gla2")
            head_gate(1)
            add_to_h(G["owo0", 2], 2)
            variance("gla3", GDV)
            inverse("gla3")
            head_gate(2)
            add_to_h(G["owo0", 3], 3)
            head_gate(3)
            split_after("owo0a")
            for h in range(GH):
                gla_low(h)
                add_to_h(G["owo0", 4 + h], 4 + h)
            split_after("owo0b")
            for c in range(KD):
                add_to_h(G["owo1", c], c)
                lo_part("mlp1", c)
                if c == 3:
                    split_after("owo1a")
            split_after("owo1b")
            variance("mlp1", D)
            inverse("mlp1")
            dve.wait_ge(rstd_ready, 4)
            mlp(1)
            y_out(KD - 1)
            variance("final", D)
            inverse("final")
            for b in range(TB):
                dve.tensor_scalar(y_tok[:, b, :], y_tok[:, b, :], rcol[:, b:b + 1], None, ALU.mult).then_inc(y_scaled, 1)

        @block.tensor
        def _(pe):
            mm = nc.tensor.matmul

            def ring(k, static=None):
                if static is not None:
                    moved(pe, k - RING, static - RING)
                elif k >= RING:
                    moved(pe, k - RING)
                return bank[(k if static is None else static) % RING]

            def tile(n, slot=None, kc=None, cols=None):
                if slot is None:
                    slot, kc, cols = n, TILES[n][1], TILES[n][2] if cols is None else cols
                pe.wait_ge(wl_ready, n + 1)
                return tile_view(wH, slot % 2, kc, cols), tile_view(wL, slot % 2, kc, cols)

            def project(dst, w, xs, c0, m=P, ready=None):
                return project_many([(dst, c0)], w, xs, m, ready)[0]

            def project_many(dsts, w, xs, m=P, ready=None):
                wh, wl = w
                lasts = [None] * len(dsts)
                for kc, (xh, xlo) in enumerate(xs):
                    if ready is not None:
                        ready(kc)
                    for d, (dst, c0) in enumerate(dsts):
                        for n, (a, b) in enumerate(((wh, xh), (wh, xlo), (wl, xh))):
                            lasts[d] = mm(dst, a[:, kc, c0:c0 + m], b, start=(kc == 0 and n == 0),
                                          stop=(kc == len(xs) - 1 and n == 2))
                return lasts

            def project_tokens(dst, w, xs, tb, cols):
                wh, wl = (v(cols) for v in w)
                for kc, (xh, xlo) in enumerate(xs):
                    at = slice(tb * P, (tb + 1) * P)
                    for n, (a, b) in enumerate(((xh, wh), (xh, wl), (xlo, wh))):
                        last = mm(dst, a[:, at], b[kc], start=(kc == 0 and n == 0), stop=(kc == len(xs) - 1 and n == 2))
                return last

            hg = [(hgH[:, c, :], hgL[:, c, :]) for c in range(KD)]
            hid = [[(hidH[:, b, c, :], hidL[:, b, c, :]) for c in range(4)] for b in range(2)]
            latents = list(zip(latent_hi, latent_lo))
            latent_q, latent_kv = latents[0:3], latents[3:5]

            def hg_wait(norm):
                return lambda kc: pe.wait_ge(hg_ready, KD * INST[norm] + kc + 1)

            def hid_wait(h0):
                return lambda kc: pe.wait_ge(hid_ready, h0 + kc + 1)

            def statistic(name):
                s, chunks = STAT[name], STATS[STAT[name]][1]
                pe.wait_ge(sq_ready, SQ[name] + chunks)
                if chunks > 1:
                    pe.wait_ge(acc_ready, ADDS[name] + chunks - 1)
                if s:
                    pe.wait_ge(var_ready, s)
                for b in range(TB):
                    last = mm(stat_bank[:, b:b + 1], acc[:, s % 2, b * P:(b + 1) * P], ones[:, 0:1], start=True, stop=True)
                last.then_inc(stat_done, 1)

            def spread(name):
                pe.wait_ge(diag_ready, SPREAD[name] + 1)
                mm(bank[5 + SPREAD[name] % 2][:, :], ones[:, :], diag[:, :, :], start=True, stop=True).then_inc(spread_done, 1)

            def spread_at(name, at=6):
                return lambda kc: spread(name) if kc == at else None

            pe.wait_ge(ident_ready, 1)
            pe.wait_ge(ld_prm, 16 * len(PARAM_ROWS))
            pe.transpose(stat_bank[:, 0:NPARAM], prm[:, :], ident[0:NPARAM, 0:NPARAM]).then_inc(params_done, 1)
            for c in range(KD):
                dst = ring(G["x", c])
                for b in range(TB):
                    if c == 0:
                        pe.wait_ge(ld_x[b], 16)
                    last = pe.transpose(dst[:, b * P:(b + 1) * P], x_tok[:, b, c * P:(c + 1) * P], ident[:, :])
                last.then_inc(gemm_done, 1)

            def pair_of(key, names, norm=None, hooks=(None, None)):
                w = tile(TILE[key])
                if norm:
                    dsts = [(ring(G[name])[:, :], i * P) for i, name in enumerate(names)]
                    for last in project_many(dsts, w, hg, ready=hg_wait(norm)):
                        last.then_inc(gemm_done, 1)
                    return
                for i, name in enumerate(names):
                    project(ring(G[name])[:, :], w, hg, i * P, ready=hooks[i]).then_inc(gemm_done, 1)

            pair_of("cq01", [("cq", 0), ("cq", 1)], "mix0")
            pe.wait_ge(consts_ready, 1)
            statistic("mix0")
            pair_of("cq2kv0", [("cq", 2), ("cq", 3)], hooks=(spread_at("mix0"), None))
            w = tile(TILE["kv1kr"], cols=192)
            project(ring(G["cq", 4])[:, :], w, hg, 0).then_inc(gemm_done, 1)
            project(ring(G["kr", 0])[:, :], w, hg, 64).then_inc(gemm_done, 1)
            statistic("q")
            pair_of("c0", [("c", 0), ("c", 1)], hooks=(spread_at("q", 7), lambda kc: statistic("kv") if kc == 0 else None))
            pair_of("u0", [("u", 0), ("u", 1)], hooks=(spread_at("kv"), None))
            pair_of("b0", [("b", 0), ("b", 1)])
            for n in "cub":
                pair_of(f"{n}1", [(n, 2), (n, 3)])
            wh, wl = tile(TILE["ukv"])
            pe.wait_ge(cn_ready, 5)

            def value_cols(v):
                return lambda _: [v[:, k, :].rearrange("p (h d) -> p h d", h=HEADS)[:, :, NOPE:NOPE + VD] for k in range(2)]

            for tb in range(TB):
                dst = ring(G["v", tb])[:, :].rearrange("p (h d) -> p h d", h=HEADS)
                project_tokens(dst, (value_cols(wh), value_cols(wl)), latent_kv, tb, None).then_inc(gemm_done, 1)
            for h in range(HEADS):
                project(ring(G["k", h])[:, :], (wh, wl), latent_kv, P * h).then_inc(gemm_done, 1)

            def query(h):
                w = tile(TILE[f"uq{h // 4}"], cols=4 * P)
                project(ring(G["q", h])[:, :], w, latent_q, P * (h % 4)).then_inc(gemm_done, 1)

            def scores(h, u):
                n = NU * h + u
                if u == 0:
                    pe.wait_ge(q_roped, h + 1)
                    pe.wait_ge(kr_copied, 1)
                    pe.wait_ge(q_nope, h + 1)
                    moved(pe, G["k", h])
                if n >= 2:
                    pe.wait_ge(p_ready, n - 1)
                for i in s_units[u]:
                    at = 0 if i != 1 else P
                    dst = s_banks[n % 2]
                    mm(dst[:, at:at + P * (i + 1)], qT[0:QK, h, i * P:(i + 1) * P], kT[0:QK, h, 0:P * (i + 1)],
                       start=True, stop=False)
                    last = mm(dst[:, at + P * i:at + P * (i + 1)], identb[:, :], causal[:, :], start=False, stop=True)
                last.then_inc(s_done, 1)

            def turned_moved(n):
                h, g = n // NG, n % NG
                if g == 1:
                    pe.wait_ge(pt_out, h + 1)
                else:
                    pe.wait_ge(pt_out_act, 2 * h + g // 2 + 1)

            def turn(h):
                pe.wait_ge(p_ready, NU * (h + 1))
                for g, blocks in enumerate(pt_groups):
                    n = NG * h + g
                    if n >= 2:
                        turned_moved(n - 2)
                    for b, (j, i) in enumerate(blocks):
                        last = pe.transpose(pt_banks[n % 2][:, b * P:(b + 1) * P],
                                            probs[:, h % 2, p_at[i] + j * P:p_at[i] + (j + 1) * P], ident[:, :])
                    last.then_inc(pt_done, 1)

            def weigh(h):
                for g in range(NG):
                    turned_moved(NG * h + g)
                if h:
                    pe.wait_ge(o_out, h)
                for i in range(TB):
                    for j in range(i + 1):
                        at = P * turned.index((j, i))
                        last = mm(o_bank[:, i * VD:(i + 1) * VD], probsT[:, h % 2, at:at + P],
                                  v_tok[:, j, h * VD:(h + 1) * VD], start=(j == 0), stop=(j == i))
                last.then_inc(o_done, 1)

            for h in range(Q_AHEAD):
                query(h)
            for step in range(STEPS):
                if step < HEADS:
                    scores(step, 0)
                    scores(step, 1)
                if 1 <= step <= HEADS:
                    turn(step - 1)
                if step + Q_AHEAD < HEADS:
                    query(step + Q_AHEAD)
                if step >= 3 and step % 2 == 1:
                    pr = (step - 3) // 2
                    pe.wait_ge(o_out, 2 * pr + 2)
                    dst = ring(G["ot", pr])
                    for b in range(TB):
                        last = pe.transpose(dst[:, b * P:(b + 1) * P], o_tok[:, pr % 2, b, :], ident[:, :])
                    last.then_inc(gemm_done, 1)
                if step < HEADS:
                    scores(step, 2)
                if step >= 2:
                    c = step - 2
                    if c % 4 == 0:
                        wo = tile(TILE["ewo0" + "ab"[c // 4]])
                    project(ring(G["ewo0", c])[:, :], wo, hid[0], P * (c % 4),
                            ready=hid_wait(READY["sconv"]) if c == 0 else None).then_inc(gemm_done, 1)
                if 1 <= step <= HEADS:
                    weigh(step - 1)

            def down(name, half, buf, chunks, ready=None):
                wo = tile(TILE[f"{name}{half}"])
                for c in chunks:
                    project(ring(G[name, c])[:, :], wo, hid[buf], P * (c % 4),
                            ready=ready if c == chunks[0] else None).then_inc(gemm_done, 1)

            moved(pe, G["ot", HEADS // 2 - 1])
            down("ewo1", "a", 1, range(4))
            down("ewo1", "b", 1, range(4, 8))

            def mlp(layer):
                n0, g0, h0 = TILE[f"mlp{layer}"], G[f"mlp{layer}", 0], READY[f"mlp{layer}"]

                def up(n, slot, k, rk):
                    for half in range(2):
                        w = tile(n + half, slot + half, KD, 256)
                        for m in range(2):
                            c = 2 * half + m
                            project(ring(k + c, rk + c)[:, :], w, hg, m * P).then_inc(gemm_done, 1)

                def down(n, slot, k, rk, hid0, buf):
                    pe.wait_ge(hid_ready, hid0 + 4)
                    for half in range(2):
                        w = tile(n + half, slot + half, 4, 512)
                        for m in range(4):
                            c = 4 * half + m
                            project(ring(k + c, rk + c)[:, :], w, hid[buf], m * P).then_inc(gemm_done, 1)

                w = tile(n0, n0, KD, 256)
                for last in project_many([(ring(g0 + m)[:, :], m * P) for m in range(2)], w, hg, ready=hg_wait(f"mlp{layer}")):
                    last.then_inc(gemm_done, 1)
                statistic(f"mlp{layer}")
                w = tile(n0 + 1, n0 + 1, KD, 256)
                project(ring(g0 + 2)[:, :], w, hg, 0, ready=spread_at(f"mlp{layer}")).then_inc(gemm_done, 1)
                project(ring(g0 + 3)[:, :], w, hg, P).then_inc(gemm_done, 1)
                with pe.Fori(1, LOOPS + 1) as i:
                    for pair in range(2):
                        n, g = n0 - 6 + 4 * pair, g0 + 4 - 24 + 12 * pair
                        up(n + 8 * i, n, g + 24 * i, g + 24)
                        down(n + 2 + 8 * i, n + 2, g + 4 + 24 * i, g + 4 + 24, h0 - 8 + 4 * pair + 8 * i, pair)
                n, g = n0 + 2 + 8 * LOOPS, g0 + 4 + 24 * LOOPS
                up(n, n, g, g)
                down(n + 2, n + 2, g + 4, g + 4, h0 + 8 * LOOPS, 0)
                if layer == 0:
                    down(n + 4, n + 4, g + 12, g + 12, h0 + 4 + 8 * LOOPS, 1)
                    return
                pe.wait_ge(hid_ready, h0 + 4 * BLOCKS)
                for c in range(KD):
                    if c % 4 == 0:
                        w = tile(n + 4 + c // 4, n + 4 + c // 4, 4, 512)
                    project(ring(G["last", c])[:, :], w, hid[1], P * (c % 4)).then_inc(gemm_done, 1)
                    if c:
                        y_turn(c - 1)

            def y_turn(c):
                pe.wait_ge(y_new, c + 1)
                dst = ring(G["yt", c])
                for b in range(TB):
                    last = pe.transpose(dst[:, b * P:(b + 1) * P], yT[:, c, b * P:(b + 1) * P], ident[:, :])
                last.then_inc(gemm_done, 1)

            mlp(0)

            w = tile(TILE["glr"])
            project(ring(G["glr", 0])[:, :], w, hg, 0, ready=hg_wait("mix1")).then_inc(gemm_done, 1)
            statistic("mix1")
            pair_of("gq", [("gq", 0), ("gq", 1)], hooks=(None, spread_at("mix1", 0)))
            pe.wait_ge(ld_gup, 16)
            moved(pe, G["glr", 0])
            for p in range(2):
                mm(ring(G["z", p])[:, :], gup[:, p * P:(p + 1) * P], glr[:, :], start=True, stop=True).then_inc(gemm_done, 1)
            pair_of("gk", [("gk", 0), ("gk", 1)])
            pair_of("x0", [("xl", 0), ("xl", 1)])
            pair_of("y0", [("y", 0), ("y", 1)])

            def lru_gates(c):
                pe.wait_ge(xc_ready, c + 1)
                pe.wait_ge(ld_wgate, 64)
                for gate, name in enumerate(("ra", "ri")):
                    mm(ring(G[name, c])[:, :], wgate[:, gate, c, :], xc[:, c, :], start=True, stop=True).then_inc(gemm_done, 1)

            lru_gates(0)
            lru_gates(1)
            pair_of("x1", [("xl", 2), ("xl", 3)])
            pair_of("y1", [("y", 2), ("y", 3)])
            lru_gates(2)
            lru_gates(3)
            for half in range(2):
                wh, wl = tile(TILE[f"gv{half}"])
                cols = [(lambda v: (lambda _: [v[:, k, :] for k in range(KD)]))(v) for v in (wh, wl)]
                for tb in range(TB):
                    project_tokens(ring(G[f"gv{half}", tb])[:, 0:256], cols, hg, tb, None).then_inc(gemm_done, 1)
            pair_of("og0", [("og", 0), ("og", 1)])
            pair_of("og1", [("og", 2), ("og", 3)])

            def key_turn(p):
                dst = ring(G["kt", p])
                for b in range(TB):
                    last = pe.transpose(dst[:, b * P:(b + 1) * P], gk[:, p, b * P:(b + 1) * P], ident[:, :])
                last.then_inc(gemm_done, 1)

            def key_values(p):
                moved(pe, G["kt", p])
                for n in range(NCH - 1):
                    tok = slice(GCH * (n % 2), GCH * (n % 2) + GCH)
                    for side in range(2):
                        h = 2 * p + side
                        last = mm(bank[3 + 2 * p + n % 2][64 * side:64 * side + 64, (n // 2) * P:(n // 2 + 1) * P],
                                  gkT[tok, n // 2, P * p + 64 * side:P * p + 64 * side + 64],
                                  gv[tok, n // 2, h * GDV:(h + 1) * GDV], start=True, stop=True)
                last.then_inc(kv_done, 1)

            def gla_scores(h):
                half, p = slice(64 * (h % 2), 64 * (h % 2) + 64), h // 2
                dst = ring(G["att", h])
                for b in range(TB):
                    last = mm(dst[:, b * P:(b + 1) * P], gki[half, p, b * P:(b + 1) * P], gq[half, p, b * P:(b + 1) * P],
                              start=True, stop=True)
                last.then_inc(gemm_done, 1)

            def gla_head(h):
                half, p = slice(64 * (h % 2), 64 * (h % 2) + 64), h // 2
                pe.wait_ge(states_ready, p + 1)
                moved(pe, G["att", h])
                dst = ring(G["o", h])
                for b in range(TB):
                    mm(dst[:, b * P:(b + 1) * P], gv[:, b, h * GDV:(h + 1) * GDV], attT[:, h, b, :], start=True, stop=False)
                    for n in (2 * b, 2 * b + 1):
                        if n:
                            last = mm(dst[:, n * GCH:(n + 1) * GCH], states[half, p, n, :], gq[half, p, n * GCH:(n + 1) * GCH],
                                      start=False, stop=(n % 2 == 1))
                last.then_inc(gemm_done, 1)

            wo = None

            def lru_down(c):
                nonlocal wo
                if c % 4 == 0:
                    wo = tile(TILE["owo0" + "ab"[c // 4]])
                project(ring(G["owo0", c])[:, :], wo, hid[0], P * (c % 4),
                        ready=hid_wait(READY["lru"]) if c == 0 else None).then_inc(gemm_done, 1)

            pe.wait_ge(gla_ready, 1)
            key_turn(0)
            key_turn(1)
            gla_scores(0)
            key_values(0)
            gla_scores(1)
            key_values(1)
            gla_scores(2)
            gla_scores(3)
            lru_down(0)
            lru_down(1)
            gla_head(0)
            gla_head(1)
            statistic("gla0")
            gla_head(2)
            statistic("gla1")
            gla_head(3)
            spread("gla0")
            lru_down(2)
            statistic("gla2")
            spread("gla1")
            lru_down(3)
            statistic("gla3")
            spread("gla2")
            lru_down(4)
            spread("gla3")
            for c in range(5, KD):
                lru_down(c)
            down("owo1", "a", 1, range(4), hid_wait(READY["gla"]))
            down("owo1", "b", 1, range(4, 8))
            mlp(1)
            y_turn(KD - 1)
            statistic("final")


_INS = ['x', 'positions', 'mixer_norm_g', 'mlp_norm_g', 'mlp_w1', 'mlp_w2', 'final_norm_g', 'ev_w_in', 'ev_conv_w',
        'mla_q_norm_g', 'mla_w_uq', 'mla_kv_norm_g', 'mla_w_ukv', 'ev_w_out', 'od_w_in', 'gla_w_gate_up', 'gla_b_gate',
        'gla_norm_g', 'lru_conv_w', 'lru_conv_b', 'lru_w_a', 'lru_b_a', 'lru_w_i', 'lru_b_i', 'lru_lambda', 'od_w_out']


def kernel(**inputs):
    import concourse.bacc as bacc
    from concourse.bass_utils import run_bass_kernel_spmd

    nc = bacc.Bacc("TRN2", target_bir_lowering=False, num_devices=1)
    arrays, t = {}, {}
    for name in _INS:
        a = np.ascontiguousarray(inputs[name])
        arrays[f"in_{name}"] = a
        t[name] = nc.dram_tensor(f"in_{name}", a.shape, mybir.dt.from_np(a.dtype), kind="ExternalInput").ap()
    freq = np.float32(10000.0) ** (-np.arange(0, ROPE, 2, dtype=np.float32) / np.float32(ROPE))
    par = np.zeros((2 * ROPE, 4), np.float32)
    par[:, 0] = np.tile(freq, 4)
    par[:ROPE, 1], par[:ROPE, 2] = 0.25, np.pi / 2
    par[:, 3] = 1.0
    par[ROPE:ROPE + ROPE // 2, 3] = -1.0
    arrays["in_rope_par"] = par
    t["rope_par"] = nc.dram_tensor("in_rope_par", par.shape, F32, kind="ExternalInput").ap()
    out = nc.dram_tensor("out_0", (1, S, D), F32, kind="ExternalOutput").ap()
    trunk(nc, t, out)
    r = run_bass_kernel_spmd(nc, [arrays], core_ids=[0])
    return r.results[0]["out_0"]
```

```python
from contextlib import ExitStack

import numpy as np

import concourse.bass as bass
from concourse import mybir

F32 = mybir.dt.float32
F32R = mybir.dt.float32r
BF16 = mybir.dt.bfloat16
I32 = mybir.dt.int32
ALU = mybir.AluOpType
ACT = mybir.ActivationFunctionType
AX_X = mybir.AxisListType.X

P = 128
S = 512
D = 1024
KD = D // P
TB = S // P
D_FF = 4 * D
EPS = 1e-6
CH = 512 // P

SC_K = 3
HEADS, NOPE, ROPE, VD = 8, 64, 32, 64
QR, KVR = 384, 256
QK = NOPE + ROPE
SCALE = QK ** -0.5
MASKED = -1e37

GH, GDK, GDV, GRANK, GTAU, GCH = 4, 64, 128, 16, 16.0, 64
NCH = S // GCH
LRU_K, LRU_C = 4, 8.0

RAW = 4
RING = 3
BLOCKS = D_FF // 512

PARAM_ROWS = [("mix0", KD), ("mix1", KD), ("mlp0", KD), ("mlp1", KD), ("final", KD), ("qg", 3), ("kvg", 2),
              ("evconv", SC_K * CH), ("gbias", 2), ("glag", 1), ("lconvw", LRU_K * CH), ("lconvb", CH),
              ("ba", CH), ("bi", CH), ("lam", CH)]
PCOL = {}
_n = 0
for _name, _rows in PARAM_ROWS:
    PCOL[_name] = _n
    _n += _rows
NPARAM = _n
NMIX = 2 * KD


def tile_table():
    tiles = [("cq01", KD, 256), ("cq2kv0", KD, 256), ("kv1kr", KD, 160)]
    for g in range(2):
        tiles += [(f"c{g}", KD, 256), (f"u{g}", KD, 256), (f"b{g}", KD, 256)]
    tiles += [("ukv", 2, 1024), ("uq0", 3, 384), ("uq1", 3, 384)]
    tiles += [("ewo0a", 4, 512), ("ewo0b", 4, 512), ("ewo1a", 4, 512), ("ewo1b", 4, 512)]
    tiles += [("mlp0", 0, 0)] * (4 * BLOCKS)
    tiles += [("glr", KD, 128), ("gq", KD, 256), ("gk", KD, 256)]
    for g in range(2):
        tiles += [(f"x{g}", KD, 256), (f"y{g}", KD, 256)]
    tiles += [("gv0", KD, 256), ("gv1", KD, 256), ("og0", KD, 256), ("og1", KD, 256)]
    tiles += [("owo0a", 4, 512), ("owo0b", 4, 512), ("owo1a", 4, 512), ("owo1b", 4, 512)]
    tiles += [("mlp1", 0, 0)] * (4 * BLOCKS)
    return tiles


STEPS = HEADS + 2
Q_AHEAD = 2


def between_turns(step):
    if step == 0:
        return [("v", 0), ("v", 1)]
    return [("q", step + Q_AHEAD) if step + Q_AHEAD < HEADS else ("ewo0", {6: 3, 7: 4, 8: 5, 9: 7}[step])]


def before_weighing(step):
    if step == 0:
        return [("v", 2), ("v", 3), ("q", Q_AHEAD)]
    return [("ewo0", {3: 0, 4: 1, 5: 2, 8: 6}[step])] if step in (3, 4, 5, 8) else []


FIRST_HEADS = [("k", 0), ("k", 1), ("k", 2), ("q", 0), ("k", 3), ("q", 1)]
SPLIT_STEPS = {2: "uq0", 5: "uq1", 7: "ewo0a", 9: "ewo0b"}


def turned_after(c):
    return [c - 1] if c > 2 else [0, 1] if c == 2 else []


def gemm_order():
    order, last = [], {}

    def use(tile, names):
        order.extend(names)
        last[tile] = len(order)

    use("cq01", [("cq", 0), ("cq", 1)])
    use("cq2kv0", [("cq", 2), ("cq", 3)])
    use("kv1kr", [("cq", 4), ("kr", 0)])
    for g in range(2):
        for n in "cub":
            use(f"{n}{g}", [(n, 2 * g), (n, 2 * g + 1)])
    order += FIRST_HEADS
    for step in range(STEPS):
        order += between_turns(step)
        if step >= 3 and step % 2 == 1:
            order.append(("ot", (step - 3) // 2))
        order += before_weighing(step)
    for tile, result in (("ukv", ("v", 3)), ("uq0", ("q", 3)), ("uq1", ("q", 7)), ("ewo0a", ("ewo0", 3)), ("ewo0b", ("ewo0", 7))):
        last[tile] = order.index(result) + 1
    use("ewo1a", [("ewo1", c) for c in range(4)])
    use("ewo1b", [("ewo1", c) for c in range(4, 8)])
    order += [("mlp0", i) for i in range(12 * BLOCKS)]
    use("glr", [("glr", 0)])
    use("gq", [("gq", 0), ("gq", 1)])
    order += [("z", 0), ("z", 1)]
    use("gk", [("gk", 0), ("gk", 1)])
    use("x0", [("xl", 0), ("xl", 1)])
    use("y0", [("y", 0), ("y", 1)])
    order += [("ra", 0), ("ri", 0)]
    use("x1", [("xl", 2), ("ra", 1), ("ri", 1), ("xl", 3)])
    use("y1", [("y", 2), ("y", 3)])
    order += [("ra", 2), ("ri", 2)]
    use("gv0", [("gv0", 0), ("gv0", 1), ("ra", 3), ("ri", 3), ("gv0", 2), ("gv0", 3)])
    use("gv1", [("gv1", t) for t in range(TB)])
    use("og0", [("og", 0), ("og", 1)])
    use("og1", [("og", 2), ("og", 3)])
    order += [("kt", 0), ("kt", 1), ("att", 0), ("owo0", 0), ("att", 1), ("owo0", 1), ("att", 2), ("att", 3)]
    for h in range(GH):
        order += [("o", h), ("owo0", 2 + h)]
    order += [("owo0", 6), ("owo0", 7)]
    last["owo0a"], last["owo0b"] = order.index(("owo0", 3)) + 1, len(order)
    use("owo1a", [("owo1", c) for c in range(4)])
    use("owo1b", [("owo1", c) for c in range(4, 8)])
    order += [("mlp1", i) for i in range(12 * BLOCKS - 8)]
    for c in range(KD):
        order.append(("last", c))
        order += [("yt", n) for n in turned_after(c)]
    order.append(("yt", KD - 1))
    return order, {key: n for n, key in enumerate(order)}, last


TILES = tile_table()
TILE = {}
for _i, (_key, _k, _c) in enumerate(TILES):
    TILE.setdefault(_key, _i)
ORDER, G, TILE_LAST = gemm_order()

BY_ACT = ("v", "k", "z", "ra", "ri", "gv0", "gv1", "kt", "o")
MOVED = []
_act = _dve = 0
for _key in ORDER:
    if _key[0] in BY_ACT:
        _act += 1
        MOVED.append((True, _act))
    else:
        _dve += 1
        MOVED.append((False, _dve))

HID = {"sconv": 0, "attn": 4, "mlp0": 8, "lru": 8 + 4 * BLOCKS, "gla": 12 + 4 * BLOCKS, "mlp1": 16 + 4 * BLOCKS}
READY = {"sconv": 0, "mlp0": 4, "lru": 4 + 4 * BLOCKS, "gla": 8 + 4 * BLOCKS, "mlp1": 12 + 4 * BLOCKS}
MIX_IN = {"sconv": 0, "lru": 4, "gla": 8}
STATS = [("mix0", KD, True), ("q", 3, True), ("kv", 2, True), ("mlp0", KD, True), ("mix1", KD, True)]
STATS += [(f"gla{h}", 1, True) for h in range(GH)] + [("mlp1", KD, True), ("final", KD, False)]
STAT = {name: i for i, (name, _, _) in enumerate(STATS)}
SPREAD = {name: sum(b for _, _, b in STATS[:i]) for i, (name, _, _) in enumerate(STATS)}
SQ, ADDS = {}, {}
_s = _a = 0
for _name, _chunks, _ in STATS:
    SQ[_name], ADDS[_name] = _s, _a
    _s += _chunks
    _a += _chunks - 1
INST = {"mix0": 0, "mlp0": 1, "mix1": 2, "mlp1": 3}


def trunk(nc, t, out):
    ctx = ExitStack()
    with ctx:
        arena_bytes = 0
        places = []

        def place(name, shape, dt, at=None):
            nonlocal arena_bytes
            size = int(np.prod(shape[1:])) * mybir.dt.size(dt)
            size = (size + 31) // 32 * 32
            where = arena_bytes if at is None else at
            if at is None:
                arena_bytes += size
            places.append(where + size)
            return nc.alloc_sbuf_tensor_at(name, shape, dt, offset=base + where), where

        base = (nc.sbuf_base + 31) // 32 * 32

        hT, _ = place("hT", [P, KD, S], F32)
        hgH, hg_at = place("hgH", [P, KD, S], F32R)
        hgL, _ = place("hgL", [P, KD, S], F32R)
        raw, _ = place("raw", [P, RAW, 2048], F32)
        wH, _ = place("wH", [P, 2, 2048], F32R)
        wL, _ = place("wL", [P, 2, 2048], F32R)
        hidH, hidH_at = place("hidH", [P, 2, 4, S], F32R)
        hidL, hidL_at = place("hidL", [P, 2, 4, S], F32R)
        rstd, _ = place("rstd", [P, S], F32)
        sqb, sqb_at = place("sqb", [P, 2, S], F32)
        diag_lo, _ = place("diag_lo", [P, TB, P], F32R, sqb_at)
        rcol_parts, _ = place("rcol_parts", [P, 2, TB], F32R)
        rcol_hi, rcol_lo = rcol_parts[:, 0, :], rcol_parts[:, 1, :]
        diag_hi, _ = place("diag_hi", [P, TB, P], F32R)
        acc, _ = place("acc", [P, 2, S], F32)
        tmpR, _ = place("tmpR", [P, S], F32)
        tmpS, _ = place("tmpS", [P, S], F32)
        ident, _ = place("ident", [P, P], F32)
        ones, _ = place("ones", [P, 1], F32)
        ones_r, _ = place("ones_r", [P, P], F32R)
        identb, _ = place("identb", [P, P], BF16)
        causal, _ = place("causal", [P, P], BF16)
        pcol, _ = place("pcol", [P, NPARAM], F32)
        small, _ = place("small", [P, 92], F32)
        resets, _ = place("resets", [P, S], F32)
        gmask, _ = place("gmask", [P, P], F32)
        gup, _ = place("gup", [GRANK, 2 * P], F32)
        area_at = arena_bytes

        NS = P * TB * (TB + 1) // 2
        conv_at = area_at + 22528
        v_tok, _ = place("v_tok", [P, TB, HEADS * VD], F32, area_at)
        o_tok, _ = place("o_tok", [P, 2, TB, P], F32, area_at + 8192)
        c_raw, _ = place("c_raw", [P, 5, S], F32, area_at)
        rope_cs, _ = place("rope_cs", [P, S], F32, area_at + 12288)
        kr_s, _ = place("kr_s", [P, S], F32, area_at + 16384)
        rope_tmp, _ = place("rope_tmp", [P, 2, S], F32, area_at + 18432)
        cu, _ = place("cu", [P, CH, S + SC_K - 1], F32, conv_at)
        c_s, _ = place("c_s", [P, 2, S], F32, conv_at + 8224)
        b_s, _ = place("b_s", [P, CH, S], F32, conv_at + 12320)
        probs, _ = place("probs", [P, 2, NS], F32, conv_at)
        probsT, _ = place("probsT", [P, 2, NS], F32, conv_at + 8 * NS)
        qT, _ = place("qT", [P, HEADS, S], F32, hg_at)
        kT, _ = place("kT", [P, HEADS, S], F32, hg_at + 4 * HEADS * S)
        x_tok, _ = place("x_tok", [P, TB, D], F32, conv_at)
        prm, _ = place("prm", [NPARAM, P], F32, area_at + 16384)
        pos_i, _ = place("pos_i", [P, S], I32, area_at + 18432)
        ang, _ = place("ang", [P, S], F32, area_at + 20480)
        ang_k, _ = place("ang_k", [P, S], F32, area_at + 14336)
        turns, _ = place("turns", [P, S], F32, conv_at + 16384)
        gq, _ = place("gq", [P, 2, S], F32, area_at)
        gk, _ = place("gk", [P, 2, S], F32, area_at + 4096)
        gki, _ = place("gki", [P, 2, S], F32, area_at + 8192)
        cum, _ = place("cum", [P, 2, S], F32, area_at + 12288)
        ge, _ = place("ge", [P, 2, S], F32, area_at + 16384)
        glr, _ = place("glr", [GRANK, S], F32, area_at + 16384)
        gel, _ = place("gel", [P, CH, S], F32, area_at + 12288)
        gv, _ = place("gv", [P, TB, GH * GDV], F32, area_at + 20480)
        og, _ = place("og", [P, GH, S], F32, area_at + 28672)
        xl, _ = place("xl", [P, S + LRU_K - 1], F32, area_at + 36864)
        wgate, _ = place("wgate", [P, 2, CH, P], F32, area_at + 38944)
        xc, _ = place("xc", [P, CH, S], F32, hidL_at + 8192)
        lr, _ = place("lr", [P, 2, S], F32, hidH_at + 8192)
        li, _ = place("li", [P, 2, S], F32, hidH_at + 12288)
        lru_t, lru_u = sqb, acc
        gkT, _ = place("gkT", [P, TB, 2 * P], F32, hg_at)
        attT, _ = place("attT", [P, GH, TB, P], F32, hg_at + 4096)
        states, _ = place("states", [P, 2, NCH, GDV], F32, hg_at + 12288)
        o_sb, _ = place("o_sb", [P, GH, S], F32, hg_at + 20480)
        yT, _ = place("yT", [P, KD, S], F32, hg_at)
        y_tok, _ = place("y_tok", [P, TB, D], F32, area_at)
        ctx.enter_context(nc.sbuf_tensor("arena", [P, (max(places) + 3) // 4], F32))

        bank = [ctx.enter_context(nc.psum_tensor(f"bank{i}", [P, S], F32)) for i in range(8)]
        stat_bank = o_bank = bank[7]
        s_banks, pt_banks = bank[3:5], bank[5:7]
        x_banks = bank[3:7]

        mx, nmx, sums, rinv = small[:, 0:8], small[:, 8:16], small[:, 16:24], small[:, 24:28]
        vcol, rcol, rcol_mix1 = small[:, 32:36], small[:, 28:32], small[:, 88:92]
        decay = small[:, 36:52].rearrange("p (a n) -> p a n", a=2)
        lam_e, lam_d, lam_s, lam_s2 = (small[:, 52 + 4 * i:56 + 4 * i] for i in range(4))
        lam_p, lam_k, lam_nk = (small[:, 68 + 4 * i:72 + 4 * i] for i in range(3))
        rope_par = small[:, 82:86]

        def col(name, c, n=1):
            return pcol[:, PCOL[name] + c:PCOL[name] + c + n]

        def sem(name):
            return ctx.enter_context(nc.semaphore(name))

        ld_x = [sem(f"ld_x{i}") for i in range(2)]
        ld_mix, ld_prm, ld_freq, ld_pos = sem("ld_mix"), sem("ld_prm"), sem("ld_freq"), sem("ld_pos")
        ld_gup, ld_wgate, ld_out = sem("ld_gup"), sem("ld_wgate"), sem("ld_out")
        x_done, x_out = sem("x_done"), sem("x_out")
        raw_loaded = [sem(f"raw_loaded{i}") for i in range(RAW)]
        wh_ready, wl_ready = sem("wh_ready"), sem("wl_ready")
        gemm_done, gemm_out, gemm_out_act = sem("gemm_done"), sem("gemm_out"), sem("gemm_out_act")
        ident_ready, consts_ready = sem("ident_ready"), sem("consts_ready")
        params_done, params_ready = sem("params_done"), sem("params_ready")
        hi_new, hg_ready, sq_ready, acc_ready = sem("hi_new"), sem("hg_ready"), sem("sq_ready"), sem("acc_ready")
        stat_done, var_ready, rt_ready = sem("stat_done"), sem("var_ready"), sem("rt_ready")
        diag_ready, spread_done, rstd_ready = sem("diag_ready"), sem("spread_done"), sem("rstd_ready")
        dve_link, act_link, pool_link = sem("dve_link"), sem("act_link"), sem("pool_link")
        rope_arg, rope_ready = sem("rope_arg"), sem("rope_ready")
        cn_scaled, cn_hi, cn_ready = sem("cn_scaled"), sem("cn_hi"), sem("cn_ready")
        cu_ready, mix_in, hid_hi, hid_ready = sem("cu_ready"), sem("mix_in"), sem("hid_hi"), sem("hid_ready")
        kr_ready, kr_copied = sem("kr_ready"), sem("kr_copied")
        q_nope, q_parts, q_roped = sem("q_nope"), sem("q_parts"), sem("q_roped")
        s_done, nmax_ready, p_ready = sem("s_done"), sem("nmax_ready"), sem("p_ready")
        pt_done, pt_out, pt_out_act, o_done, o_out = sem("pt_done"), sem("pt_out"), sem("pt_out_act"), sem("o_done"), sem("o_out")
        sq_self = sem("sq_self")
        ls_ready, cum_ready, e_ready, e_used = sem("ls_ready"), sem("cum_ready"), sem("e_ready"), sem("e_used")
        lam_exp, lam_ready, gel_ready, og_ready = sem("lam_exp"), sem("lam_ready"), sem("gel_ready"), sem("og_ready")
        gla_ready, kv_done, states_ready = sem("gla_ready"), sem("kv_done"), sem("states_ready")
        xc_ready, gates_ready = sem("xc_ready"), sem("gates_ready")
        lru_m, lru_rt, ix_ready = sem("lru_m"), sem("lru_rt"), sem("ix_ready")
        y_last = sem("y_last")
        y_new, final_ready, y_scaled, y_scaled_act = sem("y_new"), sem("final_ready"), sem("y_scaled"), sem("y_scaled_act")
        wzero = sem("wzero")

        p_at = [P * i * (i + 1) // 2 for i in range(TB)]
        turned = [(j, i) for j in range(TB) for i in range(j, TB)]
        pt_groups = [turned[n:n + 4] for n in range(0, len(turned), 4)]
        s_units = [(0, 1), (2,), (3,)]
        NU, NG = len(s_units), len(pt_groups)

        def rows(w):
            return w.rearrange("(k p) n -> p k n", p=P)

        e_in, o_in = rows(t["ev_w_in"][0]), rows(t["od_w_in"][0])
        src = {"cq01": e_in[:, :, 1536:1792], "cq2kv0": e_in[:, :, 1792:2048], "kv1kr": e_in[:, :, 2048:2208],
               "ukv": rows(t["mla_w_ukv"][0]), "glr": o_in[:, :, 1024:1152],
               "gq": o_in[:, :, 0:256], "gk": o_in[:, :, 256:512]}
        for g in range(2):
            c = 256 * g
            src[f"b{g}"], src[f"c{g}"], src[f"u{g}"] = (e_in[:, :, o + c:o + c + 256] for o in (0, 512, 1024))
            src[f"uq{g}"] = rows(t["mla_w_uq"][0])[:, :, 384 * g:384 * g + 384]
            src[f"gv{g}"], src[f"og{g}"] = (o_in[:, :, o + c:o + c + 256] for o in (512, 1040))
            src[f"x{g}"], src[f"y{g}"] = (o_in[:, :, o + c:o + c + 256] for o in (1552, 2064))
            for m, half in enumerate("ab"):
                src[f"ewo{g}{half}"] = rows(t["ev_w_out"][0])[:, 4 * g:4 * g + 4, 512 * m:512 * m + 512]
                src[f"owo{g}{half}"] = rows(t["od_w_out"][0])[:, 4 - 4 * g:8 - 4 * g, 512 * m:512 * m + 512]

        def tile_view(buf, slot, kc, n):
            return buf[:, slot, 0:kc * n].rearrange("p (k n) -> p k n", k=kc)

        LOOPS = (BLOCKS - 2) // 2

        pieces = [("mix0", t["mixer_norm_g"].rearrange("l n -> (l n)")), ("mlp0", t["mlp_norm_g"].rearrange("l n -> (l n)")),
                  ("final", t["final_norm_g"]), ("qg", t["mla_q_norm_g"][0]),
                  ("kvg", t["mla_kv_norm_g"][0]), ("evconv", t["ev_conv_w"][0].rearrange("k n -> (k n)")),
                  ("gbias", t["gla_b_gate"][0]), ("glag", t["gla_norm_g"][0]),
                  ("lconvw", t["lru_conv_w"][0].rearrange("k n -> (k n)")), ("lconvb", t["lru_conv_b"][0]),
                  ("ba", t["lru_b_a"][0]), ("bi", t["lru_b_i"][0]), ("lam", t["lru_lambda"][0])]
        latent_at = [(1, 1), (1, 2), (1, 3), (1, 0), (0, 3)]
        latent_hi = [hidH[:, b, c, :] for b, c in latent_at]
        latent_lo = [hidL[:, b, c, :] for b, c in latent_at]

        def load_params(eng, some, signal):
            for name, vec in some:
                v = vec.rearrange("(c p) -> c p", p=P)
                at = PCOL[name]
                eng.dma_start(prm[at:at + v.shape[0], :], v).then_inc(signal, 16)

        def turned_move(eng, h, groups, signal):
            for g in groups:
                n = NG * h + g
                eng.wait_ge(pt_done, n + 1)
                w = P * len(pt_groups[g])
                dst, source = probsT[:, h % 2, 4 * P * g:4 * P * g + w], pt_banks[n % 2][:, 0:w]
                if signal is pt_out_act:
                    eng.activation(dst, source, ACT.Copy).then_inc(signal, 1)
                else:
                    eng.tensor_copy(dst, source).then_inc(signal, 1)

        def moved(eng, k, static=None):
            by_act, count = MOVED[k if static is None else static]
            if static is not None:
                count = k + (count - static)
            eng.wait_ge(gemm_out_act if by_act else gemm_out, count)

        def split_pieces(key, dst, rawv):
            if key.startswith("uq"):
                d = dst.rearrange("p (k h n) -> p k h n", k=3, h=4)
                r = rawv.rearrange("p (k h n) -> p k h n", k=3, h=4)
                return ([(d[:, :, :, 0:QK], r)], [(d[:, k, :, a:a + 16], r[:, k, :, b:b + 16])
                                                  for k in range(3) for a, b in ((96, 80), (112, 64))])
            if key == "kv1kr":
                d = dst.rearrange("p (k n) -> p k n", k=KD)
                r = rawv.rearrange("p (k n) -> p k n", k=KD)
                return ([(d[:, :, 0:160], r)], [(d[:, :, 160:176], r[:, :, 144:160]), (d[:, :, 176:192], r[:, :, 128:144])])
            if key == "ukv":
                d = dst.rearrange("p (k s h n) -> p k s h n", k=2, s=2, h=HEADS)
                r = rawv.rearrange("p (k h s n) -> p k s h n", k=2, s=2, h=HEADS)
                return ([(d[:, :, s], r[:, :, s]) for s in range(2)], [])
            return ([(dst, rawv)], [])

        def split_width(n):
            key, kc, cols = TILES[n]
            return 3 * 4 * P if key.startswith("uq") else KD * 192 if key == "kv1kr" else kc * cols or 2048

        block = ctx.enter_context(nc.Block())

        @block.sync
        def _(sp):
            def load(n, view, kc, cols, count=None):
                first = isinstance(n, int) and n < RAW
                slot = n % RAW if isinstance(n, int) else count
                if not first:
                    sp.wait_ge(wl_ready, n - RAW + 1)
                sp.dma_start(tile_view(raw, slot, kc, cols), view).then_inc(raw_loaded[slot], 16)

            def plain(lo, hi):
                for n in range(lo, hi):
                    key, kc, cols = TILES[n]
                    load(n, src[key], kc, cols)

            def mlp(layer):
                w1 = rows(t["mlp_w1"][layer])
                w2 = t["mlp_w2"][layer].rearrange("(b k p) n -> b p k n", k=4, p=P)
                n0 = TILE[f"mlp{layer}"]

                def up(n, j, slot):
                    for half in range(2):
                        load(n + half, w1[:, :, bass.ds(512 * j + 256 * half, 256)], KD, 256, (slot + half) % RAW)

                def down(n, j, slot):
                    for half in range(2):
                        view = w2[bass.ds(j, 1), :, :, 512 * half:512 * half + 512].rearrange("b p k n -> p (b k) n")
                        load(n + half, view, 4, 512, (slot + half) % RAW)

                up(n0, 0, n0)
                with sp.Fori(1, LOOPS + 1) as i:
                    for pair in range(2):
                        n, j = n0 + 2 - 8 + 4 * pair, 2 * i - 2 + pair
                        up(n + 8 * i, j + 1, n)
                        down(n + 2 + 8 * i, j, n + 2)
                n = n0 + 2 + 8 * LOOPS
                up(n, BLOCKS - 1, n)
                down(n + 2, BLOCKS - 2, n + 2)
                down(n + 4, BLOCKS - 1, n + 4)

            plain(0, 1)
            for half in range(2):
                at = slice(half * D // 2, (half + 1) * D // 2)
                sp.dma_start(x_tok[:, :, at], t["x"][0].rearrange("(b p) d -> p b d", p=P)[:, :, at]).then_inc(ld_x[half], 16)
            plain(1, 2)
            load_params(sp, pieces[3:], ld_prm)
            sp.dma_start(rope_par[64:128, :], t["rope_par"]).then_inc(ld_freq, 16)
            sp.dma_start(pos_i[64:128, :], t["positions"].broadcast_to((2 * ROPE, S))).then_inc(ld_pos, 16)
            plain(2, RAW)
            sp.dma_start(gup[:, :], t["gla_w_gate_up"][0]).then_inc(ld_gup, 16)
            plain(RAW, TILE["mlp0"])
            mlp(0)
            plain(TILE["glr"], TILE["x0"])
            sp.wait_ge(wzero, 1)
            for gate, w in enumerate((t["lru_w_a"][0], t["lru_w_i"][0])):
                pairs = w.rearrange("(c b) i j -> b i c j", b=2)
                for b in range(2):
                    sp.dma_start(wgate[64 * b:64 * b + 64, gate, :, 64 * b:64 * b + 64], pairs[b]).then_inc(ld_wgate, 16)
            plain(TILE["x0"], TILE["mlp1"])
            mlp(1)
            for b in range(TB):
                sp.wait_ge(y_scaled_act if b % 2 else y_scaled, b // 2 + 1)
                sp.dma_start(out[0, b * P:(b + 1) * P, :], y_tok[:, b, :]).then_inc(ld_out, 16)
            sp.wait_ge(ld_out, 16 * TB)

        @block.gpsimd
        def _(pool):
            n_link = 0

            def link(ins):
                nonlocal n_link
                n_link += 1
                ins.then_inc(pool_link, 1)
                pool.wait_ge(pool_link, n_link)

            link(pool.memset(ident[:, :], 0.0))
            pool.affine_select(out=ident[:, :], in_=ident[:, :], compare_op=ALU.not_equal, fill=1.0, base=0,
                               pattern=[[-1, P]], channel_multiplier=1).then_inc(ident_ready, 1)
            pool.wait_ge(ident_ready, 1)
            link(pool.memset(ones[:, :], 1.0))
            link(pool.memset(causal[:, :], 0.0))
            link(pool.affine_select(out=causal[:, :], in_=causal[:, :], compare_op=ALU.is_ge, fill=MASKED, base=0,
                                    pattern=[[-1, P]], channel_multiplier=1))
            link(pool.memset(gmask[:, :], 1.0))
            link(pool.affine_select(out=gmask[:, :], in_=gmask[:, :], compare_op=ALU.is_ge, fill=0.0, base=0,
                                    pattern=[[1, P]], channel_multiplier=-1))
            link(pool.memset(gmask[0:GCH, GCH:P], 0.0))
            link(pool.memset(resets[:, :], 1.0))
            link(pool.memset(resets[:, 0:S:GCH], 0.0))
            pool.tensor_copy(identb[:, :], ident[:, :]).then_inc(consts_ready, 1)
            pool.wait_ge(consts_ready, 1)

            def add_squares(name, chunks):
                a = acc[:, STAT[name] % 2, :]
                for c in range(1, chunks):
                    n = ADDS[name] + c - 1
                    pool.wait_ge(sq_ready, SQ[name] + c + 1)
                    if n:
                        pool.wait_ge(acc_ready, n)
                    pool.tensor_tensor(a, a, sqb[:, n % 2, :], ALU.add).then_inc(acc_ready, 1)

            add_squares("mix0", KD)
            add_squares("q", 3)
            add_squares("kv", 2)

            pool.wait_ge(acc_ready, ADDS["mlp0"])
            for c in range(CH):
                if c:
                    pool.wait_ge(cu_ready, c)
                moved(pool, G["u", c])
                pool.tensor_tensor(cu[:, c, 2:2 + S], cu[:, c, 2:2 + S], c_s[:, c % 2, :], ALU.mult).then_inc(cu_ready, 1)

            pool.wait_ge(cu_ready, CH)
            for h in range(HEADS):
                if h:
                    pool.wait_ge(q_roped, h)
                pool.wait_ge(q_parts, h + 1)
                moved(pool, G["q", h])
                pool.tensor_tensor(qT[64:96, h, :], qT[64:96, h, :], rope_tmp[64:96, h % 2, :], ALU.add).then_inc(q_roped, 1)

            pool.wait_ge(q_roped, HEADS)
            add_squares("mlp0", KD)
            add_squares("mix1", KD)

            pool.wait_ge(acc_ready, ADDS["mlp1"])
            pool.wait_ge(gemm_done, G["glr", 0] + 1)
            pool.memset(wgate[:, :, :, :], 0.0).then_inc(wzero, 1)
            pool.wait_ge(wzero, 1)

            for c in range(CH):
                if c:
                    pool.wait_ge(ix_ready, c)
                moved(pool, G["ri", c])
                pool.wait_ge(xc_ready, c + 1)
                pool.tensor_tensor(li[:, c % 2, :], li[:, c % 2, :], xc[:, c, :], ALU.mult).then_inc(ix_ready, 1)
            pool.wait_ge(ix_ready, CH)
            add_squares("mlp1", KD)
            add_squares("final", KD - 1)

        @block.scalar
        def _(act):
            def split(n, slot=None, size=2048):
                width, key = size, ""
                if isinstance(n, int):
                    key, slot, size, width = TILES[n][0], n, TILES[n][1] * TILES[n][2] or 2048, split_width(n)
                    act.wait_ge(raw_loaded[slot % RAW], 16 * (n // RAW + 1))
                main, extra = split_pieces(key, wH[:, slot % 2, 0:width], raw[:, slot % RAW, 0:size])
                for dst, source in main + extra:
                    ins = act.activation(dst, source, ACT.Copy)
                ins.then_inc(wh_ready, 1)

            def used(n):
                act.wait_ge(gemm_done, TILE_LAST[TILES[n][0]])

            def split_after(key):
                n = TILE[key]
                used(n)
                split(n + 2)

            n_link = 0

            def link(ins):
                nonlocal n_link
                n_link += 1
                ins.then_inc(act_link, 1)
                act.wait_ge(act_link, n_link)

            def square(source, name, c):
                n = ADDS[name] + c - 1
                if c and n >= 2:
                    act.wait_ge(acc_ready, n - 1)
                dst = sqb[:, n % 2, :] if c else acc[:, STAT[name] % 2, :]
                act.activation(dst, source, ACT.Square).then_inc(sq_ready, 1)

            def finalize(norm, c, k=None, between=None):
                if k is None:
                    act.wait_ge(x_out, c + 1)
                else:
                    moved(act, k)
                act.activation(hgH[:, c, :], hT[:, c, :], ACT.Copy, scale=col(norm, c)).then_inc(hi_new, 1)
                if between is not None:
                    between()
                square(hT[:, c, :], norm, c)

            def root(name):
                act.wait_ge(var_ready, STAT[name] + 1)
                act.activation(vcol, vcol, ACT.Sqrt).then_inc(rt_ready, 1)

            def spread_out(name):
                act.wait_ge(spread_done, SPREAD[name] + 1)
                act.activation(rstd[:, :], bank[5 + SPREAD[name] % 2][:, :], ACT.Copy).then_inc(rstd_ready, 1)

            def hid_split(n, source, dst):
                act.wait_ge(mix_in, n + 1)
                act.activation(dst, source, ACT.Copy).then_inc(hid_hi, 1)

            def mlp(layer):
                n0, g0 = TILE[f"mlp{layer}"], G[f"mlp{layer}", 0]
                s0 = 32 * layer

                def after(n, k, slot, first=None):
                    act.wait_ge(gemm_done, k + 1)
                    if first is None:
                        split(n + 2)
                    else:
                        act.wait_ge(raw_loaded[(slot + 2) % RAW], first)
                        split(n + 2, slot + 2)

                def up(k, static, buf, chunks, sq):
                    for m in chunks:
                        moved(act, k + m, static + m)
                        act.activation(tmpS[:, :], tmpR[:, :], ACT.Square).then_inc(sq_self, 1)
                        act.wait_ge(sq_self, sq + m + 1)
                        act.activation(hidH[:, buf, m, :], tmpS[:, :], ACT.Copy).then_inc(hid_hi, 1)

                root(f"mlp{layer}")
                after(n0, g0 + 1, n0)
                spread_out(f"mlp{layer}")
                up(g0, g0, 0, range(4), s0)
                after(n0 + 1, g0 + 3, n0 + 1)
                with act.Fori(1, LOOPS + 1) as i:
                    for pair in range(2):
                        n, g = n0 - 6 + 4 * pair, g0 + 4 - 24 + 12 * pair
                        for half in range(2):
                            up(g + 24 * i, g + 24, (pair + 1) % 2, (2 * half, 2 * half + 1), s0 + 4 - 8 + 4 * pair + 8 * i)
                            m = n + half
                            after(m + 8 * i, g + 2 * half + 1 + 24 * i, m, 32 * i + 16 * ((m + 2) // RAW + 1))
                        for half in range(2):
                            m = n + 2 + half
                            after(m + 8 * i, g + 4 + 4 * half + 3 + 24 * i, m, 32 * i + 16 * ((m + 2) // RAW + 1))
                n, g = n0 + 2 + 8 * LOOPS, g0 + 4 + 24 * LOOPS
                for half in range(2):
                    up(g, g, (BLOCKS - 1) % 2, (2 * half, 2 * half + 1), s0 + 4 + 8 * LOOPS)
                    after(n + half, g + 2 * half + 1, n + half)
                for half in range(2):
                    m = n + 2 + half
                    if m + 2 < len(TILES):
                        after(m, g + 4 + 4 * half + 3, m)
                for c in range(KD):
                    if layer == 0:
                        m = n + 4 + c // 4
                        finalize("mix1", c, g + 12 + c, (lambda: after(m, g + 12 + c, m)) if c % 4 == 3 else None)
                    else:
                        moved(act, G["last", c])
                        if c < KD - 1:
                            act.activation(yT[:, c, :], hT[:, c, :], ACT.Copy, scale=col("final", c)).then_inc(y_new, 1)
                        square(hT[:, c, :], "final", c)

            load_params(act, pieces[0:1], ld_mix)
            load_params(act, pieces[1:3], ld_prm)
            split(0)
            act.wait_ge(params_ready, 1)
            for c in range(KD):
                finalize("mix0", c)
            split(1)
            act.wait_ge(consts_ready, 1)
            act.activation(ones_r[:, :], ones[:, :].to_broadcast((P, P)), ACT.Copy)
            root("mix0")
            spread_out("mix0")

            def latent_square(c):
                moved(act, G["cq", c])
                square(c_raw[:, c, :], *(("q", c) if c < 3 else ("kv", c - 3)))

            latent_square(0)
            latent_square(1)
            split_after("cq01")
            act.wait_ge(rope_arg, 1)
            act.activation(rope_cs[64:128, :], ang_k[64:128, :], ACT.Sin, scale=rope_par[64:128, 3:4]).then_inc(rope_ready, 1)
            latent_square(2)
            latent_square(3)
            split_after("cq2kv0")
            latent_square(4)
            split_after("kv1kr")
            root("q")
            root("kv")
            split_after("c0")
            for c in range(5):
                act.wait_ge(cn_scaled, c + 1)
                act.activation(latent_hi[c], c_raw[:, c, :], ACT.Copy).then_inc(cn_hi, 1)
            for key in ("u0", "b0", "c1", "u1", "b1"):
                split_after(key)

            def move(key, dst, source, **how):
                act.wait_ge(gemm_done, G[key] + 1)
                act.activation(dst, source, ACT.Copy, **how).then_inc(gemm_out_act, 1)

            def keys_out(pr):
                act.wait_ge(gemm_done, G["k", pr] + 1)
                for side in range(2):
                    ins = act.activation(kT[0:NOPE, 2 * pr + side, :],
                                         bank[G["k", pr] % RING][NOPE * side:NOPE * side + NOPE, :], ACT.Copy)
                ins.then_inc(gemm_out_act, 1)

            def copy_kr(h):
                if h == 0:
                    act.wait_ge(kr_ready, 1)
                act.activation(kT[64:96, h, :], kr_s[64:96, :], ACT.Copy).then_inc(kr_copied, 1)

            def q_out(h):
                act.wait_ge(gemm_done, G["q", h] + 1)
                act.activation(qT[0:NOPE, h, :], bank[G["q", h] % RING][0:NOPE, :], ACT.Copy).then_inc(q_nope, 1)

            for name, n in FIRST_HEADS:
                if name == "k":
                    keys_out(n)
                else:
                    q_out(n)
                    copy_kr(n)

            def exps(h, units):
                for u in units:
                    blocks = s_units[u]
                    n = NU * h + u
                    act.wait_ge(nmax_ready, n + 1)
                    if u == 0 and h >= 2:
                        act.wait_ge(pt_done, NG * (h - 1))
                    for i in blocks:
                        at = 0 if i != 1 else P
                        w = P * (i + 1)
                        e = 4 * (h % 2) + i
                        ins = act.activation(probs[:, h % 2, p_at[i]:p_at[i] + w], s_banks[n % 2][:, at:at + w], ACT.Exp,
                                             bias=nmx[:, e:e + 1], scale=SCALE, accum_out=sums[:, e:e + 1])
                    ins.then_inc(p_ready, 1)

            def attention_out(results):
                for name, n in results:
                    if name == "v":
                        move((name, n), v_tok[:, n, :], bank[G[name, n] % RING][:, :])
                        if n < 2:
                            hid_split(MIX_IN["sconv"] + n, b_s[:, n, :], hidH[:, 0, n, :])
                        if n == TB - 1:
                            split_after("ukv")
                    if name == "q":
                        q_out(n)
                        copy_kr(n)

            for step in range(STEPS):
                if step < HEADS:
                    exps(step, (0,))
                if 1 <= step <= HEADS:
                    turned_move(act, step - 1, (0,), pt_out_act)
                if step < HEADS:
                    exps(step, (1,))
                attention_out(between_turns(step))
                if 1 <= step <= HEADS:
                    turned_move(act, step - 1, (2,), pt_out_act)
                if step >= 3 and step % 2 == 1:
                    pr = (step - 3) // 2
                    act.wait_ge(gemm_done, G["ot", pr] + 1)
                    act.activation(hidH[:, 1, pr, :], bank[G["ot", pr] % RING][:, :], ACT.Copy).then_inc(hid_hi, 1)
                if step < HEADS:
                    exps(step, (2,))
                attention_out(before_weighing(step))
                if step == 1:
                    for c in (2, 3):
                        hid_split(MIX_IN["sconv"] + c, b_s[:, c, :], hidH[:, 0, c, :])
                if step in SPLIT_STEPS:
                    split_after(SPLIT_STEPS[step])
            for c in range(KD):
                finalize("mlp0", c, G["ewo1", c])
                if c == 3:
                    split_after("ewo1a")
            split_after("ewo1b")
            mlp(0)

            root("mix1")
            split_after("glr")
            spread_out("mix1")
            link(act.activation(lam_e, col("lam", 0, CH), ACT.Abs))
            act.activation(lam_e, lam_e, ACT.Exp, scale=-1.0).then_inc(lam_exp, 1)
            split_after("gq")
            for p in range(2):
                act.wait_ge(gemm_done, G["z", p] + 1)
                act.activation(cum[:, p, :], bank[G["z", p] % RING][:, :], ACT.Identity,
                               bias=col("gbias", p)).then_inc(gemm_out_act, 1)
            moved(act, G["z", 1])
            link(act.activation(ge[:, :, :], cum[:, :, :], ACT.Abs))
            link(act.activation(ge[:, :, :], ge[:, :, :], ACT.Exp, scale=-1.0))
            act.activation(ge[:, :, :], ge[:, :, :], ACT.Ln, bias=ones[:, 0:1]).then_inc(ls_ready, 1)
            split_after("gk")
            act.wait_ge(cum_ready, 1)
            act.activation(ge[:, :, :], cum[:, :, :], ACT.Exp, scale=1 / GTAU).then_inc(e_ready, 1)
            act.wait_ge(e_used, 1)
            act.activation(ge[:, :, :], cum[:, :, :], ACT.Exp, scale=-1 / GTAU).then_inc(e_ready, 1)
            ends = cum[:, :, :].rearrange("p a (n t) -> p a n t", t=GCH)[:, :, :, GCH - 1]
            act.activation(decay, ends, ACT.Exp, scale=1 / GTAU).then_inc(e_ready, 1)
            act.wait_ge(cum_ready, 2)
            act.activation(ge[:, :, :], ge[:, :, :], ACT.Exp, scale=1 / GTAU).then_inc(e_ready, 1)
            split_after("x0")

            def gelu(c):
                moved(act, G["y", c])
                act.activation(gel[:, c, :], gel[:, c, :], ACT.Gelu_apprx_tanh).then_inc(gel_ready, 1)

            def sigmoids(c):
                if c == 0:
                    act.wait_ge(lam_ready, 1)
                if c >= 2:
                    act.wait_ge(mix_in, MIX_IN["lru"] + c - 1)
                for name, dst, bias in (("ra", lr, "ba"), ("ri", li, "bi")):
                    act.wait_ge(gemm_done, G[name, c] + 1)
                    act.activation(dst[:, c % 2, :], bank[G[name, c] % RING][:, :], ACT.Sigmoid,
                                   bias=col(bias, c)).then_inc(gemm_out_act, 1)

            def gates(pair):
                moved(act, G["ri", pair[-1]])
                for c in pair:
                    act.activation(lru_t[:, c % 2, :], lr[:, c % 2, :], ACT.Tanh, scale=lam_k[:, c:c + 1])
                for c in pair:
                    link(act.activation(lr[:, c % 2, :], lr[:, c % 2, :], ACT.Exp, scale=lam_nk[:, c:c + 1]))
                for c in pair:
                    act.activation(lru_u[:, c % 2, :], lr[:, c % 2, :], ACT.Square).then_inc(gates_ready, 1)

            def roots(pair):
                for c in pair:
                    act.wait_ge(lru_m, c + 1)
                    act.activation(lru_t[:, c % 2, :], lru_t[:, c % 2, :], ACT.Sqrt).then_inc(lru_rt, 1)

            def lru_hi(c):
                hid_split(MIX_IN["lru"] + c, gel[:, c, :], hidH[:, 0, c, :])

            def v_out(half, blocks):
                for tb in blocks:
                    move((f"gv{half}", tb), gv[:, tb, 256 * half:256 * half + 256],
                         bank[G[f"gv{half}", tb] % RING][:, 0:256], scale=rcol_mix1[:, tb:tb + 1])

            gelu(0)
            gelu(1)
            sigmoids(0)
            split_after("y0")
            sigmoids(1)
            gates((0, 1))
            split_after("x1")
            roots((0, 1))
            gelu(2)
            gelu(3)
            sigmoids(2)
            lru_hi(0)
            lru_hi(1)
            split_after("y1")
            v_out(0, range(2))
            sigmoids(3)
            v_out(0, range(2, TB))
            gates((2, 3))
            v_out(1, range(2))
            split_after("gv0")
            roots((2, 3))
            v_out(1, range(2, TB))
            split_after("gv1")
            lru_hi(2)
            lru_hi(3)

            def gates_silu(heads):
                for h in heads:
                    moved(act, G["og", h])
                    act.activation(og[:, h, :], og[:, h, :], ACT.Silu).then_inc(og_ready, 1)

            gates_silu(range(2))
            split_after("og0")
            for p in range(2):
                move(("kt", p), gkT[:, :, p * P:(p + 1) * P], bank[G["kt", p] % RING][:, :].rearrange("p (b d) -> p b d", b=TB))
            gates_silu(range(2, GH))
            split_after("og1")

            def head_out(h):
                act.wait_ge(gemm_done, G["o", h] + 1)
                source = bank[G["o", h] % RING][:, :]
                if h >= 2:
                    act.wait_ge(stat_done, STAT["gla0"] + h - 1)
                square(source, f"gla{h}", 0)
                act.activation(o_sb[:, h, :], source, ACT.Copy).then_inc(gemm_out_act, 1)

            head_out(0)
            head_out(1)
            root("gla0")
            head_out(2)
            root("gla1")
            split_after("owo0a")
            head_out(3)
            root("gla2")
            root("gla3")
            for h in range(GH):
                hid_split(MIX_IN["gla"] + h, o_sb[:, h, :], hidH[:, 1, h, :])
            split_after("owo0b")
            for c in range(KD):
                finalize("mlp1", c, G["owo1", c])
                if c == 3:
                    split_after("owo1a")
            split_after("owo1b")
            mlp(1)
            root("final")
            act.wait_ge(final_ready, 1)
            for b in range(1, TB, 2):
                act.activation(y_tok[:, b, :], y_tok[:, b, :], ACT.Copy, scale=rcol[:, b:b + 1]).then_inc(y_scaled_act, 1)

        @block.vector
        def _(dve):
            n_link = 0

            def link(ins):
                nonlocal n_link
                n_link += 1
                ins.then_inc(dve_link, 1)
                dve.wait_ge(dve_link, n_link)

            def f32(ap):
                return ap.bitcast(F32)

            def split(n, slot=None, size=2048):
                width, key = size, ""
                if isinstance(n, int):
                    key, slot, size, width = TILES[n][0], n, TILES[n][1] * TILES[n][2] or 2048, split_width(n)
                dve.wait_ge(wh_ready, n + 1)
                main, extra = split_pieces(key, wL[:, slot % 2, 0:width], raw[:, slot % RAW, 0:size])
                hi_main, hi_extra = split_pieces(key, f32(wH[:, slot % 2, 0:width]), raw[:, slot % RAW, 0:size])
                for (dst, source), (hi, _) in zip(main + extra, hi_main + hi_extra):
                    ins = dve.tensor_tensor(dst, source, hi, ALU.subtract)
                ins.then_inc(wl_ready, 1)

            def split_after(key):
                split(TILE[key] + 2)

            def out_of(k, rows=P, lo=0, cols=S):
                dve.wait_ge(gemm_done, k + 1)
                return bank[k % RING][lo:rows, 0:cols]

            def lo_part(norm, c):
                dve.wait_ge(hi_new, KD * INST[norm] + c + 1)
                dve.scalar_tensor_tensor(out=hgL[:, c, :], in0=hT[:, c, :], scalar=col(norm, c), in1=f32(hgH[:, c, :]),
                                         op0=ALU.mult, op1=ALU.subtract).then_inc(hg_ready, 1)

            def variance(name, count):
                dve.wait_ge(stat_done, STAT[name] + 1)
                dve.tensor_scalar(vcol, stat_bank[:, 0:TB], 1.0 / count, EPS, ALU.mult, ALU.add).then_inc(var_ready, 1)

            def inverse(name):
                dst = rcol_mix1 if name == "mix1" else rcol
                dve.wait_ge(rt_ready, STAT[name] + 1)
                if SPREAD[name]:
                    dve.wait_ge(diag_ready, SPREAD[name])
                link(dve.reciprocal(dst, vcol))
                if SPREAD[name]:
                    dve.wait_ge(spread_done, SPREAD[name])
                link(dve.tensor_copy(rcol_hi, dst))
                link(dve.tensor_tensor(rcol_lo, dst, f32(rcol_hi), ALU.subtract))
                for column, diagonals in ((rcol_hi, diag_hi), (rcol_lo, diag_lo)):
                    ins = dve.tensor_tensor(diagonals[:, :, :], ident[:, :].unsqueeze(1).to_broadcast((P, TB, P)),
                                            f32(column).unsqueeze(2).to_broadcast((P, TB, P)), ALU.mult)
                ins.then_inc(diag_ready, 1)

            def spread_of(name):
                dve.wait_ge(spread_done, SPREAD[name] + 1)
                return bank[5 + SPREAD[name] % 2][:, :]

            def add_to_h(k, c):
                dve.tensor_tensor(hT[:, c, :], out_of(k), hT[:, c, :], ALU.add).then_inc(gemm_out, 1)

            def hid_low(hid, source, dst_hi, dst):
                dve.wait_ge(hid_hi, hid + 1)
                dve.tensor_tensor(dst, source, f32(dst_hi), ALU.subtract).then_inc(hid_ready, 1)

            def mlp(layer):
                n0, g0, h0 = TILE[f"mlp{layer}"], G[f"mlp{layer}", 0], HID[f"mlp{layer}"]

                def result(k, ring):
                    dve.wait_ge(gemm_done, k + 1)
                    return bank[ring % RING][:, :]

                def up(k, ring, hid, buf, chunks):
                    for m in chunks:
                        dve.scalar_tensor_tensor(out=tmpR[:, :], in0=result(k + m, ring + m), scalar=0.0, in1=rstd[:, :],
                                                 op0=ALU.max, op1=ALU.mult).then_inc(gemm_out, 1)
                        hid_low(hid + m, tmpS[:, :], hidH[:, buf, m, :], hidL[:, buf, m, :])

                def down(k, ring, chunks):
                    for c in chunks:
                        dve.tensor_tensor(hT[:, c, :], result(k + c, ring + c), hT[:, c, :], ALU.add).then_inc(gemm_out, 1)

                def lo(n, slot):
                    split(n + 2, slot + 2)

                variance(f"mlp{layer}", D)
                inverse(f"mlp{layer}")
                lo(n0, n0)
                dve.wait_ge(rstd_ready, 2 + 2 * layer)
                up(g0, g0, h0, 0, range(4))
                lo(n0 + 1, n0 + 1)
                with dve.Fori(1, LOOPS + 1) as i:
                    for pair in range(2):
                        n, g, hid = n0 - 6 + 4 * pair, g0 + 4 - 24 + 12 * pair, h0 + 4 - 8 + 4 * pair
                        for half in range(2):
                            up(g + 24 * i, g, hid + 8 * i, (pair + 1) % 2, (2 * half, 2 * half + 1))
                            lo(n + half + 8 * i, n + half)
                        for half in range(2):
                            down(g + 4 + 24 * i, g + 4, range(4 * half, 4 * half + 4))
                            lo(n + 2 + half + 8 * i, n + 2 + half)
                n, g, hid = n0 + 2 + 8 * LOOPS, g0 + 4 + 24 * LOOPS, h0 + 4 + 8 * LOOPS
                for half in range(2):
                    up(g, g, hid, (BLOCKS - 1) % 2, (2 * half, 2 * half + 1))
                    split(n + half + 2)
                for half in range(2):
                    down(g + 4, g + 4, range(4 * half, 4 * half + 4))
                    if n + 4 + half < len(TILES):
                        split(n + 4 + half)
                for c in range(KD):
                    if layer == 0:
                        add_to_h(g + 12 + c, c)
                        lo_part("mix1", c)
                    else:
                        add_to_h(G["last", c], c)
                        if c == KD - 1:
                            moved(dve, G["last", c])
                            dve.tensor_scalar(yT[:, c, :], hT[:, c, :], col("final", c), None, ALU.mult).then_inc(y_last, 1)
                            total, n_add = acc[:, STAT["final"] % 2, :], ADDS["final"] + c - 1
                            dve.wait_ge(sq_ready, SQ["final"] + c + 1)
                            dve.wait_ge(acc_ready, n_add)
                            dve.tensor_tensor(total, total, sqb[:, n_add % 2, :], ALU.add).then_inc(acc_ready, 1)
                        for n_turn in turned_after(c):
                            y_out(n_turn)
                    if c % 4 == 3 and n + 6 + c // 4 < len(TILES):
                        split(n + 6 + c // 4)

            def y_out(c):
                k = G["yt", c]
                dve.tensor_copy(y_tok[:, :, c * P:(c + 1) * P],
                                out_of(k).rearrange("p (b f) -> p b f", b=TB)).then_inc(gemm_out, 1)

            dve.wait_ge(params_done, 1)
            dve.tensor_copy(pcol[:, 0:NMIX], stat_bank[:, 0:NMIX]).then_inc(params_ready, 1)
            dve.wait_ge(params_ready, 1)
            split(0)

            def move_x(c):
                dve.wait_ge(x_done, c + 1)
                dve.tensor_copy(hT[:, c, :], x_banks[c % 4][:, :]).then_inc(x_out, 1)
                dve.wait_ge(x_out, c + 1)

            move_x(0)
            for c in range(KD):
                if c + 1 < KD:
                    move_x(c + 1)
                lo_part("mix0", c)
            dve.wait_ge(params_done, 2)
            dve.tensor_copy(pcol[:, NMIX:NPARAM], stat_bank[:, NMIX:NPARAM]).then_inc(params_ready, 1)
            dve.wait_ge(params_ready, 2)
            split(1)

            rows = slice(64, P)
            dve.wait_ge(ld_pos, 16)
            dve.wait_ge(ld_freq, 16)
            a, k, whole = ang[rows, :], ang_k[rows, :], turns[rows, :]
            link(dve.tensor_copy(a, pos_i[rows, :]))
            link(dve.tensor_scalar(a, a, rope_par[rows, 0:1], None, ALU.mult))
            two_pi = 2 * np.pi
            C1 = 6.28125
            C2 = float(np.round((two_pi - C1) * 2 ** 20) / 2 ** 20)
            C3 = float(two_pi - C1 - C2)
            BIG = 1.5 * 2 ** 23
            link(dve.tensor_scalar(k, a, 1 / two_pi, rope_par[rows, 1:2], ALU.mult, ALU.add))
            variance("mix0", D)
            link(dve.tensor_scalar(k, k, BIG, None, ALU.add))
            inverse("mix0")

            def scaled_out(name, c, dst):
                dve.tensor_tensor(dst, out_of(G[name, c]), rstd[:, :], ALU.mult).then_inc(gemm_out, 1)

            dve.wait_ge(rstd_ready, 1)
            scaled_out("cq", 0, c_raw[:, 0, :])
            scaled_out("cq", 1, c_raw[:, 1, :])
            split_after("cq01")
            link(dve.tensor_scalar(whole, k, BIG, None, ALU.subtract))
            link(dve.scalar_tensor_tensor(out=k, in0=whole, scalar=-C1, in1=a, op0=ALU.mult, op1=ALU.add))
            link(dve.scalar_tensor_tensor(out=k, in0=whole, scalar=-C2, in1=k, op0=ALU.mult, op1=ALU.add))
            link(dve.scalar_tensor_tensor(out=k, in0=whole, scalar=-C3, in1=k, op0=ALU.mult, op1=ALU.add))
            link(dve.tensor_scalar(k, k, rope_par[rows, 2:3], 3.1415925, ALU.add, ALU.min))
            dve.tensor_scalar(k, k, -3.1415925, None, ALU.max).then_inc(rope_arg, 1)
            scaled_out("cq", 2, c_raw[:, 2, :])
            scaled_out("cq", 3, c_raw[:, 3, :])
            split_after("cq2kv0")
            scaled_out("cq", 4, c_raw[:, 4, :])
            cos, sin = slice(64, 96), slice(96, P)
            dve.tensor_tensor(tmpR[64:P, :], out_of(G["kr", 0], P, 64), rstd[64:P, :], ALU.mult).then_inc(gemm_out, 1)
            moved(dve, G["kr", 0])
            variance("q", QR)
            dve.wait_ge(rope_ready, 1)
            link(dve.tensor_tensor(kr_s[cos, :], tmpR[cos, :], rope_cs[cos, :], ALU.mult))
            link(dve.tensor_tensor(rope_tmp[cos, 0, :], tmpR[sin, :], rope_cs[sin, :], ALU.mult))
            dve.tensor_tensor(kr_s[cos, :], kr_s[cos, :], rope_tmp[cos, 0, :], ALU.add).then_inc(kr_ready, 1)
            dve.wait_ge(kr_ready, 1)
            split_after("kv1kr")
            inverse("q")

            def scale_latent(name, c, gain):
                dve.scalar_tensor_tensor(out=c_raw[:, c, :], in0=c_raw[:, c, :], scalar=gain, in1=spread_of(name),
                                         op0=ALU.mult, op1=ALU.mult).then_inc(cn_scaled, 1)

            def c_out(c):
                scaled_out("c", c, c_s[:, c % 2, :])

            def u_out(c):
                scaled_out("u", c, cu[:, c, 2:2 + S])

            def b_out(c):
                scaled_out("b", c, b_s[:, c, :])

            def short_conv(c):
                dve.wait_ge(cu_ready, c + 1)
                if c:
                    dve.wait_ge(mix_in, MIX_IN["sconv"] + c)
                w = [col("evconv", CH * k + c) for k in range(SC_K)]
                link(dve.tensor_scalar(tmpR[:, :], cu[:, c, 0:S], w[0], None, ALU.mult))
                for k in range(1, SC_K):
                    link(dve.scalar_tensor_tensor(out=tmpR[:, :], in0=cu[:, c, k:k + S], scalar=w[k], in1=tmpR[:, :],
                                                  op0=ALU.mult, op1=ALU.add))
                dve.tensor_tensor(b_s[:, c, :], b_s[:, c, :], tmpR[:, :], ALU.mult).then_inc(mix_in, 1)

            link(dve.memset(cu[:, :, 0:SC_K - 1], 0.0))
            c_out(0)
            variance("kv", KVR)
            for c in range(3):
                scale_latent("q", c, col("qg", c))
            inverse("kv")
            c_out(1)
            split_after("c0")
            for c in range(2):
                scale_latent("kv", 3 + c, col("kvg", c))
            for c in range(5):
                dve.wait_ge(cn_hi, c + 1)
                dve.tensor_tensor(latent_lo[c], c_raw[:, c, :], f32(latent_hi[c]), ALU.subtract).then_inc(cn_ready, 1)
            u_out(0)
            u_out(1)
            split_after("u0")
            b_out(0)
            b_out(1)
            split_after("b0")
            short_conv(0)
            c_out(2)
            short_conv(1)
            c_out(3)
            split_after("c1")
            u_out(2)
            u_out(3)
            split_after("u1")
            b_out(2)
            b_out(3)
            split_after("b1")

            def q_rotary(h):
                if h >= 2:
                    dve.wait_ge(q_roped, h - 1)
                k = G["q", h]
                dve.tensor_tensor(rope_tmp[cos, h % 2, :], out_of(k, P, 96), rope_cs[sin, :], ALU.mult).then_inc(q_parts, 1)
                dve.wait_ge(q_nope, h + 1)
                dve.tensor_tensor(qT[cos, h, :], out_of(k, 96, 64), rope_cs[cos, :], ALU.mult).then_inc(gemm_out, 1)

            short_conv(2)
            q_rotary(0)
            q_rotary(1)

            def maxima(h, u):
                n = NU * h + u
                dve.wait_ge(s_done, n + 1)
                for i in s_units[u]:
                    at = 0 if i != 1 else P
                    e = 4 * (h % 2) + i
                    link(dve.tensor_reduce(mx[:, e:e + 1], s_banks[n % 2][:, at:at + P * (i + 1)], AX_X, ALU.max))
                lo, hi = 4 * (h % 2) + s_units[u][0], 4 * (h % 2) + s_units[u][-1] + 1
                dve.tensor_scalar(nmx[:, lo:hi], mx[:, lo:hi], -SCALE, None, ALU.mult).then_inc(nmax_ready, 1)

            def head_out(h):
                dve.wait_ge(o_done, h + 1)
                dve.wait_ge(p_ready, NU * (h + 1))
                link(dve.reciprocal(rinv, sums[:, 4 * (h % 2):4 * (h % 2) + 4]))
                dst = o_tok[:, h // 2 % 2, :, VD * (h % 2):VD * (h % 2) + VD]
                dve.tensor_tensor(dst, o_bank[:, 0:TB * VD].rearrange("p (b v) -> p b v", b=TB),
                                  rinv.unsqueeze(2).to_broadcast((P, TB, VD)), ALU.mult).then_inc(o_out, 1)

            def attention_results(results):
                for name, n in results:
                    if name == "q":
                        q_rotary(n)
                    if name == "ewo0":
                        add_to_h(G[name, n], n)
                    if name == "v" and n < 2:
                        hid_low(HID["sconv"] + n, b_s[:, n, :], hidH[:, 0, n, :], hidL[:, 0, n, :])

            for step in range(STEPS):
                if step < HEADS:
                    maxima(step, 0)
                    maxima(step, 1)
                if step == 1:
                    split_after("ukv")
                if step - 1 in SPLIT_STEPS:
                    split_after(SPLIT_STEPS[step - 1])
                if 1 <= step <= HEADS:
                    turned_move(dve, step - 1, (1,), pt_out)
                if step < HEADS:
                    maxima(step, 2)
                if step == 0:
                    short_conv(3)
                attention_results(between_turns(step))
                if step >= 3 and step % 2 == 1:
                    pr = (step - 3) // 2
                    ot = out_of(G["ot", pr])
                    dve.wait_ge(hid_hi, HID["attn"] + pr + 1)
                    dve.tensor_tensor(hidL[:, 1, pr, :], ot, f32(hidH[:, 1, pr, :]), ALU.subtract).then_inc(gemm_out, 1)
                attention_results(before_weighing(step))
                if step == 1:
                    for c in (2, 3):
                        hid_low(HID["sconv"] + c, b_s[:, c, :], hidH[:, 0, c, :], hidL[:, 0, c, :])
                if 1 <= step <= HEADS:
                    head_out(step - 1)
            split_after(SPLIT_STEPS[STEPS - 1])
            for c in range(KD):
                add_to_h(G["ewo1", c], c)
                lo_part("mlp0", c)
                if c == 3:
                    split_after("ewo1a")
            split_after("ewo1b")
            mlp(0)

            variance("mix1", D)
            inverse("mix1")
            split_after("glr")
            dve.wait_ge(rstd_ready, 3)
            dve.tensor_tensor(glr[:, :], out_of(G["glr", 0], GRANK), rstd[0:GRANK, :], ALU.mult).then_inc(gemm_out, 1)
            scaled_out("gq", 0, gq[:, 0, :])
            scaled_out("gq", 1, gq[:, 1, :])
            split_after("gq")

            dve.wait_ge(lam_exp, 1)
            link(dve.tensor_scalar(lam_d, lam_e, 2.0, None, ALU.add))
            link(dve.reciprocal(lam_d, lam_d))
            link(dve.tensor_tensor(lam_s, lam_e, lam_d, ALU.mult))
            link(dve.tensor_tensor(lam_s2, lam_s, lam_s, ALU.mult))
            link(dve.tensor_scalar(lam_p, lam_s2, 1 / 17, None, ALU.mult))
            for odd in (15, 13, 11, 9, 7, 5, 3):
                link(dve.scalar_tensor_tensor(out=lam_p, in0=lam_p, scalar=1 / odd, in1=lam_s2, op0=ALU.add, op1=ALU.mult))
            link(dve.scalar_tensor_tensor(out=lam_p, in0=lam_p, scalar=1.0, in1=lam_s, op0=ALU.add, op1=ALU.mult))
            link(dve.tensor_scalar(lam_d, col("lam", 0, CH), -1.0, 0.0, ALU.mult, ALU.max))
            link(dve.scalar_tensor_tensor(out=lam_p, in0=lam_p, scalar=2.0, in1=lam_d, op0=ALU.mult, op1=ALU.add))
            link(dve.tensor_scalar(lam_k, lam_p, LRU_C, None, ALU.mult))
            dve.tensor_scalar(lam_nk, lam_p, -LRU_C, None, ALU.mult).then_inc(lam_ready, 1)

            link(dve.memset(xl[:, 0:LRU_K - 1], 0.0))
            scaled_out("gk", 0, gk[:, 0, :])
            dve.wait_ge(ls_ready, 1)
            for p in range(2):
                link(dve.scalar_tensor_tensor(out=gki[:, p, :], in0=cum[:, p, :], scalar=0.0, in1=ge[:, p, :],
                                              op0=ALU.min, op1=ALU.subtract))
                ins = dve.tensor_tensor_scan(cum[:, p, :], resets[:, :], gki[:, p, :], 0.0, ALU.mult, ALU.add)
                if p == 0:
                    link(ins)
                else:
                    ins.then_inc(cum_ready, 1)
            scaled_out("gk", 1, gk[:, 1, :])
            split_after("gk")
            dve.wait_ge(e_ready, 1)
            dve.scalar_tensor_tensor(out=gq[:, :, :], in0=gq[:, :, :], scalar=GDK ** -0.5, in1=ge[:, :, :],
                                     op0=ALU.mult, op1=ALU.mult).then_inc(e_used, 1)
            dve.wait_ge(e_ready, 3)
            link(dve.tensor_tensor(gki[:, :, :], gk[:, :, :], ge[:, :, :], ALU.mult))
            for p in range(2):
                by_chunk = cum[:, p, :].rearrange("p (n t) -> p n t", t=GCH)
                ins = dve.tensor_tensor(ge[:, p, :].rearrange("p (n t) -> p n t", t=GCH),
                                        by_chunk[:, :, GCH - 1:GCH].to_broadcast((P, NCH, GCH)), by_chunk, ALU.subtract)
                if p == 0:
                    link(ins)
                else:
                    ins.then_inc(cum_ready, 1)

            def lru_conv(c):
                if c:
                    dve.wait_ge(xc_ready, c)
                scaled_out("xl", c, xl[:, LRU_K - 1:LRU_K - 1 + S])
                moved(dve, G["xl", c])
                w = [col("lconvw", CH * k + c) for k in range(LRU_K)]
                link(dve.tensor_scalar(xc[:, c, :], xl[:, 0:S], w[0], col("lconvb", c), ALU.mult, ALU.add))
                for k in range(1, LRU_K):
                    ins = dve.scalar_tensor_tensor(out=xc[:, c, :], in0=xl[:, k:k + S], scalar=w[k], in1=xc[:, c, :],
                                                   op0=ALU.mult, op1=ALU.add)
                    if k < LRU_K - 1:
                        link(ins)
                    else:
                        ins.then_inc(xc_ready, 1)

            def lru_factors(c):
                dve.wait_ge(gates_ready, c + 1)
                dve.scalar_tensor_tensor(out=lru_t[:, c % 2, :], in0=lru_u[:, c % 2, :], scalar=1.0, in1=lru_t[:, c % 2, :],
                                         op0=ALU.add, op1=ALU.mult).then_inc(lru_m, 1)

            def recurrence(c):
                dve.wait_ge(lru_rt, c + 1)
                dve.wait_ge(ix_ready, c + 1)
                link(dve.tensor_tensor(li[:, c % 2, :], li[:, c % 2, :], lru_t[:, c % 2, :], ALU.mult))
                link(dve.tensor_tensor_scan(lru_u[:, c % 2, :], lr[:, c % 2, :], li[:, c % 2, :], 0.0, ALU.mult, ALU.add))
                dve.wait_ge(gel_ready, c + 1)
                dve.tensor_tensor(gel[:, c, :], gel[:, c, :], lru_u[:, c % 2, :], ALU.mult).then_inc(mix_in, 1)

            def lru_low(c):
                hid_low(HID["lru"] + c, gel[:, c, :], hidH[:, 0, c, :], hidL[:, 0, c, :])

            dve.wait_ge(e_ready, 4)
            dve.tensor_tensor(gk[:, :, :], gk[:, :, :], ge[:, :, :], ALU.mult).then_inc(gla_ready, 1)
            lru_conv(0)
            lru_conv(1)
            split_after("x0")
            dve.wait_ge(gla_ready, 1)
            scaled_out("y", 0, gel[:, 0, :])
            scaled_out("y", 1, gel[:, 1, :])
            lru_conv(2)
            split_after("y0")
            lru_conv(3)
            lru_factors(0)
            lru_factors(1)
            split_after("x1")
            scaled_out("y", 2, gel[:, 2, :])
            recurrence(0)
            scaled_out("y", 3, gel[:, 3, :])
            recurrence(1)
            lru_low(0)
            lru_low(1)
            split_after("y1")
            lru_factors(2)
            lru_factors(3)
            split_after("gv0")
            recurrence(2)
            recurrence(3)
            split_after("gv1")
            lru_low(2)
            lru_low(3)
            for h in range(GH):
                scaled_out("og", h, og[:, h, :])
                if h == 1:
                    split_after("og0")

            def chunk_states(p):
                dve.wait_ge(kv_done, p + 1)
                for n in range(NCH - 1):
                    kv = bank[3 + 2 * p + n % 2][:, (n // 2) * P:(n // 2 + 1) * P]
                    if n == 0:
                        ins = dve.tensor_copy(states[:, p, 1, :], kv)
                    else:
                        ins = dve.scalar_tensor_tensor(out=states[:, p, n + 1, :], in0=states[:, p, n, :],
                                                       scalar=decay[:, p, n:n + 1], in1=kv, op0=ALU.mult, op1=ALU.add)
                    if n < NCH - 2:
                        link(ins)
                    else:
                        ins.then_inc(states_ready, 1)

            def att_out(h):
                dve.tensor_tensor(attT[:, h, :, :], out_of(G["att", h]).rearrange("p (b i) -> p b i", b=TB),
                                  gmask[:, :].unsqueeze(1).to_broadcast((P, TB, P)), ALU.mult).then_inc(gemm_out, 1)

            att_out(0)
            add_to_h(G["owo0", 0], 0)
            chunk_states(0)
            att_out(1)
            add_to_h(G["owo0", 1], 1)
            chunk_states(1)
            att_out(2)
            att_out(3)
            split_after("og1")

            def head_gate(h):
                moved(dve, G["o", h])
                link(dve.tensor_tensor(o_sb[:, h, :], o_sb[:, h, :], spread_of(f"gla{h}"), ALU.mult))
                dve.wait_ge(og_ready, h + 1)
                dve.scalar_tensor_tensor(out=o_sb[:, h, :], in0=o_sb[:, h, :], scalar=col("glag", 0), in1=og[:, h, :],
                                         op0=ALU.mult, op1=ALU.mult).then_inc(mix_in, 1)

            def gla_low(h):
                hid_low(HID["gla"] + h, o_sb[:, h, :], hidH[:, 1, h, :], hidL[:, 1, h, :])

            def add_down(c):
                add_to_h(G["owo0", c], c)

            add_down(2)
            variance("gla0", GDV)
            inverse("gla0")
            add_down(3)
            variance("gla1", GDV)
            inverse("gla1")
            head_gate(0)
            split_after("owo0a")
            add_down(4)
            variance("gla2", GDV)
            inverse("gla2")
            head_gate(1)
            add_down(5)
            variance("gla3", GDV)
            inverse("gla3")
            head_gate(2)
            head_gate(3)
            for h in range(3):
                gla_low(h)
            add_down(6)
            gla_low(3)
            add_down(7)
            split_after("owo0b")
            for c in range(KD):
                add_to_h(G["owo1", c], c)
                lo_part("mlp1", c)
                if c == 3:
                    split_after("owo1a")
            split_after("owo1b")
            mlp(1)
            y_out(KD - 1)
            variance("final", D)
            dve.wait_ge(rt_ready, STAT["final"] + 1)
            dve.wait_ge(diag_ready, SPREAD["mlp1"] + 1)
            dve.reciprocal(rcol, vcol).then_inc(final_ready, 1)
            dve.wait_ge(final_ready, 1)
            for b in range(0, TB, 2):
                dve.tensor_scalar(y_tok[:, b, :], y_tok[:, b, :], rcol[:, b:b + 1], None, ALU.mult).then_inc(y_scaled, 1)

        @block.tensor
        def _(pe):
            mm = nc.tensor.matmul

            def ring(k, static=None):
                if static is not None:
                    moved(pe, k - RING, static - RING)
                elif k >= RING:
                    moved(pe, k - RING)
                return bank[(k if static is None else static) % RING]

            def tile(n, slot=None, kc=None, cols=None):
                if slot is None:
                    slot, kc, cols = n, TILES[n][1], TILES[n][2] if cols is None else cols
                pe.wait_ge(wl_ready, n + 1)
                return tile_view(wH, slot % 2, kc, cols), tile_view(wL, slot % 2, kc, cols)

            def project(dst, w, xs, c0, m=P, ready=None):
                return project_many([(dst, c0)], w, xs, m, ready)[0]

            def project_many(dsts, w, xs, m=P, ready=None):
                wh, wl = w
                lasts, places = [None] * len(dsts), [None] * len(dsts)
                order = [(0, kc) for kc in range(len(xs))]
                if len(dsts) == 2:
                    order = [(0, 0), (0, 1), (1, 0), (1, 1)] + [(d, kc) for kc in range(2, len(xs)) for d in range(2)]
                for d, kc in order:
                    if d == 0 and ready is not None:
                        ready(kc)
                    dst, c0 = dsts[d]
                    if kc == 0:
                        places[d] = dst() if callable(dst) else dst
                    xh, xlo = xs[kc]
                    for n, (a, b) in enumerate(((wh, xh), (wh, xlo), (wl, xh))):
                        lasts[d] = mm(places[d], a[:, kc, c0:c0 + m], b, start=(kc == 0 and n == 0),
                                      stop=(kc == len(xs) - 1 and n == 2))
                return lasts

            def project_tokens(dst, w, xs, tb, cols):
                wh, wl = w
                for kc, (xh, xlo) in enumerate(xs):
                    at = slice(tb * P, (tb + 1) * P)
                    for n, (a, b) in enumerate(((xh, wh), (xh, wl), (xlo, wh))):
                        last = mm(dst, a[:, at], b[:, kc, cols], start=(kc == 0 and n == 0), stop=(kc == len(xs) - 1 and n == 2))
                return last

            hg = [(hgH[:, c, :], hgL[:, c, :]) for c in range(KD)]
            hid = [[(hidH[:, b, c, :], hidL[:, b, c, :]) for c in range(4)] for b in range(2)]
            latents = list(zip(latent_hi, latent_lo))
            latent_q, latent_kv = latents[0:3], latents[3:5]

            def hg_wait(norm):
                return lambda kc: pe.wait_ge(hg_ready, KD * INST[norm] + kc + 1)

            def hid_wait(h0):
                return lambda kc: pe.wait_ge(hid_ready, h0 + kc + 1)

            def statistic(name):
                s, chunks = STAT[name], STATS[STAT[name]][1]
                pe.wait_ge(sq_ready, SQ[name] + chunks)
                if chunks > 1:
                    pe.wait_ge(acc_ready, ADDS[name] + chunks - 1)
                if s:
                    pe.wait_ge(var_ready, s)
                for b in range(TB):
                    last = mm(stat_bank[:, b:b + 1], acc[:, s % 2, b * P:(b + 1) * P], ones[:, 0:1], start=True, stop=True)
                last.then_inc(stat_done, 1)

            def spread(name):
                pe.wait_ge(diag_ready, SPREAD[name] + 1)
                dst = bank[5 + SPREAD[name] % 2][:, :]
                mm(dst, ones_r[:, :], diag_hi[:, :, :], start=True, stop=False)
                mm(dst, ones_r[:, :], diag_lo[:, :, :], start=False, stop=True).then_inc(spread_done, 1)

            def spread_at(name, at=6):
                return lambda kc: spread(name) if kc == at else None

            pe.wait_ge(ident_ready, 1)
            pe.wait_ge(ld_mix, 16)
            pe.transpose(stat_bank[:, 0:NMIX], prm[0:NMIX, :], ident[0:NMIX, 0:NMIX]).then_inc(params_done, 1)

            def x_turn(c):
                if c >= 4:
                    pe.wait_ge(x_out, c - 3)
                if c in (0, KD // 2):
                    pe.wait_ge(ld_x[c // (KD // 2)], 16)
                for b in range(TB):
                    last = pe.transpose(x_banks[c % 4][:, b * P:(b + 1) * P], x_tok[:, b, c * P:(c + 1) * P], ident[:, :])
                last.then_inc(x_done, 1)

            def pair_of(key, names, ready=(None, None)):
                w = tile(TILE[key])
                for i, name in enumerate(names):
                    project(ring(G[name])[:, :], w, hg, i * P, ready=ready[i]).then_inc(gemm_done, 1)

            def x_and_hg(kc):
                if kc < 4:
                    x_turn(kc + 4)
                if kc == 4:
                    pe.wait_ge(ld_prm, 16 * (len(pieces) - 1))
                    pe.wait_ge(params_ready, 1)
                    pe.transpose(stat_bank[:, 0:NPARAM], prm[:, :], ident[0:NPARAM, 0:NPARAM]).then_inc(params_done, 1)
                pe.wait_ge(hg_ready, kc + 1)

            for c in range(4):
                x_turn(c)
            for last in project_many([(bank[G["cq", c] % RING][:, :], c * P) for c in range(2)], tile(TILE["cq01"]), hg,
                                     ready=x_and_hg):
                last.then_inc(gemm_done, 1)
            pe.wait_ge(consts_ready, 1)
            pe.wait_ge(params_ready, 2)
            statistic("mix0")
            pair_of("cq2kv0", [("cq", 2), ("cq", 3)], ready=(spread_at("mix0", 5), None))
            w = tile(TILE["kv1kr"], cols=192)
            project(ring(G["cq", 4])[:, :], w, hg, 0).then_inc(gemm_done, 1)
            project(ring(G["kr", 0])[:, :], w, hg, 64).then_inc(gemm_done, 1)
            statistic("q")
            pair_of("c0", [("c", 0), ("c", 1)], ready=(lambda kc: statistic("kv") if kc == 6 else None, spread_at("q", 1)))
            pair_of("u0", [("u", 0), ("u", 1)], ready=(spread_at("kv"), None))
            pair_of("b0", [("b", 0), ("b", 1)])
            for n in "cub":
                pair_of(f"{n}1", [(n, 2), (n, 3)])
            wh, wl = tile(TILE["ukv"])
            pe.wait_ge(cn_ready, 5)

            values_at = slice(HEADS * NOPE, HEADS * (NOPE + VD))

            def value(tb):
                project_tokens(ring(G["v", tb])[:, :], (wh, wl), latent_kv, tb, values_at).then_inc(gemm_done, 1)

            def keys(pr):
                project(ring(G["k", pr])[:, :], (wh, wl), latent_kv, P * pr).then_inc(gemm_done, 1)

            def query(h):
                w = tile(TILE[f"uq{h // 4}"], cols=4 * P)
                project(ring(G["q", h])[:, :], w, latent_q, P * (h % 4)).then_inc(gemm_done, 1)

            def scores(h, u):
                n = NU * h + u
                if u == 0:
                    pe.wait_ge(q_roped, h + 1)
                    pe.wait_ge(kr_copied, h + 1)
                    pe.wait_ge(q_nope, h + 1)
                    moved(pe, G["k", h // 2])
                if n >= 2:
                    pe.wait_ge(p_ready, n - 1)
                for i in s_units[u]:
                    at = 0 if i != 1 else P
                    dst = s_banks[n % 2]
                    mm(dst[:, at:at + P * (i + 1)], qT[0:QK, h, i * P:(i + 1) * P], kT[0:QK, h, 0:P * (i + 1)],
                       start=True, stop=False)
                    last = mm(dst[:, at + P * i:at + P * (i + 1)], identb[:, :], causal[:, :], start=False, stop=True)
                last.then_inc(s_done, 1)

            def turned_moved(n):
                h, g = n // NG, n % NG
                if g == 1:
                    pe.wait_ge(pt_out, h + 1)
                else:
                    pe.wait_ge(pt_out_act, 2 * h + g // 2 + 1)

            def turn(h, groups):
                pe.wait_ge(p_ready, NU * (h + 1))
                for g in groups:
                    n, blocks = NG * h + g, pt_groups[g]
                    if n >= 2:
                        turned_moved(n - 2)
                    for b, (j, i) in enumerate(blocks):
                        last = pe.transpose(pt_banks[n % 2][:, b * P:(b + 1) * P],
                                            probs[:, h % 2, p_at[i] + j * P:p_at[i] + (j + 1) * P], ident[:, :])
                    last.then_inc(pt_done, 1)

            def weigh(h):
                for g in range(NG):
                    turned_moved(NG * h + g)
                if h:
                    pe.wait_ge(o_out, h)
                else:
                    moved(pe, G["v", TB - 1])
                for i in range(TB):
                    for j in range(i + 1):
                        at = P * turned.index((j, i))
                        last = mm(o_bank[:, i * VD:(i + 1) * VD], probsT[:, h % 2, at:at + P],
                                  v_tok[:, j, h * VD:(h + 1) * VD], start=(j == 0), stop=(j == i))
                last.then_inc(o_done, 1)

            def short_down(c):
                nonlocal wo
                if c % 4 == 0:
                    wo = tile(TILE["ewo0" + "ab"[c // 4]])
                project(ring(G["ewo0", c])[:, :], wo, hid[0], P * (c % 4),
                        ready=hid_wait(READY["sconv"]) if c == 0 else None).then_inc(gemm_done, 1)

            wo = None
            fillers = {"k": keys, "v": value, "q": query, "ewo0": short_down}
            for name, n in FIRST_HEADS:
                fillers[name](n)
            for step in range(STEPS):
                if step < HEADS:
                    scores(step, 0)
                    scores(step, 1)
                if 1 <= step <= HEADS:
                    turn(step - 1, (0, 1))
                for name, n in between_turns(step):
                    fillers[name](n)
                if 1 <= step <= HEADS:
                    turn(step - 1, (2,))
                if step >= 3 and step % 2 == 1:
                    pr = (step - 3) // 2
                    pe.wait_ge(o_out, 2 * pr + 2)
                    dst = ring(G["ot", pr])
                    for b in range(TB):
                        last = pe.transpose(dst[:, b * P:(b + 1) * P], o_tok[:, pr % 2, b, :], ident[:, :])
                    last.then_inc(gemm_done, 1)
                if step < HEADS:
                    scores(step, 2)
                for name, n in before_weighing(step):
                    fillers[name](n)
                if 1 <= step <= HEADS:
                    weigh(step - 1)

            def down(name, half, buf, chunks, ready=None):
                wo = tile(TILE[f"{name}{half}"])
                for c in chunks:
                    project(ring(G[name, c])[:, :], wo, hid[buf], P * (c % 4),
                            ready=ready if c == chunks[0] else None).then_inc(gemm_done, 1)

            down("ewo1", "a", 1, range(4), lambda kc: moved(pe, G["ot", kc]))
            down("ewo1", "b", 1, range(4, 8))

            def mlp(layer):
                n0, g0, h0 = TILE[f"mlp{layer}"], G[f"mlp{layer}", 0], READY[f"mlp{layer}"]

                def up(n, slot, k, rk):
                    for half in range(2):
                        w = tile(n + half, slot + half, KD, 256)
                        for m in range(2):
                            c = 2 * half + m
                            project(ring(k + c, rk + c)[:, :], w, hg, m * P).then_inc(gemm_done, 1)

                def down(n, slot, k, rk, hid0, buf):
                    pe.wait_ge(hid_ready, hid0 + 4)
                    for half in range(2):
                        w = tile(n + half, slot + half, 4, 512)
                        for m in range(4):
                            c = 4 * half + m
                            project(ring(k + c, rk + c)[:, :], w, hid[buf], m * P).then_inc(gemm_done, 1)

                w = tile(n0, n0, KD, 256)
                dsts = [((lambda k: lambda: ring(k)[:, :])(g0 + m), m * P) for m in range(2)]
                for last in project_many(dsts, w, hg, ready=hg_wait(f"mlp{layer}")):
                    last.then_inc(gemm_done, 1)
                statistic(f"mlp{layer}")
                w = tile(n0 + 1, n0 + 1, KD, 256)
                project(ring(g0 + 2)[:, :], w, hg, 0, ready=spread_at(f"mlp{layer}", 5)).then_inc(gemm_done, 1)
                project(ring(g0 + 3)[:, :], w, hg, P).then_inc(gemm_done, 1)
                with pe.Fori(1, LOOPS + 1) as i:
                    for pair in range(2):
                        n, g = n0 - 6 + 4 * pair, g0 + 4 - 24 + 12 * pair
                        up(n + 8 * i, n, g + 24 * i, g + 24)
                        down(n + 2 + 8 * i, n + 2, g + 4 + 24 * i, g + 4 + 24, h0 - 8 + 4 * pair + 8 * i, pair)
                n, g = n0 + 2 + 8 * LOOPS, g0 + 4 + 24 * LOOPS
                up(n, n, g, g)
                down(n + 2, n + 2, g + 4, g + 4, h0 + 8 * LOOPS, 0)
                if layer == 0:
                    down(n + 4, n + 4, g + 12, g + 12, h0 + 4 + 8 * LOOPS, 1)
                    return
                pe.wait_ge(hid_ready, h0 + 4 * BLOCKS)
                for c in range(KD):
                    if c % 4 == 0:
                        w = tile(n + 4 + c // 4, n + 4 + c // 4, 4, 512)
                    project(ring(G["last", c])[:, :], w, hid[1], P * (c % 4)).then_inc(gemm_done, 1)
                    for n_turn in turned_after(c):
                        y_turn(n_turn)

            def y_turn(c):
                if c < KD - 1:
                    pe.wait_ge(y_new, c + 1)
                else:
                    pe.wait_ge(y_last, 1)
                dst = ring(G["yt", c])
                for b in range(TB):
                    last = pe.transpose(dst[:, b * P:(b + 1) * P], yT[:, c, b * P:(b + 1) * P], ident[:, :])
                last.then_inc(gemm_done, 1)

            mlp(0)

            w = tile(TILE["glr"])
            project(ring(G["glr", 0])[:, :], w, hg, 0, ready=hg_wait("mix1")).then_inc(gemm_done, 1)
            statistic("mix1")
            pair_of("gq", [("gq", 0), ("gq", 1)], ready=(None, spread_at("mix1", 0)))
            pe.wait_ge(ld_gup, 16)
            moved(pe, G["glr", 0])
            for p in range(2):
                mm(ring(G["z", p])[:, :], gup[:, p * P:(p + 1) * P], glr[:, :], start=True, stop=True).then_inc(gemm_done, 1)
            pair_of("gk", [("gk", 0), ("gk", 1)])
            pair_of("x0", [("xl", 0), ("xl", 1)])
            pair_of("y0", [("y", 0), ("y", 1)])

            def lru_gates(c):
                pe.wait_ge(xc_ready, c + 1)
                pe.wait_ge(ld_wgate, 64)
                for gate, name in enumerate(("ra", "ri")):
                    mm(ring(G[name, c])[:, :], wgate[:, gate, c, :], xc[:, c, :], start=True, stop=True).then_inc(gemm_done, 1)

            lru_gates(0)
            w = tile(TILE["x1"])
            project(ring(G["xl", 2])[:, :], w, hg, 0).then_inc(gemm_done, 1)
            lru_gates(1)
            project(ring(G["xl", 3])[:, :], w, hg, P).then_inc(gemm_done, 1)
            pair_of("y1", [("y", 2), ("y", 3)])
            lru_gates(2)
            for half in range(2):
                w = tile(TILE[f"gv{half}"])
                for tb in range(TB):
                    project_tokens(ring(G[f"gv{half}", tb])[:, 0:256], w, hg, tb, slice(0, 256)).then_inc(gemm_done, 1)
                    if half == 0 and tb == 1:
                        lru_gates(3)
            pair_of("og0", [("og", 0), ("og", 1)])
            pair_of("og1", [("og", 2), ("og", 3)])

            def key_turn(p):
                dst = ring(G["kt", p])
                for b in range(TB):
                    last = pe.transpose(dst[:, b * P:(b + 1) * P], gk[:, p, b * P:(b + 1) * P], ident[:, :])
                last.then_inc(gemm_done, 1)

            def key_values(p):
                moved(pe, G["kt", p])
                for n in range(NCH - 1):
                    tok = slice(GCH * (n % 2), GCH * (n % 2) + GCH)
                    for side in range(2):
                        h = 2 * p + side
                        last = mm(bank[3 + 2 * p + n % 2][64 * side:64 * side + 64, (n // 2) * P:(n // 2 + 1) * P],
                                  gkT[tok, n // 2, P * p + 64 * side:P * p + 64 * side + 64],
                                  gv[tok, n // 2, h * GDV:(h + 1) * GDV], start=True, stop=True)
                last.then_inc(kv_done, 1)

            def gla_scores(h):
                half, p = slice(64 * (h % 2), 64 * (h % 2) + 64), h // 2
                dst = ring(G["att", h])
                for b in range(TB):
                    last = mm(dst[:, b * P:(b + 1) * P], gki[half, p, b * P:(b + 1) * P], gq[half, p, b * P:(b + 1) * P],
                              start=True, stop=True)
                last.then_inc(gemm_done, 1)

            def gla_head(h):
                half, p = slice(64 * (h % 2), 64 * (h % 2) + 64), h // 2
                pe.wait_ge(states_ready, p + 1)
                moved(pe, G["att", h])
                dst = ring(G["o", h])
                for b in range(TB):
                    mm(dst[:, b * P:(b + 1) * P], gv[:, b, h * GDV:(h + 1) * GDV], attT[:, h, b, :], start=True, stop=False)
                    for n in (2 * b, 2 * b + 1):
                        if n:
                            last = mm(dst[:, n * GCH:(n + 1) * GCH], states[half, p, n, :], gq[half, p, n * GCH:(n + 1) * GCH],
                                      start=False, stop=(n % 2 == 1))
                last.then_inc(gemm_done, 1)

            wo = None

            def lru_down(c):
                nonlocal wo
                if c % 4 == 0:
                    wo = tile(TILE["owo0" + "ab"[c // 4]])
                project(ring(G["owo0", c])[:, :], wo, hid[0], P * (c % 4),
                        ready=hid_wait(READY["lru"]) if c == 0 else None).then_inc(gemm_done, 1)

            pe.wait_ge(gla_ready, 1)
            key_turn(0)
            key_turn(1)
            gla_scores(0)
            lru_down(0)
            key_values(0)
            gla_scores(1)
            lru_down(1)
            key_values(1)
            gla_scores(2)
            gla_scores(3)
            gla_head(0)
            lru_down(2)
            gla_head(1)
            statistic("gla0")
            lru_down(3)
            gla_head(2)
            spread("gla0")
            statistic("gla1")
            lru_down(4)
            gla_head(3)
            spread("gla1")
            statistic("gla2")
            lru_down(5)
            spread("gla2")
            statistic("gla3")
            lru_down(6)
            spread("gla3")
            lru_down(7)
            down("owo1", "a", 1, range(4), hid_wait(READY["gla"]))
            down("owo1", "b", 1, range(4, 8))
            mlp(1)
            y_turn(KD - 1)
            statistic("final")


_INS = ['x', 'positions', 'mixer_norm_g', 'mlp_norm_g', 'mlp_w1', 'mlp_w2', 'final_norm_g', 'ev_w_in', 'ev_conv_w',
        'mla_q_norm_g', 'mla_w_uq', 'mla_kv_norm_g', 'mla_w_ukv', 'ev_w_out', 'od_w_in', 'gla_w_gate_up', 'gla_b_gate',
        'gla_norm_g', 'lru_conv_w', 'lru_conv_b', 'lru_w_a', 'lru_b_a', 'lru_w_i', 'lru_b_i', 'lru_lambda', 'od_w_out']


def kernel(**inputs):
    import concourse.bacc as bacc
    from concourse.bass_utils import run_bass_kernel_spmd

    nc = bacc.Bacc("TRN2", target_bir_lowering=False, num_devices=1)
    arrays, t = {}, {}
    for name in _INS:
        a = np.ascontiguousarray(inputs[name])
        arrays[f"in_{name}"] = a
        t[name] = nc.dram_tensor(f"in_{name}", a.shape, mybir.dt.from_np(a.dtype), kind="ExternalInput").ap()
    freq = np.float32(10000.0) ** (-np.arange(0, ROPE, 2, dtype=np.float32) / np.float32(ROPE))
    par = np.zeros((2 * ROPE, 4), np.float32)
    par[:, 0] = np.tile(freq, 4)
    par[:ROPE, 1], par[:ROPE, 2] = 0.25, np.pi / 2
    par[:, 3] = 1.0
    par[ROPE:ROPE + ROPE // 2, 3] = -1.0
    arrays["in_rope_par"] = par
    t["rope_par"] = nc.dram_tensor("in_rope_par", par.shape, F32, kind="ExternalInput").ap()
    out = nc.dram_tensor("out_0", (1, S, D), F32, kind="ExternalOutput").ap()
    trunk(nc, t, out)
    r = run_bass_kernel_spmd(nc, [arrays], core_ids=[0])
    return r.results[0]["out_0"]
```
